# Optimizing a Trainium2 kernel written in Bass

```python
import math
import jax, jax.numpy as jnp
from jax import lax
import numpy as np

D_MODEL = 1024
BATCH = 1
SEQ = 512
DEPTH = 1

CHUNK = 64
Q_BLOCK = 128
MIX_WIDTH = D_MODEL
CONV_CH = MIX_WIDTH // 2
CONV_K = 31
N_HEADS = 8
V_HEAD_DIM = (MIX_WIDTH - CONV_CH) // N_HEADS
QK_NOPE_DIM = 64
QK_ROPE_DIM = 32
QK_HEAD_DIM = QK_NOPE_DIM + QK_ROPE_DIM
Q_LORA_RANK = D_MODEL // 4
KV_LORA_RANK = D_MODEL // 8
ROPE_THETA = 10000.0
IN_WIDTH = 2 * CONV_CH + Q_LORA_RANK + KV_LORA_RANK + QK_ROPE_DIM
N_GROUPS = 4
EXPERTS_PER_GROUP = 8
N_EXPERTS = N_GROUPS * EXPERTS_PER_GROUP
TOP_K = 2
D_EXPERT = D_MODEL // 4
EPS = 1e-6


def rms_norm(x, g):
    xf = x.astype(jnp.float32)
    y = xf * lax.rsqrt(jnp.mean(xf * xf, axis=-1, keepdims=True) + EPS)
    return (y * g.astype(jnp.float32)).astype(x.dtype)

def layer_norm(x, g, b):
    xf = x.astype(jnp.float32)
    mu = jnp.mean(xf, axis=-1, keepdims=True)
    var = jnp.mean(jnp.square(xf - mu), axis=-1, keepdims=True)
    y = (xf - mu) * lax.rsqrt(var + EPS)
    return (y * g.astype(jnp.float32) + b.astype(jnp.float32)).astype(x.dtype)

def apply_rope(x, cos, sin):
    x1, x2 = jnp.split(x, 2, axis=-1)
    cos = cos.astype(x.dtype)
    sin = sin.astype(x.dtype)
    return jnp.concatenate([x1 * cos - x2 * sin, x1 * sin + x2 * cos], axis=-1)

def conv_group(val, gate, conv_w, conv_b, ln_g, ln_b):
    u = val * jax.nn.sigmoid(gate)
    kern = conv_w[:, None, :].astype(u.dtype)
    dw = lax.conv_general_dilated(
        u, kern, window_strides=(1,), padding=[(CONV_K - 1, 0)],
        dimension_numbers=("NWC", "WIO", "NWC"),
        feature_group_count=CONV_CH) + conv_b.astype(u.dtype)
    return jax.nn.silu(layer_norm(dw, ln_g, ln_b))

def mla_group(c_q, c_kv, k_rope, cos, sin, q_a_norm, w_q_b, kv_a_norm, w_kv_b,
              q_norm, k_norm):
    b, s, _ = c_q.shape
    q = (rms_norm(c_q, q_a_norm) @ w_q_b).reshape(b, s, N_HEADS, QK_HEAD_DIM)
    kv = (rms_norm(c_kv, kv_a_norm) @ w_kv_b).reshape(b, s, N_HEADS, QK_NOPE_DIM + V_HEAD_DIM)
    k_nope, v = kv[..., :QK_NOPE_DIM], kv[..., QK_NOPE_DIM:]
    k_r = jnp.broadcast_to(k_rope[:, :, None, :], (b, s, N_HEADS, QK_ROPE_DIM))
    k = jnp.concatenate([k_nope, k_r], axis=-1)
    q = rms_norm(q, q_norm)
    k = rms_norm(k, k_norm)
    cos_h, sin_h = cos[:, :, None, :], sin[:, :, None, :]
    q = jnp.concatenate([q[..., :QK_NOPE_DIM], apply_rope(q[..., QK_NOPE_DIM:], cos_h, sin_h)], axis=-1)
    k = jnp.concatenate([k[..., :QK_NOPE_DIM], apply_rope(k[..., QK_NOPE_DIM:], cos_h, sin_h)], axis=-1)

    n_blk = s // Q_BLOCK
    key_chunk = jnp.arange(s) // CHUNK
    scale = QK_HEAD_DIM ** -0.5
    q_blocks = q.reshape(b, n_blk, Q_BLOCK, N_HEADS, QK_HEAD_DIM).swapaxes(0, 1)

    def block_attn(args):
        qb, blk = args
        sc = jnp.einsum("bqhd,bkhd->bhqk", qb, k).astype(jnp.float32) * scale
        q_chunk = (blk * Q_BLOCK + jnp.arange(Q_BLOCK)) // CHUNK
        mask = key_chunk[None, :] <= q_chunk[:, None]
        sc = jnp.where(mask[None, None], sc, -jnp.inf)
        p = jax.nn.softmax(sc, axis=-1).astype(v.dtype)
        return jnp.einsum("bhqk,bkhd->bqhd", p, v)

    out = lax.map(block_attn, (q_blocks, jnp.arange(n_blk)))
    return out.swapaxes(0, 1).reshape(b, s, N_HEADS * V_HEAD_DIM)

def hier_moe(h, w_group, b_group, w_expert, b_expert, w_gate_e, w_up_e, w_down_e):
    n = h.shape[0]
    g_logits = (h @ w_group).astype(jnp.float32) + b_group.astype(jnp.float32)
    g_prob = jax.nn.softmax(g_logits, axis=-1)
    g_top, g_idx = lax.top_k(g_prob, 1)
    e_logits = ((h @ w_expert).astype(jnp.float32) + b_expert.astype(jnp.float32)
                ).reshape(n, N_GROUPS, EXPERTS_PER_GROUP)
    sel = jnp.broadcast_to(g_idx[:, :, None], (n, 1, EXPERTS_PER_GROUP))
    e_in = jnp.take_along_axis(e_logits, sel, axis=1)[:, 0]
    e_prob = jax.nn.softmax(e_in, axis=-1)
    e_top, e_idx = lax.top_k(e_prob, TOP_K)
    w = g_top * e_top / jnp.sum(e_top, axis=-1, keepdims=True)
    glob_idx = g_idx * EXPERTS_PER_GROUP + e_idx
    gates = jnp.sum(jax.nn.one_hot(glob_idx, N_EXPERTS, dtype=jnp.float32) * w[..., None],
                    axis=1).astype(h.dtype)
    y = jnp.zeros_like(h)
    for e in range(N_EXPERTS):
        a = jax.nn.silu(h @ w_gate_e[e]) * (h @ w_up_e[e])
        y = y + gates[:, e:e + 1] * (a @ w_down_e[e])
    return y

def hybrid_layer(x, c, cos, sin, w_ada, b_ada, norm_mix, w_in, conv_w, conv_b,
                 conv_ln_g, conv_ln_b, q_a_norm, w_q_b, kv_a_norm, w_kv_b, q_norm,
                 k_norm, w_out, norm_ffn, w_group, b_group, w_expert, b_expert,
                 w_gate_e, w_up_e, w_down_e):
    b, s, d = x.shape
    mod = jax.nn.silu(c) @ w_ada + b_ada
    sh_a, sc_a, g_a, sh_f, sc_f, g_f = jnp.split(mod, 6, axis=-1)

    h = rms_norm(x, norm_mix) * (1 + sc_a[:, None]) + sh_a[:, None]
    proj = h @ w_in
    o1 = CONV_CH
    o2 = o1 + CONV_CH
    o3 = o2 + Q_LORA_RANK
    o4 = o3 + KV_LORA_RANK
    conv_val, conv_gate, c_q, c_kv, k_rope = jnp.split(proj, [o1, o2, o3, o4], axis=-1)
    y_conv = conv_group(conv_val, conv_gate, conv_w, conv_b, conv_ln_g, conv_ln_b)
    y_attn = mla_group(c_q, c_kv, k_rope, cos, sin, q_a_norm, w_q_b, kv_a_norm,
                       w_kv_b, q_norm, k_norm)
    mixed = jnp.concatenate([y_conv, y_attn], axis=-1) @ w_out
    x = x + g_a[:, None] * mixed

    h2 = rms_norm(x, norm_ffn) * (1 + sc_f[:, None]) + sh_f[:, None]
    y = hier_moe(h2.reshape(b * s, d), w_group, b_group, w_expert, b_expert,
                 w_gate_e, w_up_e, w_down_e).reshape(b, s, d)
    return x + g_f[:, None] * y

def first_inputs(seed: int = 0) -> dict:
    key = jax.random.key(seed)
    ks = jax.random.split(key, 32)
    f32 = jnp.float32

    def nrm(k, shape, scale):
        return jax.random.normal(k, shape, f32) * scale

    def gain(k, n):
        return 1.0 + 0.01 * jax.random.normal(k, (DEPTH, n), f32)

    positions = (jax.random.randint(ks[2], (BATCH, 1), 0, 4096, dtype=jnp.int32)
                 + jnp.arange(SEQ, dtype=jnp.int32)[None, :])
    return {
        "x": nrm(ks[0], (BATCH, SEQ, D_MODEL), 1.0),
        "c": nrm(ks[1], (BATCH, D_MODEL), 1.0),
        "positions": positions,
        "w_ada": nrm(ks[3], (DEPTH, D_MODEL, 6 * D_MODEL), 0.5 * D_MODEL ** -0.5),
        "b_ada": nrm(ks[4], (DEPTH, 6 * D_MODEL), 0.01),
        "norm_mix": gain(ks[5], D_MODEL),
        "w_in": nrm(ks[6], (DEPTH, D_MODEL, IN_WIDTH), D_MODEL ** -0.5),
        "conv_w": nrm(ks[7], (DEPTH, CONV_K, CONV_CH), CONV_K ** -0.5),
        "conv_b": nrm(ks[8], (DEPTH, CONV_CH), 0.01),
        "conv_ln_g": gain(ks[9], CONV_CH),
        "conv_ln_b": nrm(ks[10], (DEPTH, CONV_CH), 0.01),
        "q_a_norm": gain(ks[11], Q_LORA_RANK),
        "w_q_b": nrm(ks[12], (DEPTH, Q_LORA_RANK, N_HEADS * QK_HEAD_DIM), Q_LORA_RANK ** -0.5),
        "kv_a_norm": gain(ks[13], KV_LORA_RANK),
        "w_kv_b": nrm(ks[14], (DEPTH, KV_LORA_RANK, N_HEADS * (QK_NOPE_DIM + V_HEAD_DIM)), KV_LORA_RANK ** -0.5),
        "q_norm": gain(ks[15], QK_HEAD_DIM),
        "k_norm": gain(ks[16], QK_HEAD_DIM),
        "w_out": nrm(ks[17], (DEPTH, MIX_WIDTH, D_MODEL), MIX_WIDTH ** -0.5),
        "norm_ffn": gain(ks[18], D_MODEL),
        "w_group": nrm(ks[19], (DEPTH, D_MODEL, N_GROUPS), D_MODEL ** -0.5),
        "b_group": nrm(ks[20], (DEPTH, N_GROUPS), 0.01),
        "w_expert": nrm(ks[21], (DEPTH, D_MODEL, N_EXPERTS), D_MODEL ** -0.5),
        "b_expert": nrm(ks[22], (DEPTH, N_EXPERTS), 0.01),
        "w_gate_e": nrm(ks[23], (DEPTH, N_EXPERTS, D_MODEL, D_EXPERT), D_MODEL ** -0.5),
        "w_up_e": nrm(ks[24], (DEPTH, N_EXPERTS, D_MODEL, D_EXPERT), D_MODEL ** -0.5),
        "w_down_e": nrm(ks[25], (DEPTH, N_EXPERTS, D_EXPERT, D_MODEL), D_EXPERT ** -0.5),
    }

def first_block(x, c, positions, w_ada, b_ada, norm_mix, w_in, conv_w, conv_b,
              conv_ln_g, conv_ln_b, q_a_norm, w_q_b, kv_a_norm, w_kv_b, q_norm,
              k_norm, w_out, norm_ffn, w_group, b_group, w_expert, b_expert,
              w_gate_e, w_up_e, w_down_e):
    inv_freq = ROPE_THETA ** (-jnp.arange(0, QK_ROPE_DIM, 2, dtype=jnp.float32) / QK_ROPE_DIM)
    ang = positions.astype(jnp.float32)[..., None] * inv_freq
    cos, sin = jnp.cos(ang), jnp.sin(ang)
    for l in range(DEPTH):
        x = hybrid_layer(x, c, cos, sin, w_ada[l], b_ada[l], norm_mix[l], w_in[l],
                         conv_w[l], conv_b[l], conv_ln_g[l], conv_ln_b[l],
                         q_a_norm[l], w_q_b[l], kv_a_norm[l], w_kv_b[l], q_norm[l],
                         k_norm[l], w_out[l], norm_ffn[l], w_group[l], b_group[l],
                         w_expert[l], b_expert[l], w_gate_e[l], w_up_e[l], w_down_e[l])
    return x


DEPTH_2 = 2

HEAD_DIM = 64
SWA_Q_HEADS = 8
SWA_KV_HEADS = 2
SWA_G = SWA_Q_HEADS // SWA_KV_HEADS
DSA_Q_HEADS = 8
DSA_KV_HEADS = 1
DSA_G = DSA_Q_HEADS // DSA_KV_HEADS
IDX_HEADS = 8
IDX_DIM = 32
TOPK_MAX = 256
WINDOW = 128
BLOCK = 128
PLE_DIM = 256
MIX_WIDTH_2 = (SWA_Q_HEADS + DSA_Q_HEADS) * HEAD_DIM
D_FF = -(-(8 * D_MODEL) // (3 * 256)) * 256
DN_ALPHA = (2 * DEPTH_2) ** 0.25
DN_BETA = (8 * DEPTH_2) ** -0.25
LN_EPS = 1e-5
NEG = -1e30
IN_SIZES = (SWA_Q_HEADS * HEAD_DIM, SWA_KV_HEADS * HEAD_DIM, SWA_KV_HEADS * HEAD_DIM,
            DSA_Q_HEADS * HEAD_DIM, DSA_KV_HEADS * HEAD_DIM, DSA_KV_HEADS * HEAD_DIM,
            IDX_HEADS * IDX_DIM, IDX_DIM, IDX_HEADS)
IN_COLS = sum(IN_SIZES)


def layer_norm_2(x, g, b):
    xf = x.astype(jnp.float32)
    mu = xf.mean(-1, keepdims=True)
    var = jnp.square(xf - mu).mean(-1, keepdims=True)
    y = (xf - mu) * lax.rsqrt(var + LN_EPS)
    return (y * g.astype(jnp.float32) + b.astype(jnp.float32)).astype(x.dtype)

def rope(x, positions):
    half = x.shape[-1] // 2
    inv = ROPE_THETA ** (-jnp.arange(half, dtype=jnp.float32) / half)
    ang = positions.astype(jnp.float32)[..., None] * inv
    ang = ang.reshape(ang.shape[:2] + (1,) * (x.ndim - 3) + (half,))
    cos, sin = jnp.cos(ang), jnp.sin(ang)
    x1 = x[..., :half].astype(jnp.float32)
    x2 = x[..., half:].astype(jnp.float32)
    return jnp.concatenate([x1 * cos - x2 * sin, x2 * cos + x1 * sin], -1).astype(x.dtype)

def swa_sink_attention(q, k, v, sinks):
    B, S, Hkv, G, D = q.shape
    nb = S // BLOCK
    qb = q.reshape(B, nb, BLOCK, Hkv, G, D)
    kb = k.reshape(B, nb, BLOCK, Hkv, D)
    vb = v.reshape(B, nb, BLOCK, Hkv, D)
    prev = lambda t: jnp.concatenate([jnp.zeros_like(t[:, :1]), t[:, :-1]], axis=1)
    kk = jnp.concatenate([prev(kb), kb], axis=2)
    vv = jnp.concatenate([prev(vb), vb], axis=2)
    s = jnp.einsum('bnqhgd,bnkhd->bnhgqk', qb, kk).astype(jnp.float32) * (D ** -0.5)
    i = jnp.arange(BLOCK)[:, None]
    j = jnp.arange(2 * BLOCK)[None, :]
    diff = BLOCK + i - j
    band = (diff >= 0) & (diff < WINDOW)
    not_pad = (jnp.arange(nb)[:, None, None] > 0) | (j[None] >= BLOCK)
    mask = band[None] & not_pad
    s = jnp.where(mask[None, :, None, None], s, NEG)
    sink = sinks.astype(jnp.float32)[None, None, :, :, None, None]
    m = jnp.maximum(s.max(-1, keepdims=True), sink)
    pr = jnp.exp(s - m)
    denom = pr.sum(-1, keepdims=True) + jnp.exp(sink - m)
    o = jnp.einsum('bnhgqk,bnkhd->bnqhgd', (pr / denom).astype(v.dtype), vv)
    return o.reshape(B, S, Hkv * G * D)

def dsa_sparse_attention(q, k, v, qi, ki, wi, k_top):
    B, S, Hkv, G, D = q.shape
    nb = S // BLOCK
    to_blocks = lambda t: jnp.moveaxis(t.reshape((B, nb, BLOCK) + t.shape[2:]), 1, 0)
    gather = jax.vmap(lambda kv, ix: kv[ix])
    key_pos = jnp.arange(S)

    def one_block(args):
        n, qb, qib, wib = args
        t = n * BLOCK + jnp.arange(BLOCK)
        sc = jnp.einsum('bqhd,bsd->bqhs', qib, ki).astype(jnp.float32)
        idx_score = jnp.einsum('bqhs,bqh->bqs', jax.nn.relu(sc), wib.astype(jnp.float32))
        causal = key_pos[None, :] <= t[:, None]
        idx_score = jnp.where(causal[None], idx_score, NEG)
        _, sel = lax.top_k(idx_score, k_top)
        ks = gather(k, sel)
        vs = gather(v, sel)
        s = jnp.einsum('bqhgd,bqjhd->bqhgj', qb, ks).astype(jnp.float32) * (D ** -0.5)
        valid = sel <= t[None, :, None]
        s = jnp.where(valid[:, :, None, None, :], s, NEG)
        pr = jax.nn.softmax(s, axis=-1)
        o = jnp.einsum('bqhgj,bqjhd->bqhgd', pr.astype(v.dtype), vs)
        return o.reshape(B, BLOCK, Hkv * G * D)

    out = lax.map(one_block, (jnp.arange(nb), to_blocks(q), to_blocks(qi), to_blocks(wi)))
    return jnp.moveaxis(out, 0, 1).reshape(B, S, Hkv * G * D)

def hybrid_layer_2(x, p_i, positions, w_in, sinks, idx_k_g, idx_k_b, w_o, ln1_g, ln1_b,
                 w_gu, w_down, w_pg, w_pp, ln2_g, ln2_b):
    B, S, _ = x.shape
    k_top = min(TOPK_MAX, S // 4)
    h = x @ w_in
    cuts = [int(c) for c in np.cumsum(IN_SIZES)[:-1]]
    qa, ka, va, qb, kb, vb, qi, ki, wi = jnp.split(h, cuts, axis=-1)
    qa = rope(qa.reshape(B, S, SWA_KV_HEADS, SWA_G, HEAD_DIM), positions)
    ka = rope(ka.reshape(B, S, SWA_KV_HEADS, HEAD_DIM), positions)
    va = va.reshape(B, S, SWA_KV_HEADS, HEAD_DIM)
    qb = rope(qb.reshape(B, S, DSA_KV_HEADS, DSA_G, HEAD_DIM), positions)
    kb = rope(kb.reshape(B, S, DSA_KV_HEADS, HEAD_DIM), positions)
    vb = vb.reshape(B, S, DSA_KV_HEADS, HEAD_DIM)
    qi = rope(qi.reshape(B, S, IDX_HEADS, IDX_DIM), positions)
    ki = rope(layer_norm_2(ki, idx_k_g, idx_k_b), positions)
    wi = wi * (IDX_HEADS ** -0.5 * IDX_DIM ** -0.5)
    oa = swa_sink_attention(qa, ka, va, sinks.reshape(SWA_KV_HEADS, SWA_G))
    ob = dsa_sparse_attention(qb, kb, vb, qi, ki, wi, k_top)
    mix = jnp.concatenate([oa, ob], axis=-1) @ w_o
    x = layer_norm_2(DN_ALPHA * x + mix, ln1_g, ln1_b)
    g, u = jnp.split(x @ w_gu, 2, axis=-1)
    ffn = (jax.nn.silu(g) * u) @ w_down
    ple = (p_i @ w_pp) * jax.nn.sigmoid(x @ w_pg)
    return layer_norm_2(DN_ALPHA * x + ffn + ple, ln2_g, ln2_b)

def second_inputs(seed: int = 0) -> dict:
    key = jax.random.key(seed)
    ks = jax.random.split(key, 20)
    nrm = lambda k, shape, scale: jax.random.normal(k, shape, jnp.float32) * scale
    L = DEPTH_2
    offs = jax.random.randint(ks[2], (BATCH, 1), 0, 1024)
    positions = (offs + jnp.arange(SEQ)[None, :]).astype(jnp.int32)
    return {
        "x": nrm(ks[0], (BATCH, SEQ, D_MODEL), 1.0),
        "p": nrm(ks[1], (DEPTH_2, BATCH, SEQ, PLE_DIM), 1.0),
        "positions": positions,
        "ln_in_g": 1.0 + nrm(ks[3], (D_MODEL,), 0.02),
        "ln_in_b": nrm(ks[4], (D_MODEL,), 0.02),
        "w_in": nrm(ks[5], (L, D_MODEL, IN_COLS), D_MODEL ** -0.5),
        "attn_sinks": nrm(ks[6], (L, SWA_Q_HEADS), 0.5),
        "idx_k_g": 1.0 + nrm(ks[7], (L, IDX_DIM), 0.02),
        "idx_k_b": nrm(ks[8], (L, IDX_DIM), 0.02),
        "w_o": nrm(ks[9], (L, MIX_WIDTH_2, D_MODEL), DN_BETA * MIX_WIDTH_2 ** -0.5),
        "ln1_g": 1.0 + nrm(ks[10], (L, D_MODEL), 0.02),
        "ln1_b": nrm(ks[11], (L, D_MODEL), 0.02),
        "w_gu": nrm(ks[12], (L, D_MODEL, 2 * D_FF), D_MODEL ** -0.5),
        "w_down": nrm(ks[13], (L, D_FF, D_MODEL), DN_BETA * D_FF ** -0.5),
        "w_pg": nrm(ks[14], (L, D_MODEL, D_MODEL), D_MODEL ** -0.5),
        "w_pp": nrm(ks[15], (L, PLE_DIM, D_MODEL), DN_BETA * PLE_DIM ** -0.5),
        "ln2_g": 1.0 + nrm(ks[16], (L, D_MODEL), 0.02),
        "ln2_b": nrm(ks[17], (L, D_MODEL), 0.02),
    }

def second_block(x, p, positions, ln_in_g, ln_in_b, w_in, attn_sinks, idx_k_g, idx_k_b, w_o,
              ln1_g, ln1_b, w_gu, w_down, w_pg, w_pp, ln2_g, ln2_b):
    x = layer_norm_2(x, ln_in_g, ln_in_b)
    for i in range(DEPTH_2):
        x = hybrid_layer_2(x, p[i], positions, w_in[i], attn_sinks[i], idx_k_g[i], idx_k_b[i],
                         w_o[i], ln1_g[i], ln1_b[i], w_gu[i], w_down[i], w_pg[i], w_pp[i],
                         ln2_g[i], ln2_b[i])
    return x


def setup_inputs(seed=0):
    out = dict(first_inputs(seed))
    for name, value in second_inputs(seed + 1).items():
        if name != "x":
            out[name + "_2"] = value
    return out


def reference(
    x, c, positions, w_ada, b_ada, norm_mix, w_in, conv_w, conv_b, conv_ln_g, conv_ln_b,
    q_a_norm, w_q_b, kv_a_norm, w_kv_b, q_norm, k_norm, w_out, norm_ffn, w_group, b_group,
    w_expert, b_expert, w_gate_e, w_up_e, w_down_e, p_2, positions_2, ln_in_g_2, ln_in_b_2,
    w_in_2, attn_sinks_2, idx_k_g_2, idx_k_b_2, w_o_2, ln1_g_2, ln1_b_2, w_gu_2, w_down_2,
    w_pg_2, w_pp_2, ln2_g_2, ln2_b_2,
):
    x = first_block(
        x, c, positions, w_ada, b_ada, norm_mix, w_in, conv_w, conv_b, conv_ln_g, conv_ln_b,
        q_a_norm, w_q_b, kv_a_norm, w_kv_b, q_norm, k_norm, w_out, norm_ffn, w_group, b_group,
        w_expert, b_expert, w_gate_e, w_up_e, w_down_e,
    )
    return second_block(
        x, p_2, positions_2, ln_in_g_2, ln_in_b_2, w_in_2, attn_sinks_2, idx_k_g_2, idx_k_b_2,
        w_o_2, ln1_g_2, ln1_b_2, w_gu_2, w_down_2, w_pg_2, w_pp_2, ln2_g_2, ln2_b_2,
    )


_drawn_inputs = setup_inputs


def setup_inputs(seed=0):
    import zlib

    import numpy as np

    out = dict(_drawn_inputs(seed))
    spreads = {}
    factors = {'b_ada': 4.89,
     'norm_mix': 8.0,
     'conv_b': 8.0,
     'conv_ln_g': 8.0,
     'conv_ln_b': 8.0,
     'q_a_norm': 8.0,
     'kv_a_norm': 8.0,
     'q_norm': 8.0,
     'k_norm': 8.0,
     'norm_ffn': 7.461,
     'b_group': 64.0,
     'b_expert': 8.0,
     'attn_sinks_2': 8.0,
     'idx_k_g_2': 64.0,
     'idx_k_b_2': 64.0}
    for name, (base, spread) in spreads.items():
        noise = np.random.default_rng([zlib.crc32(name.encode()), seed]).standard_normal(out[name].shape)
        drawn = base * np.exp(spread * noise) if base else spread * noise
        out[name] = __import__('jax').numpy.asarray(drawn.astype(out[name].dtype))
    for name, factor in factors.items():
        out[name] = (out[name] * factor).astype(out[name].dtype)
    return out
```

```python
from contextlib import ExitStack

import numpy as np
import concourse.bass as bass
from concourse import mybir

P = 128
F32, BF16, I32 = mybir.dt.float32, mybir.dt.bfloat16, mybir.dt.int32
ALU = mybir.AluOpType
ACT = mybir.ActivationFunctionType
AX = mybir.AxisListType.X

S, D = 512, 1024
T, C8 = S // P, D // P
CONV, TAPS = 512, 31
MC = CONV // P
PAD = TAPS - 1
NH, NOPE, ROPE, VD = 8, 64, 32, 64
QK = NOPE + ROPE
QR, KR = D // 4, D // 8
LAT = QR + KR + ROPE
IN1 = 2 * CONV + LAT
CHUNK = 64
NG, EPG = 4, 8
NE = NG * EPG
FE = D // 4
EPS, LN_EPS = 1e-6, 1e-5
NEG = -1e30

HD = 64
FF = 2816
FC = FF // P
PLE = 256
KTOP = 128
LAYERS = 2
ALPHA = (2 * LAYERS) ** 0.25
IXH, IXD = 8, 32
IN2 = 1704

SLOT = C8 * 2 * FE + 2 * D
XCOLS = 2 * S + P
ROUNDS = S // P
ARENA = 53200
CREDIT = 4

THETA = 10000.0
TWO_PI = [6.28125, 0.0019350051879882812, 3.0199159819567e-07]
ROUND = 12582912.0


QA, KA, VA, QB, KB, VB, QI, KI, WI = 0, 512, 640, 768, 1280, 1344, 1408, 1664, 1696
IN_CUTS = [(QI, IN2), (QA, KA), (KA, QB), (QB, KB), (KB, QI)]
TURNED = [("qi", 0), ("qi", 1), ("ki", 0), ("ka", 0), ("ka", 1), ("qa", 0), ("qa", 1), ("qa", 2), ("qa", 3),
          ("kb", 0), ("qb", 0), ("qb", 1), ("qb", 2), ("qb", 3)]
UNITS = [(kind, t, h) for kind in "ab" for t in range(T) for h in range(8)]
TAKEN = -3e38
PICKS = KTOP // 8


class Banks:

    def __init__(self, before=None):
        self.before = before or [0] * 8
        self.uses = [0] * 8
        self.where = {}
        self.next = 0

    def take(self, key, bank=None, among=8):
        if bank is None:
            bank = self.next % among
            self.next = bank + 1
        self.where[key] = (bank, self.uses[bank])
        self.uses[bank] += 1


class Chain:

    def __init__(self, eng, sem):
        self.eng, self.sem, self.n = eng, sem, 0

    def mark(self, ins):
        ins.then_inc(self.sem, 1)
        self.n += 1

    def settle(self):
        self.eng.wait_ge(self.sem, self.n)

    def link(self, ins):
        self.mark(ins)
        self.settle()

    def restart(self):
        self.eng.sem_clear(self.sem)
        self.n = 0


def plan_first():
    b = Banks()
    for j in range(4):
        b.take(("ada", j))
    b.take(("taps",))
    b.take(("modT", 0))
    for c in range(C8):
        b.take(("hT", c))
    for m in range(MC):
        b.take(("val", m))
        b.take(("gate", m))
    for t in range(T):
        b.take(("lat", t))
    for n in range(3):
        b.take(("latT", n))
    for t in range(T):
        for half in range(2):
            b.take(("q", t, half))
            b.take(("kv", t, half))
    for j in range(4, 12):
        b.take(("ada", j))
    b.take(("modT", 1))
    for h in range(NH):
        b.take(("qT", h))
        b.take(("kT", h))
    b.next = 0
    for t in range(T):
        b.take(("o", t), bank=6 + t % 2)
        for h in range(NH):
            b.take(("s", t, h), among=6)
            b.take(("pT", t, h), among=6)
    b.next = 0
    for j in range(4):
        b.take(("oT", j))
    b.take(("mean",))
    b.take(("var",))
    for t in range(T):
        for half in range(2):
            b.take(("mix", t, half))
    for c in range(C8):
        b.take(("h2T", c))
    for t in range(T):
        b.take(("logit", t))
    b.take(("rank",))
    b.take(("slots",))
    for g in range(2):
        for c in range(C8):
            b.take(("xsT", g, c))
    return b


def plan_layer(before):
    b = Banks(before)
    for c in range(C8):
        b.take(("xT", c))
    for j in range(len(IN_CUTS)):
        for t in range(T):
            b.take(("in", t, j))
    for j in TURNED:
        b.take(j)
    b.next = 0
    for t in range(1, T):
        for h in range(IXH):
            b.take(("ix", t, h), among=6)
    b.next = 0
    for n, (kind, t, h) in enumerate(UNITS):
        if h == 0:
            b.take(("o", kind, t), bank=6 + (n // 8) % 2)
        b.take(("s", kind, t, h), among=6)
        b.take(("pT", kind, t, h), among=6)
    b.next = 0
    for j in range(C8):
        b.take(("oT", j))
    for t in range(T):
        for half in range(2):
            b.take(("mix", t, half))
    for c in range(C8):
        b.take(("x1T", c))
    for c in range(2):
        b.take(("plT", c))
    for t in range(T):
        for half in range(2):
            b.take(("pg", t, half))
            b.take(("pp", t, half))
    for t in range(T):
        for half in range(2):
            b.take(("dn", t, half), bank=2 * t + half)
    return b


def build(nc, i, out, stop=None):
    ctx = ExitStack()
    with ctx:
        arena = ctx.enter_context(nc.sbuf_tensor("arena", [P, ARENA], F32))

        def at(off, *shape, dt=F32):
            n = int(np.prod(shape))
            ap = arena[:, off:off + n]
            if dt == BF16:
                ap = arena[:, off:off + n // 2].bitcast(BF16)
            elif dt == I32:
                ap = ap.bitcast(I32)
            if len(shape) == 2:
                return ap.rearrange("p (a b) -> p a b", a=shape[0])
            if len(shape) == 3:
                return ap.rearrange("p (a b c) -> p a b c", a=shape[0], b=shape[1])
            if len(shape) == 4:
                return ap.rearrange("p (a b c d) -> p a b c d", a=shape[0], b=shape[1], c=shape[2])
            return ap

        cursor = [0]

        def new(*shape, dt=F32):
            o = cursor[0]
            n = int(np.prod(shape))
            cursor[0] += (n + 1) // 2 if dt == BF16 else n
            cursor[0] += cursor[0] % 2
            return at(o, *shape, dt=dt)

        def sem(name):
            return ctx.enter_context(nc.semaphore(name))

        bank = [ctx.enter_context(nc.psum_tensor(f"bank{n}", [P, 512], F32)) for n in range(8)]
        bank_full = [sem(f"bank_full{n}") for n in range(8)]
        bank_free = [sem(f"bank_free{n}") for n in range(8)]

        ident = new(P)
        ones = new(P)
        before_me = new(P)
        ident_b = new(P, dt=BF16)
        chunk_mask = new(P, dt=BF16)
        own_mask = new(P, dt=BF16)
        prev_mask = new(P, dt=BF16)
        freqs = new(48)
        pos_i = new(2, T, dt=I32)
        pos = new(2, T)
        trig = new(2, 2, T, 16)
        trig64 = new(2, T, 32)
        half_neg = new(T)
        eps_col = new(2)
        first_small = cursor[0]
        c_in = new(C8)
        c_silu = new(C8)
        b_ada = new(6, C8)
        g_mix = new(C8)
        g_ffn = new(C8)
        mod = new(4, C8)
        conv_w = new(MC, TAPS)
        conv_b = new(MC)
        cln_g = new(MC)
        cln_b = new(MC)
        qa_g = new(2)
        kva_g = new(1)
        qn_g = new(QK)
        kn_g = new(QK)
        b_route = new(NG + NE)
        ss = new(T)
        rstd = new(T)
        ss_q = new(2, T)
        r_q = new(2, T)
        hss = new(2, T, NH)
        hr = new(2, T, NH)
        mx = new(T, NH)
        nmx = new(T, NH)
        lsum = new(T, NH)
        rl = new(T, NH)
        end_small, cursor[0] = cursor[0], first_small
        sinks = new(8)
        nsinks = new(8)
        ix_g = new(IXD)
        ix_b = new(IXD)
        wi = new(T, IXH)
        mx2 = new(2, T, 8)
        nmx2 = new(2, T, 8)
        ls2 = new(2, T, 8)
        es2 = new(T, 8)
        rl2 = new(2, T, 8)
        top8 = new(8)
        bst = new(T, 2, 6)
        bag = new(T, 2)
        lrs = new(T)
        assert cursor[0] <= end_small
        cursor[0] = end_small
        gate_a = new(D)
        gate_f = new(D)
        X = new(T, D)
        H = new(T, D)
        HT = new(C8, S)
        base = cursor[0]
        rt0 = base

        ada_w = [at(base, C8, 512), at(base + 4096, C8, 512)]
        w_out = at(base, C8, D)
        off = base + 8192
        w_in = at(off, C8, IN1)
        QT = at(off, NH, S)
        KT = at(off + NH * S, NH, S)
        V = at(off + 2 * NH * S, T, NH * VD)
        off += C8 * IN1
        w_q = at(off, 2, NH * QK)
        off += 2 * NH * QK
        w_kv = at(off, NH * (NOPE + VD))
        off += NH * (NOPE + VD)
        w_route = at(off, C8, NG + NE)
        off += C8 * (NG + NE)
        U = at(off, MC, PAD + S)
        off += MC * (PAD + S)
        DW = at(off, MC, S)
        mod_row0 = at(off, 2048)
        off += MC * S
        LATB = at(off, T, LAT)
        tap_rows = at(off, CONV)
        latT = at(off + T * LAT, 3, S)
        Pr = at(off, 3, S)
        PT = at(off + 3 * S, 3, S)
        mod_row1 = at(off, 2048)
        off += T * LAT + 3 * S
        K = at(off, T, NH, QK)
        off += T * NH * QK
        c_wide = at(off, C8, P)
        off += C8 * P
        junk = at(off, 256)
        off += 256
        sig = at(off, 2, 512)
        sqs = at(off, NH, QK)
        stat = at(off, 2, 512)
        xtmp = at(off + 1024, 2, 512)
        off += 2048
        assert off <= ARENA, off
        H0 = cursor[0] - C8 * S - T * D
        Q = at(H0, T, NH, QK)
        rope_t = QT.rearrange("p h n -> p (h n)")[:, 0:4 * T * NH * 16].rearrange("p (k n) -> p k n", k=4)
        O = at(H0, T, NH * VD)
        mixT = HT

        ring = [at(base + n * SLOT, C8, 2, FE) for n in range(4)]
        ring_d = [at(base + n * SLOT + C8 * 2 * FE, 2, D) for n in range(4)]
        stage = [at(base + 3 * SLOT, T, D), H]
        Yin = at(base, T, 2, D)
        off = base + 4 * SLOT
        XsT = at(off, C8, XCOLS)
        off += C8 * XCOLS
        XW = [at(cursor[0] - C8 * S + n * C8 * P, C8, P) for n in range(2)]
        off2 = cursor[0] - C8 * S + 2 * C8 * P
        SG = at(off2, 2, FE)
        A = at(off2 + 2 * FE, 2, FE)
        AT = at(off2 + 4 * FE, 2, 2, P)
        Y = at(H0, 4, D)

        def route(*shape, dt=F32):
            nonlocal off
            ap = at(off, *shape, dt=dt)
            off += int(np.prod(shape))
            assert off <= ARENA, off
            return ap

        L = route(T, NG + NE)
        ramp = route(NE)
        slot0 = route(NE)
        ids_i = route(T, 2, dt=I32)
        ids = route(T, 2)
        gred = route(T, 4)
        geq = route(T, NG)
        gexp = route(T, NG)
        gsel = route(T, NG)
        ML = route(T, NE)
        tmp32 = route(T, NE)
        OH = [route(T, NE) for _ in range(2)]
        MM = route(T, NE)
        wts = route(T, 2)
        ered = route(T, 8)
        rank = route(T, NE)
        cnt = route(NE)
        pre = [route(NE) for _ in range(2)]
        off_e = route(NE)
        win_f = route(T, NE)
        win = route(T * NE + 2, dt=I32)
        rounds_f = route(4)
        rounds = route(2, dt=I32)
        dest_f = route(2, T, 2)
        dest = route(2, T, 2, dt=I32)
        slots_f = route(P)
        slots_i = route(P, dt=I32)
        idx_now = route(4, dt=I32)

        offB = base
        PJ = at(offB + 13632 + 8192, T, IN2)
        w_in2 = at(offB, C8, IN2)
        o = offB
        turned = {}
        for key in TURNED:
            turned[key] = at(o, S)
            o += S
        IX = at(o, 3, S)
        o += 3 * S
        SELM = at(o, 3, S, dt=BF16)
        o += 3 * S // 2
        R = at(o, 2, S)
        o += 2 * S
        Pr2 = at(o, 3, S)
        PT2 = at(o + 3 * S, 3, S)
        assert o + 6 * S <= offB + 13632
        aT = at(offB, FC, S)
        lnin_g = at(offB + 13632 + 8192, D)
        lnin_b = at(offB + 13632 + 8192 + D, D)
        w_o2 = at(offB + 13632, C8, D)
        gu = [at(offB + 13632 + n * 2 * D, 2, C8, P) for n in range(2)]
        o = offB + 13632 + 8192
        p_in = at(o, T, PLE)
        pT = at(o + T * PLE, 2, S)
        w_pp = at(o + T * PLE + 2 * S, 2, D)
        SF = at(o + T * PLE + 2 * S + 2 * D, 2, S)
        o += T * IN2
        w_pg = at(o, C8, D)
        w_dn = at(o, 8, D)
        assert o + C8 * D <= ARENA, o + C8 * D
        rt = H.rearrange("p t n -> p (t n)").rearrange("p (k n) -> p k n", k=4)
        O2 = at(H0, 2, T, 512)
        PLB = H
        lnG, lnB = gate_a, gate_f
        KD = gate_a.rearrange("p (t g n d) -> p t g n d", t=T, g=2, n=2)
        KBD = gate_f[:, 0:512].rearrange("p (t n d) -> p t n d", t=T, n=2)
        KID = gate_f[:, 512:].rearrange("p (t n d) -> p t n d", t=T, n=4)

        b1 = plan_first()
        b2 = plan_layer(b1.uses)

        class Use:

            def __init__(self, banks):
                self.b = banks

            def begin(self, pe, key, i=0):
                n, u = self.b.where[key]
                if self.b.before[n] + u > 0:
                    pe.wait_ge(bank_free[n], self.b.before[n] + u + i * self.b.uses[n])
                return bank[n]

            def full(self, ins, key):
                ins.then_inc(bank_full[self.b.where[key][0]], 1)

            def read(self, eng, key, i=0):
                n, u = self.b.where[key]
                eng.wait_ge(bank_full[n], self.b.before[n] + u + 1 + i * self.b.uses[n])
                return bank[n]

            def free(self, ins, key):
                ins.then_inc(bank_free[self.b.where[key][0]], 1)

            def evacuated(self, eng, key, i=0):
                n, u = self.b.where[key]
                eng.wait_ge(bank_free[n], self.b.before[n] + u + 1 + i * self.b.uses[n])

            def all_evacuated(self, eng, keys, i=0):
                last = {self.b.where[key][0]: key for key in sorted(keys, key=lambda k: self.b.where[k][1])}
                for key in last.values():
                    self.evacuated(eng, key, i)

        u1 = Use(b1)
        u2 = Use(b2)

        class Sig:

            def __init__(self, name, per):
                self.sem, self.per, self.n = sem(name), per, 0

            def inc(self, ins):
                ins.then_inc(self.sem, 1)
                self.n += 1

            def wait(self, eng, layer, k):
                eng.wait_ge(self.sem, layer * self.per + k)

        s_x = sem("x_loaded")
        s_small = sem("small_loaded")
        s_c = sem("c_loaded")
        s_ada = [sem("ada_loaded0"), sem("ada_loaded1")]
        s_win = sem("w_in_loaded")
        s_wq = sem("w_q_loaded")
        s_wout = sem("w_out_loaded")
        s_const = sem("constants")
        s_apart = sem("apart")
        s_silu = sem("c_silu_done")
        s_cw = sem("c_wide_done")
        s_ss = sem("square_sums")
        s_rstd = sem("rstd_done")
        s_xhat = sem("normalised")
        s_modrow = sem("mod_row_done")
        s_mod = sem("mod_done")
        s_sig = sem("gate_sigmoid")
        s_conv = sem("conv_taps_done")
        s_cent = sem("conv_centred")
        s_csq = sem("conv_squared")
        s_cstd = sem("conv_std")
        s_cnorm = sem("conv_normalised")
        s_yconv = sem("conv_out")
        s_angle = sem("angles")
        s_trig = sem("trig_done")
        s_latss = sem("latent_sums")
        s_latr = sem("latent_rstd")
        s_latn = sem("latents_normalised")
        s_hss = sem("head_sums")
        s_hstd = sem("head_std")
        s_rot = sem("heads_rotated")
        s_negmax = sem("negated_max")
        s_csum = sem("conv_squares_summed")
        s_pv = sem("values_weighted")
        s_prob = sem("probabilities")
        s_x1 = sem("x1_done")
        s_ss2 = sem("x1_square_sums")
        s_rstd2 = sem("x1_rstd")
        s_xhat2 = sem("x1_normalised")
        s_gexp = sem("group_exponentials")
        s_eexp = sem("expert_exponentials")
        s_gdiff = sem("group_differences")
        s_ediff = sem("expert_difference")
        s_masks = sem("expert_masks")
        s_dest = sem("destinations")
        s_fill = sem("slot_table_filled")
        s_slots = sem("slot_table_scattered")
        s_slotin = sem("slot_table_loaded")
        s_stage = [sem("sorted_rows0"), sem("sorted_rows1")]
        s_rounds = sem("rounds_known")
        s_pad = sem("xs_pad")
        s_w = [sem(f"expert_weights{n}") for n in range(4)]
        m_xw = sem("window_copied")
        m_gu = sem("gate_up_done")
        m_silu = sem("silu_done")
        m_a = sem("product_done")
        m_at = sem("product_transposed")
        m_atc = sem("product_copied")
        m_y = sem("down_done")
        m_ya = sem("down_copied_a")
        m_yb = sem("down_copied_b")
        m_st = [sem(f"rows_stored{n}") for n in range(4)]
        SCATTERED = 32
        s_yin = [sem(f"expert_rows_loaded{n}") for n in range(T)]
        s_x2 = sem("x2_done")
        s_lnin = sem("ln_in_loaded")
        s_mean = sem("ln_in_stats")
        s_lnr = sem("ln_in_rstd")
        a_free = sem("region_a_free")
        b_free = sem("region_b_free")
        layer_in = sem("layer_input_ready")
        d_in2 = sem("w_in2_loaded")
        d_o2 = sem("w_o_loaded")
        d_pg = sem("w_pg_loaded")
        d_sm = sem("layer_small_loaded")
        d_ln1 = sem("ln1_loaded")
        d_ln2 = sem("ln2_loaded")
        d_pp = sem("ple_loaded")
        d_gu = [sem("gate_up_loaded0"), sem("gate_up_loaded1")]
        d_dn = [sem(f"w_down_loaded{n}") for n in range(8)]
        y_kst = Sig("key_stats", 1)
        y_krs = Sig("key_rstd", 1)
        y_rot = Sig("rotated", 6)
        y_ix = Sig("index_scores_added", 3 * IXH)
        y_sel = Sig("selected", 3)
        y_neg = Sig("negated_max2", 64)
        y_pv = Sig("values_weighted2", 56)
        y_sinkd = Sig("sink_differences", T)
        y_sinke = Sig("sink_exponentials", T)
        y_mst = Sig("ln1_stats", 1)
        y_mrs = Sig("ln1_rstd", 1)
        y_mx = Sig("ln1_scaled", T)
        y_x1 = Sig("ln1_done", T)
        y_est = Sig("ln2_stats", 1)
        y_ers = Sig("ln2_rstd", 1)
        y_ex = Sig("ln2_scaled", T)
        y_dn = Sig("down_chunk_used", FC - 1)
        y_dve = Sig("ple_added", T)
        f_g = sem("ff_gate_up_done")
        f_s = sem("ff_silu_done")
        f_a = sem("ff_product_done")
        s_cmb = sem("combine_own")
        s_out = sem("out_stored")
        link_pe, link_dve, link_act, link_pool = sem("pe_own"), sem("dve_own"), sem("act_own"), sem("pool_own")

        slot_table = nc.dram_tensor("slot_table", (NE * S, 1), F32, kind="Internal").ap()
        sorted_rows = nc.dram_tensor("sorted_rows", (2 * S, D), F32, kind="Internal").ap()
        expert_rows = nc.dram_tensor("expert_rows", (2 * S, D), F32, kind="Internal").ap()

        block = ctx.enter_context(nc.Block())
        SMALL = 0

        def apart(eng):
            eng.sem_inc(s_apart, 1)

        def width(n):
            kind, t, h = UNITS[n]
            return min(t + 1, 2) * P if kind == "a" else (t + 1) * P

        def weighted2(eng, n, l):
            kind, t, h = UNITS[n]
            if h == 7:
                u2.read(eng, ("o", kind, t), l)
            else:
                y_pv.wait(eng, l, n - n // 8 + 1)

        @block.sync
        def _(sp):
            sp.dma_start(c_in, i["c"].rearrange("b (p c) -> (b p) c", c=C8)).then_inc(s_c, 16)
            def load_ada(j):
                if j >= 2:
                    u1.evacuated(sp, ("ada", j - 2))
                sp.dma_start(ada_w[j % 2], i["w_ada"][0, :, j * 512:(j + 1) * 512]
                             .rearrange("(p c) n -> p c n", c=C8)).then_inc(s_ada[j % 2], 16)

            load_ada(0)
            for t in range(T):
                sp.dma_start(X[:, t], i["x"][0, t * P:(t + 1) * P]).then_inc(s_x, 16)
            for j in range(1, 4):
                load_ada(j)
            sp.dma_start(w_in, i["w_in"][0].rearrange("(p c) n -> p c n", c=C8)).then_inc(s_win, 16)
            sp.dma_start(w_q, i["w_q_b"][0].rearrange("(c p) n -> p c n", c=2)).then_inc(s_wq, 16)
            sp.dma_start(w_kv, i["w_kv_b"][0]).then_inc(s_wq, 16)
            for j in range(4, 12):
                load_ada(j)
            for n in (10, 11):
                u1.evacuated(sp, ("ada", n))
            sp.dma_start(w_out[:, 0:4], i["w_out"][0, 0:512].rearrange("(m p) n -> p m n", p=P)).then_inc(s_wout, 16)
            sp.dma_start(w_out[:, 4:8], i["w_out"][0, 512:1024].rearrange("(m p) n -> p m n", p=P)).then_inc(s_wout, 16)
            sp.dma_start(w_route[:, :, 0:NG], i["w_group"][0].rearrange("(p c) n -> p c n", c=C8)).then_inc(s_wout, 16)
            sp.dma_start(w_route[:, :, NG:], i["w_expert"][0].rearrange("(p c) n -> p c n", c=C8)).then_inc(s_wout, 16)
            def load_expert(n, s, pre_use):
                sp.wait_ge(m_y, pre_use)
                for k, w in enumerate(("w_gate_e", "w_up_e")):
                    sp.dma_start(ring[s][:, :, k], i[w][0][bass.ds(n, 1)].rearrange("a (p c) n -> (a p) c n", c=C8)).then_inc(s_w[s], 16)
                sp.dma_start(ring_d[s], i["w_down_e"][0][bass.ds(n, 1)].rearrange("a (p c) n -> (a p) c n", c=2)).then_inc(s_w[s], 16)

            sp.wait_ge(s_x1, T)
            sp.wait_ge(s_slots, 16 * (2 * T))
            sp.dma_start(slots_f, slot_table.rearrange("(q p) o -> q (p o)", p=P)).then_inc(s_slotin, 16)
            for n in range(4):
                sp.wait_ge(m_st[n], SCATTERED)
            for g in range(2):
                for q in range(T):
                    sp.dma_start(stage[g][:, q], sorted_rows[(T * g + q) * P:(T * g + q + 1) * P]).then_inc(s_stage[g], 16)
            for c in range(C8):
                u1.evacuated(sp, ("xsT", 0, c))
            with sp.Fori(0, NE // 4) as it:
                for s in range(4):
                    load_expert(it * 4 + s, s, it * 4 + s + 1)
            sp.wait_ge(s_rounds, 1)
            n_rounds = sp.value_load(rounds[0:1, 0:1], min_val=1, max_val=ROUNDS)
            with sp.If(n_rounds > 1):
                with sp.Fori(1, n_rounds) as r:
                    with sp.Fori(0, NE // 4) as it:
                        for s in range(4):
                            load_expert(it * 4 + s, s, r * NE + it * 4 + s + 1)
            for n in range(4):
                sp.wait_ge(m_st[n], SCATTERED + 16 * (NE // 4) * n_rounds)
            for t in range(T):
                sp.dma_start(Yin[:, t], expert_rows[2 * t * P:2 * (t + 1) * P].rearrange("(p k) n -> p k n", k=2)).then_inc(s_yin[t], 16)
            sp.wait_ge(b_free, 1)
            sp.dma_start(lnin_g, i["ln_in_g_2"].partition_broadcast(P)).then_inc(s_lnin, 16)
            sp.dma_start(lnin_b, i["ln_in_b_2"].partition_broadcast(P)).then_inc(s_lnin, 16)
            with sp.Fori(0, LAYERS) as l:
                def of(name):
                    return i[name][bass.ds(l, 1)]

                sp.wait_ge(b_free, l + 1)
                sp.dma_start(w_o2, of("w_o_2").rearrange("a (m p) n -> (a p) m n", p=P)).then_inc(d_o2, 16)
                sp.wait_ge(a_free, l + 1)
                for k in range(2):
                    sp.dma_start(w_in2[:, 4 * k:4 * k + 4], of("w_in_2").rearrange("a (p c) n -> (a p) c n", c=C8)[:, 4 * k:4 * k + 4])\
                      .then_inc(d_in2, 16)
                sp.dma_start(sinks, of("attn_sinks_2").rearrange("a n -> (a n)").partition_broadcast(P)).then_inc(d_sm, 16)
                sp.dma_start(ix_g, of("idx_k_g_2").rearrange("a n -> (a n)").partition_broadcast(P)).then_inc(d_sm, 16)
                sp.dma_start(ix_b, of("idx_k_b_2").rearrange("a n -> (a n)").partition_broadcast(P)).then_inc(d_sm, 16)
                sp.dma_start(w_pg, of("w_pg_2").rearrange("a (p c) n -> (a p) c n", c=C8)).then_inc(d_pg, 16)
                u2.read(sp, ("ix", 1, 0), l)
                sp.dma_start(lnG, of("ln1_g_2").rearrange("a n -> (a n)").partition_broadcast(P)).then_inc(d_ln1, 16)
                sp.dma_start(lnB, of("ln1_b_2").rearrange("a n -> (a n)").partition_broadcast(P)).then_inc(d_ln1, 16)
                u2.read(sp, ("oT", 0), l)
                sp.dma_start(p_in, of("p_2").rearrange("l b (t p) n -> (l b p) t n", p=P)).then_inc(d_pp, 16)
                sp.dma_start(w_pp, of("w_pp_2").rearrange("a (c p) n -> (a p) c n", p=P)).then_inc(d_pp, 16)
                u2.evacuated(sp, ("mix", T - 1, 1), l)
                apart(sp)
                with sp.Fori(0, FC // 2) as it:
                    for s in range(2):
                        sp.wait_ge(f_g, l * FC + it * 2 + s - 2 + 1 + CREDIT)
                        for k in range(2):
                            sp.dma_start(gu[s][:, k], of("w_gu_2").rearrange("a (p c) (k f n) -> k f (a p) c n", c=C8, k=2, n=P)
                                         [k, bass.ds(it * 2 + s, 1)].rearrange("f p c n -> (f p) c n")).then_inc(d_gu[s], 16)
                y_x1.wait(sp, l, T)
                sp.dma_start(lnG, of("ln2_g_2").rearrange("a n -> (a n)").partition_broadcast(P)).then_inc(d_ln2, 16)
                sp.dma_start(lnB, of("ln2_b_2").rearrange("a n -> (a n)").partition_broadcast(P)).then_inc(d_ln2, 16)
                u2.read(sp, ("pp", T - 1, 1), l)
                for f in range(FC):
                    if f >= 8:
                        y_dn.wait(sp, l, f - 8 + 1)
                    sp.dma_start(w_dn[:, f % 8], of("w_down_2").rearrange("a (f p) n -> f (a p) n", p=P)[f]).then_inc(d_dn[f % 8], 16)
            sp.wait_ge(layer_in, (LAYERS + 1) * T)
            for t in range(T):
                sp.dma_start(out[0, t * P:(t + 1) * P], X[:, t]).then_inc(s_out, 16)
            sp.wait_ge(s_out, 16 * T)

        small = [
            (freqs, i["freqs"].partition_broadcast(P)),
            (pos_i[:, 0], i["positions"][0].rearrange("(t p) -> p t", p=P)),
            (pos_i[:, 1], i["positions_2"][0].rearrange("(t p) -> p t", p=P)),
            (b_ada, i["b_ada"][0].rearrange("(v p c) -> p v c", p=P, c=C8)),
            (g_mix, i["norm_mix"][0].rearrange("(p c) -> p c", c=C8)),
            (g_ffn, i["norm_ffn"][0].rearrange("(p c) -> p c", c=C8)),
            (qa_g, i["q_a_norm"][0].rearrange("(c p) -> p c", p=P)),
            (kva_g, i["kv_a_norm"][0].rearrange("(c p) -> p c", p=P)),
            (qn_g, i["q_norm"][0].partition_broadcast(P)),
            (kn_g, i["k_norm"][0].partition_broadcast(P)),
            (conv_b, i["conv_b"][0].rearrange("(m p) -> p m", p=P)),
            (cln_g, i["conv_ln_g"][0].rearrange("(m p) -> p m", p=P)),
            (cln_b, i["conv_ln_b"][0].rearrange("(m p) -> p m", p=P)),
            (b_route[:, 0:NG], i["b_group"][0].partition_broadcast(P)),
            (b_route[:, NG:], i["b_expert"][0].partition_broadcast(P)),
            (gate_a, i["b_ada"][0, 2 * D:3 * D].partition_broadcast(P)),
            (gate_f, i["b_ada"][0, 5 * D:6 * D].partition_broadcast(P)),
        ]
        small += [(tap_rows[0:TAPS], i["conv_w"][0])]
        SMALL = 16 * len(small)

        @block.gpsimd
        def _(pool):
            own = Chain(pool, link_pool)
            for k, (dst, src) in enumerate(small):
                pool.dma_start(dst, src, allow_slow_non_contiguous=True).then_inc(s_small, 16)
            own.mark(pool.memset(ident, 0.0))
            own.mark(pool.memset(ones, 1.0))
            own.mark(pool.memset(before_me, 1.0))
            own.mark(pool.memset(chunk_mask, 0.0))
            own.mark(pool.memset(own_mask, 0.0))
            own.mark(pool.memset(prev_mask, 0.0))
            own.mark(pool.memset(half_neg, -0.5))
            own.mark(pool.memset(eps_col, EPS))
            own.mark(pool.memset(U[:, :, 0:PAD], 0.0))
            own.settle()
            own.mark(pool.affine_select(ident, ident, [[-1, P]], ALU.not_equal, 1.0, base=0, channel_multiplier=1))
            own.mark(pool.affine_select(before_me, before_me, [[1, P]], ALU.is_gt, 0.0, base=0, channel_multiplier=-1))
            own.mark(pool.memset(chunk_mask[0:CHUNK, CHUNK:P], NEG))
            own.mark(pool.affine_select(own_mask, own_mask, [[-1, P]], ALU.is_ge, NEG, base=0, channel_multiplier=1))
            own.mark(pool.affine_select(prev_mask, prev_mask, [[1, P]], ALU.is_gt, NEG, base=0, channel_multiplier=-1))
            own.settle()
            pool.tensor_copy(ident_b, ident).then_inc(s_const, 1)
            pool.wait_ge(s_ss, T)
            own.link(pool.tensor_scalar(rstd, ss, 1.0 / D, EPS, ALU.mult, ALU.add))
            pool.tensor_tensor(rstd, rstd, half_neg, ALU.pow).then_inc(s_rstd, 1)
            pool.wait_ge(s_latss, 2 * T)
            own.mark(pool.tensor_scalar(r_q[:, 0], ss_q[:, 0], 1.0 / QR, EPS, ALU.mult, ALU.add))
            own.mark(pool.tensor_scalar(r_q[:, 1], ss_q[:, 1], 1.0 / KR, EPS, ALU.mult, ALU.add))
            own.settle()
            pool.tensor_tensor(r_q[:, 0], r_q[:, 0], half_neg, ALU.pow).then_inc(s_latr, 1)
            pool.tensor_tensor(r_q[:, 1], r_q[:, 1], half_neg, ALU.pow).then_inc(s_latr, 1)
            pool.wait_ge(s_x1, T)
            own.mark(pool.iota(ramp, [[-1, NE]], base=NE, channel_multiplier=0, allow_small_or_imprecise_dtypes=True))
            own.mark(pool.iota(slot0, [[S, NE]], base=0, channel_multiplier=0, allow_small_or_imprecise_dtypes=True))
            own.mark(pool.iota(ids, [[2 * P, T], [1, 2]], base=0, channel_multiplier=2, allow_small_or_imprecise_dtypes=True))
            own.mark(pool.memset(slots_f, 1e6))
            own.settle()
            pool.memset(XsT[:, :, 2 * S:], 0.0).then_inc(s_pad, 1)
            pool.dma_start(slot_table.rearrange("(q p) o -> q (p o)", p=P), slots_f).then_inc(s_fill, 16)
            pool.wait_ge(s_ss2, T)
            own.link(pool.tensor_scalar(rstd, ss, 1.0 / D, EPS, ALU.mult, ALU.add))
            pool.tensor_tensor(rstd, rstd, half_neg, ALU.pow).then_inc(s_rstd2, 1)
            pool.wait_ge(s_dest, 1)
            pool.wait_ge(s_fill, 16)
            for t in range(T):
                for k in range(2):
                    pool.indirect_dma_start(slot_table, bass.IndirectOffsetOnAxis(dest[:, 1, t, k:k + 1], 0),
                                            ids[:, t, k:k + 1], None).then_inc(s_slots, 16)
            for t in range(T):
                for k in range(2):
                    pool.indirect_dma_start(sorted_rows, bass.IndirectOffsetOnAxis(dest[:, 0, t, k:k + 1], 0),
                                            H[:, t], None).then_inc(m_st[t], 16)
            u1.evacuated(pool, ("slots",))
            last_row = pool.to_reg(2 * S - 1)
            n_rounds = pool.value_load(rounds[0:1, 0:1], min_val=1, max_val=ROUNDS)
            with pool.Fori(0, n_rounds) as r:
                with pool.Fori(0, NE // 4) as it:
                    own.restart()
                    for s in range(4):
                        n = r * NE + it * 4 + s
                        pool.wait_ge(m_st[s], SCATTERED + 16 * (r * (NE // 4) + it))
                        own.link(pool.tensor_copy(idx_now[:, s:s + 1], slots_i[:, bass.ds((it * 4 + s) * ROUNDS + r, 1)]))
                        pool.wait_ge(m_ya, n + 1 + CREDIT)
                        pool.wait_ge(m_yb, n + 1 + CREDIT)
                        apart(pool)
                        pool.indirect_dma_start(expert_rows, bass.IndirectOffsetOnAxis(idx_now[:, s:s + 1], 0), Y[:, s], None,
                                                bounds_check=last_row, oob_is_err=False).then_inc(m_st[s], 16)
            own.settle()

            def rstd_of(stats, done, width_eps):
                apart(pool)
                own.link(pool.tensor_scalar(lrs, stats, width_eps, None, ALU.add))
                done(pool.tensor_tensor(lrs, lrs, half_neg, ALU.pow))

            pool.wait_ge(s_mean, T)
            rstd_of(bag[:, :, 1], lambda ins: ins.then_inc(s_lnr, 1), LN_EPS)
            with pool.Fori(0, LAYERS) as l:
                own.restart()
                y_kst.wait(pool, l, 1)
                rstd_of(bag[:, :, 1], y_krs.inc, LN_EPS)
                y_mst.wait(pool, l, 1)
                rstd_of(bag[:, :, 1], y_mrs.inc, LN_EPS)
                for t in range(T):
                    y_mx.wait(pool, l, t + 1)
                    y_x1.inc(pool.tensor_tensor(X[:, t], X[:, t], lnB, ALU.add))
                y_est.wait(pool, l, 1)
                rstd_of(bag[:, :, 1], y_ers.inc, LN_EPS)
                for t in range(T):
                    y_ex.wait(pool, l, t + 1)
                    pool.tensor_tensor(X[:, t], X[:, t], lnB, ALU.add).then_inc(layer_in, 1)
                own.settle()

        @block.scalar
        def _(act):
            own = Chain(act, link_act)
            act.wait_ge(s_c, 16)
            act.activation(c_silu, c_in, ACT.Silu).then_inc(s_silu, 1)
            act.wait_ge(s_x, 16 * T)
            for t in range(T):
                act.activation(HT[:, t * 2:t * 2 + 2], X[:, t], ACT.Square, accum_out=ss[:, t:t + 1]).then_inc(s_ss, 1)
            act.wait_ge(s_angle, 1)
            own.mark(act.activation(trig[:, 0], trig[:, 0], ACT.Sin))
            own.mark(act.activation(trig[:, 1], trig[:, 1], ACT.Sin))
            act.activation(trig64, trig64, ACT.Sin).then_inc(s_trig, 1)
            for j in range(4):
                ps = u1.read(act, ("ada", j))
                u1.free(act.copy(mod_row0[:, j * 512:(j + 1) * 512], ps[:]), ("ada", j))
            act.wait_ge(s_mod, 1)
            for c in range(0, C8, 2):
                ps = u1.read(act, ("hT", c))
                u1.free(act.activation(HT[:, c], ps[:], ACT.Identity, bias=mod[:, 0, c:c + 1],
                                       scale=mod[:, 1, c:c + 1]), ("hT", c))
            for m in range(MC):
                ps = u1.read(act, ("gate", m))
                if m >= 2:
                    u1.evacuated(act, ("val", m - 2))
                u1.free(act.activation(sig[:, m % 2], ps[:], ACT.Sigmoid), ("gate", m))
            for t in range(T):
                ps = u1.read(act, ("lat", t))
                u1.free(act.copy(LATB[:, t], ps[:, 0:LAT]), ("lat", t))
                u1.evacuated(act, ("lat", t))
                if t:
                    act.wait_ge(s_latss, 2 * t)
                act.activation(junk[:, 0:QR], LATB[:, t, 0:QR], ACT.Square, accum_out=ss_q[:, 0, t:t + 1]).then_inc(s_latss, 1)
                act.wait_ge(s_latss, 2 * t + 1)
                act.activation(junk[:, 0:KR], LATB[:, t, QR:QR + KR], ACT.Square, accum_out=ss_q[:, 1, t:t + 1]).then_inc(s_latss, 1)
            for t in range(T):
                for half in range(2):
                    hs = slice(4 * half, 4 * half + 4)
                    ps = u1.read(act, ("q", t, half))
                    u1.free(act.copy(Q[:, t, hs], ps[:, 0:384].rearrange("p (h d) -> p h d", d=QK)), ("q", t, half))
                    ps = u1.read(act, ("kv", t, half))
                    kv = ps[:].rearrange("p (h d) -> p h d", d=NOPE + VD)
                    own.mark(act.copy(K[:, t, hs, 0:NOPE], kv[:, :, 0:NOPE]))
                    u1.free(act.copy(V[:, t, 256 * half:256 * half + 256].rearrange("p (h d) -> p h d", d=VD),
                                     kv[:, :, NOPE:]), ("kv", t, half))
            for j in (6, 7, 8, 9):
                ps = u1.read(act, ("ada", j))
                u1.free(act.copy(mod_row1[:, (j - 6) * 512:(j - 5) * 512], ps[:]), ("ada", j))
            act.wait_ge(s_hss, 1)
            act.activation(hr, hss, ACT.Sqrt).then_inc(s_hstd, 1)
            for h in range(NH):
                ps = u1.read(act, ("qT", h))
                u1.free(act.copy(QT[0:QK, h], ps[0:QK, :]), ("qT", h))
            n = 0
            for t in range(T):
                for h in range(NH):
                    w = (t + 1) * P
                    act.wait_ge(s_negmax, n + 1)
                    if n >= 3:
                        u1.evacuated(act, ("pT",) + divmod(n - 3, NH))
                    ps = u1.read(act, ("s", t, h))
                    ins = act.activation(Pr[:, n % 3, 0:w], ps[:, 0:w], ACT.Exp, bias=nmx[:, t, h:h + 1],
                                         scale=QK ** -0.5, accum_out=lsum[:, t, h:h + 1])
                    u1.free(ins, ("s", t, h))
                    n += 1
            for j in range(4):
                ps = u1.read(act, ("oT", j))
                u1.free(act.copy(mixT[:, 4 + j], ps[:]), ("oT", j))
            for m in range(MC):
                act.wait_ge(s_cent, m + 1)
                if m >= 2:
                    act.wait_ge(s_csum, m - 1)
                act.activation(stat[:, m % 2], DW[:, m], ACT.Square).then_inc(s_csq, 1)
            ps = u1.read(act, ("var",))
            u1.free(act.activation(stat[:, 0], ps[:], ACT.Sqrt, bias=eps_col[:, 0:1], scale=1.0 / CONV), ("var",))
            for m in range(MC):
                act.wait_ge(s_cnorm, m + 1)
                act.activation(mixT[:, m], DW[:, m], ACT.Silu, bias=cln_b[:, m:m + 1], scale=cln_g[:, m:m + 1]).then_inc(s_yconv, 1)
            for t in range(T):
                act.wait_ge(s_x1, t + 1)
                act.activation(H[:, t], X[:, t], ACT.Square, accum_out=ss[:, t:t + 1]).then_inc(s_ss2, 1)
            for c in range(0, C8, 2):
                ps = u1.read(act, ("h2T", c))
                u1.free(act.activation(HT[:, c], ps[:], ACT.Identity, bias=mod[:, 2, c:c + 1],
                                       scale=mod[:, 3, c:c + 1]), ("h2T", c))
            act.wait_ge(s_gdiff, 1)
            act.activation(gexp, gexp, ACT.Exp).then_inc(s_gexp, 1)
            act.wait_ge(s_ediff, 1)
            act.activation(ered[:, :, 4], ered[:, :, 4], ACT.Exp).then_inc(s_eexp, 1)
            for g in range(2):
                for c in range(0, C8, 2):
                    ps = u1.read(act, ("xsT", g, c))
                    u1.free(act.activation(XsT[:, c, g * S:(g + 1) * S], ps[:], ACT.Identity, bias=mod[:, 2, c:c + 1],
                                           scale=mod[:, 3, c:c + 1]), ("xsT", g, c))
            act.sem_inc(m_silu, CREDIT)
            act.sem_inc(m_atc, CREDIT)
            act.sem_inc(m_yb, CREDIT)

            def silu(n, s):
                act.wait_ge(m_gu, n + 1 + CREDIT)
                act.wait_ge(m_a, n - 2 + 1 + CREDIT)
                act.activation(SG[:, s % 2], bank[s % 2][:, 0:FE], ACT.Silu).then_inc(m_silu, 1)

            def copy_at(n, s):
                act.wait_ge(m_at, n + 1 + CREDIT)
                act.wait_ge(m_y, n - 2 + 1 + CREDIT)
                act.copy(AT[:, s % 2], bank[2 + s % 2][:, 0:2 * P].rearrange("p (c m) -> p c m", c=2)).then_inc(m_atc, 1)

            def copy_y(n, it, s):
                act.wait_ge(m_y, n + 1 + CREDIT)
                act.wait_ge(m_st[s], SCATTERED + 16 * it)
                act.copy(Y[:, s, 512:], bank[5 + 2 * (s % 2)][:]).then_inc(m_yb, 1)

            act.wait_ge(s_rounds, 1)
            n_rounds = act.value_load(rounds[0:1, 0:1], min_val=1, max_val=ROUNDS)
            with act.Fori(0, n_rounds) as r:
                with act.Fori(0, NE // 4) as it:
                    n = r * NE + it * 4
                    for s in range(4):
                        silu(n + s, s)
                        if s:
                            copy_y(n + s - 1, r * (NE // 4) + it, s - 1)
                        copy_at(n + s, s)
                    copy_y(n + 3, r * (NE // 4) + it, 3)
            act.sem_inc(f_s, CREDIT)
            with act.Fori(0, LAYERS) as l:
                own.restart()
                for c in range(0, C8, 2):
                    ps = u2.read(act, ("xT", c), l)
                    u2.free(act.copy(HT[:, c], ps[:]), ("xT", c))
                for j, (a, b) in enumerate(IN_CUTS):
                    for t in range(T):
                        ps = u2.read(act, ("in", t, j), l)
                        u2.free(act.copy(PJ[:, t, a:b], ps[:, 0:b - a]), ("in", t, j))
                for n, key in enumerate(TURNED):
                    if n % 2 == 0:
                        ps = u2.read(act, key, l)
                        u2.free(act.copy(turned[key], ps[:]), key)
                n = 0
                for t in range(1, T):
                    for h in range(IXH):
                        if n >= 2:
                            y_ix.wait(act, l, n - 1)
                        ps = u2.read(act, ("ix", t, h), l)
                        u2.free(act.activation(R[:, n % 2, 0:(t + 1) * P], ps[:, 0:(t + 1) * P], ACT.Relu), ("ix", t, h))
                        n += 1

                def take_pt(n):
                    kind, t, h = UNITS[n]
                    w = width(n)
                    if n >= 3:
                        weighted2(act, n - 3, l)
                    ps = u2.read(act, ("pT", kind, t, h), l)
                    u2.free(act.copy(PT2[:, n % 3, 0:w], ps[:, 0:w]), ("pT", kind, t, h))

                for n, (kind, t, h) in enumerate(UNITS):
                    w = width(n)
                    kk = 0 if kind == "a" else 1
                    y_neg.wait(act, l, n + 1)
                    if n >= 3:
                        u2.evacuated(act, ("pT",) + UNITS[n - 3], l)
                    ps = u2.read(act, ("s", kind, t, h), l)
                    u2.free(act.activation(Pr2[:, n % 3, 0:w], ps[:, 0:w], ACT.Exp, bias=nmx2[:, kk, t, h:h + 1],
                                           scale=HD ** -0.5, accum_out=ls2[:, kk, t, h:h + 1]), ("s", kind, t, h))
                    if 2 <= n < 34:
                        take_pt(n - 2)
                    if kind == "a" and h == 7:
                        y_sinkd.wait(act, l, t + 1)
                        y_sinke.inc(act.activation(es2[:, t], es2[:, t], ACT.Exp))
                for j in range(0, C8, 2):
                    ps = u2.read(act, ("oT", j), l)
                    u2.free(act.copy(HT[:, j], ps[:]), ("oT", j))
                for c in range(0, C8, 2):
                    ps = u2.read(act, ("x1T", c), l)
                    u2.free(act.copy(HT[:, c], ps[:]), ("x1T", c))
                ps = u2.read(act, ("plT", 0), l)
                u2.free(act.copy(pT[:, 0], ps[:]), ("plT", 0))
                n = 0
                for t in range(T):
                    for half in range(2):
                        if n >= 2:
                            u2.evacuated(act, ("pp", (n - 2) // 2, n % 2), l)
                        ps = u2.read(act, ("pg", t, half), l)
                        u2.free(act.activation(SF[:, n % 2], ps[:], ACT.Sigmoid), ("pg", t, half))
                        n += 1
                with act.Fori(0, FC // 2) as it:
                    for s in range(2):
                        n = l * FC + it * 2 + s
                        act.wait_ge(f_g, n + 1 + CREDIT)
                        act.wait_ge(f_a, n - 2 + 1 + CREDIT)
                        act.activation(SF[:, s], bank[2 * s][:], ACT.Silu).then_inc(f_s, 1)

        @block.vector
        def _(dve):
            own = Chain(dve, link_dve)
            dve.wait_ge(s_silu, 1)
            dve.tensor_copy(c_wide, c_silu.unsqueeze(2).broadcast_to([P, C8, P])).then_inc(s_cw, 1)
            dve.wait_ge(s_small, SMALL)
            own.link(dve.tensor_copy(pos, pos_i))

            def angles(cos, sin, blk, f0, n):
                for t in range(T):
                    own.mark(dve.tensor_scalar(sin[:, t], freqs[:, f0:f0 + n], pos[:, blk, t:t + 1], None, ALU.mult))
                own.settle()
                own.link(dve.tensor_scalar(cos, sin, 1 / (2 * np.pi), ROUND, ALU.mult, ALU.add))
                own.link(dve.tensor_scalar(cos, cos, -ROUND, None, ALU.add))
                for part in TWO_PI:
                    own.link(dve.scalar_tensor_tensor(sin, cos, -part, sin, ALU.mult, ALU.add))
                own.link(dve.tensor_scalar(sin, sin, 3.1415925, -3.1415925, ALU.min, ALU.max))
                own.link(dve.tensor_scalar(cos, sin, -1.0, None, ALU.mult))
                own.link(dve.tensor_tensor(cos, cos, sin, ALU.min))
                own.mark(dve.tensor_scalar(cos, cos, float(np.pi / 2), None, ALU.add))

            angles(trig[:, 0, 0], trig[:, 0, 1], 0, 0, 16)
            angles(trig[:, 1, 0], trig[:, 1, 1], 1, 0, 16)
            angles(trig64[:, 0], trig64[:, 1], 1, 16, 32)
            own.settle()
            dve.tensor_copy(ss_q[:, 0, 0:1], pos[:, 0, 0:1]).then_inc(s_angle, 1)
            ps = u1.read(dve, ("taps",))
            u1.free(dve.tensor_copy(conv_w, ps[:, 0:MC * 32].rearrange("p (m k) -> p m k", m=MC)[:, :, 0:TAPS]), ("taps",))
            dve.wait_ge(s_rstd, 1)
            for t in range(T):
                dve.tensor_scalar(H[:, t], X[:, t], rstd[:, t:t + 1], None, ALU.mult).then_inc(s_xhat, 1)

            def modulation(n, gain):
                ps = u1.read(dve, ("modT", n))
                pm = ps[:, 0:2 * C8].rearrange("p (v c) -> p v c", v=2)
                own.link(dve.tensor_tensor(mod[:, 2 * n:2 * n + 2], pm, b_ada[:, 3 * n:3 * n + 2], ALU.add))
                u1.free(dve.tensor_scalar(mod[:, 2 * n + 1], mod[:, 2 * n + 1], 1.0, None, ALU.add), ("modT", n))
                u1.evacuated(dve, ("modT", n))
                dve.tensor_tensor(mod[:, 2 * n + 1], mod[:, 2 * n + 1], gain, ALU.mult).then_inc(s_mod, 1)

            modulation(0, g_mix)
            dve.wait_ge(s_mod, 1)
            for c in range(1, C8, 2):
                ps = u1.read(dve, ("hT", c))
                u1.free(dve.tensor_scalar(HT[:, c], ps[:], mod[:, 1, c:c + 1], mod[:, 0, c:c + 1],
                                          ALU.mult, ALU.add), ("hT", c))
            for m in range(MC):
                u1.evacuated(dve, ("gate", m))
                ps = u1.read(dve, ("val", m))
                ins = dve.tensor_tensor(U[:, m, PAD:], ps[:], sig[:, m % 2], ALU.mult)
                u1.free(ins, ("val", m))

            dve.wait_ge(s_latr, 2)
            for t in range(T):
                dve.tensor_scalar(LATB[:, t, 0:QR], LATB[:, t, 0:QR], r_q[:, 0, t:t + 1], None, ALU.mult).then_inc(s_latn, 1)
                dve.tensor_scalar(LATB[:, t, QR:QR + KR], LATB[:, t, QR:QR + KR], r_q[:, 1, t:t + 1], None, ALU.mult).then_inc(s_latn, 1)
            for n in range(3):
                ps = u1.read(dve, ("latT", n))
                gain = qa_g[:, n:n + 1] if n < 2 else kva_g
                u1.free(dve.tensor_scalar(latT[:, n], ps[:], gain, None, ALU.mult), ("latT", n))

            def conv(m, k):
                if k == 0:
                    u1.evacuated(dve, ("val", m))
                    own.mark(dve.tensor_scalar(DW[:, m], U[:, m, 0:S], conv_w[:, m, 0:1], conv_b[:, m:m + 1], ALU.mult, ALU.add))
                    return
                own.settle()
                ins = dve.scalar_tensor_tensor(DW[:, m], U[:, m, k:k + S], conv_w[:, m, k:k + 1], DW[:, m], ALU.mult, ALU.add)
                if k < TAPS - 1:
                    own.mark(ins)
                else:
                    ins.then_inc(s_conv, 1)

            for k in range(TAPS):
                conv(0, k)
            for t in range(T):
                for half in range(2):
                    u1.evacuated(dve, ("kv", t, half))
                    u1.evacuated(dve, ("q", t, half))
                own.link(dve.tensor_copy(K[:, t, :, NOPE:], LATB[:, t, LAT - ROPE:].unsqueeze(1).broadcast_to([P, NH, ROPE])))
                for n, B in ((0, Q), (1, K)):
                    own.link(dve.tensor_tensor(sqs, B[:, t], B[:, t], ALU.mult))
                    own.link(dve.tensor_reduce(hss[:, n, t], sqs, AX, ALU.add))
            dve.tensor_scalar(hss, hss, 1.0 / QK, EPS, ALU.mult, ALU.add).then_inc(s_hss, 1)
            for j in (4, 5):
                ps = u1.read(dve, ("ada", j))
                g = gate_a[:, (j % 2) * 512:(j % 2 + 1) * 512]
                u1.free(dve.tensor_tensor(g, ps[:], g, ALU.add), ("ada", j))
            dve.wait_ge(s_hstd, 1)
            own.link(dve.reciprocal(hr, hr))
            for n, (B, g) in enumerate(((Q, qn_g), (K, kn_g))):
                for t in range(T):
                    own.mark(dve.tensor_tensor(B[:, t], B[:, t], hr[:, n, t].unsqueeze(2).broadcast_to([P, NH, QK]), ALU.mult))
                own.settle()
                for t in range(T):
                    own.mark(dve.tensor_tensor(B[:, t], B[:, t], g.unsqueeze(1).broadcast_to([P, NH, QK]), ALU.mult))
                own.settle()
                x1, x2 = B[:, :, :, NOPE:NOPE + 16], B[:, :, :, NOPE + 16:]
                cos, sin = (trig[:, 0, k].unsqueeze(2).broadcast_to([P, T, NH, 16]) for k in range(2))
                r = [rope_t[:, k].rearrange("p (t h d) -> p t h d", t=T, h=NH) for k in range(4)]
                dve.wait_ge(s_trig, 1)
                for k, (x, f) in enumerate(((x1, cos), (x2, sin), (x1, sin), (x2, cos))):
                    own.mark(dve.tensor_tensor(r[k], x, f, ALU.mult))
                own.settle()
                own.mark(dve.tensor_tensor(x1, r[0], r[1], ALU.subtract))
                dve.tensor_tensor(x2, r[2], r[3], ALU.add).then_inc(s_rot, 1)
            own.settle()
            for k in range(TAPS):
                conv(1, k)
            for j in (10, 11):
                ps = u1.read(dve, ("ada", j))
                g = gate_f[:, (j % 2) * 512:(j % 2 + 1) * 512]
                u1.free(dve.tensor_tensor(g, ps[:], g, ALU.add), ("ada", j))
            modulation(1, g_ffn)
            for h in range(NH):
                ps = u1.read(dve, ("kT", h))
                u1.free(dve.tensor_copy(KT[0:QK, h], ps[0:QK, :]), ("kT", h))

            def weighted(eng, n):
                t, h = divmod(n, NH)
                if h == NH - 1:
                    u1.read(eng, ("o", t))
                else:
                    eng.wait_ge(s_pv, t * (NH - 1) + h + 1)

            def row_max(n):
                t, h = divmod(n, NH)
                ps = u1.read(dve, ("s", t, h))
                own.link(dve.tensor_reduce(mx[:, t, h:h + 1], ps[:, 0:(t + 1) * P], AX, ALU.max))
                dve.tensor_scalar(nmx[:, t, h:h + 1], mx[:, t, h:h + 1], -(QK ** -0.5), None, ALU.mult).then_inc(s_negmax, 1)

            def take_pt(n):
                t, h = divmod(n, NH)
                if n >= 3:
                    weighted(dve, n - 3)
                ps = u1.read(dve, ("pT", t, h))
                u1.free(dve.tensor_copy(PT[:, n % 3, 0:(t + 1) * P], ps[:, 0:(t + 1) * P]), ("pT", t, h))

            def take_o(t):
                u1.evacuated(dve, ("s", t, NH - 1))
                own.link(dve.reciprocal(rl[:, t], lsum[:, t]))
                ps = u1.read(dve, ("o", t))
                u1.free(dve.tensor_tensor(O[:, t].rearrange("p (h d) -> p h d", d=VD), ps[:].rearrange("p (h d) -> p h d", d=VD),
                                          rl[:, t].unsqueeze(2).broadcast_to([P, NH, VD]), ALU.mult), ("o", t))

            for n in range(T * NH + 3):
                if n < T * NH:
                    row_max(n)
                for k in (2 * n, 2 * n + 1):
                    if k < 2 * TAPS:
                        conv(2 + k // TAPS, k % TAPS)
                if 2 <= n < T * NH + 2:
                    take_pt(n - 2)
                if n >= 4 and (n - 3) % NH == 0:
                    take_o((n - 3) // NH - 1)
            take_o(T - 1)
            ps = u1.read(dve, ("mean",))
            for m in range(MC):
                dve.scalar_tensor_tensor(DW[:, m], ps[:], -1.0 / CONV, DW[:, m], ALU.mult, ALU.add).then_inc(s_cent, 1)
            dve.wait_ge(s_cent, MC)
            u1.free(dve.memset(mx[:, 0, 0:1], 0.0), ("mean",))
            u1.evacuated(dve, ("var",))
            own.link(dve.reciprocal(stat[:, 1], stat[:, 0]))
            for m in range(MC):
                dve.tensor_tensor(DW[:, m], DW[:, m], stat[:, 1], ALU.mult).then_inc(s_cnorm, 1)
            for t in range(T):
                if t:
                    dve.wait_ge(s_x1, t)
                for half in range(2):
                    cs = slice(512 * half, 512 * half + 512)
                    ps = u1.read(dve, ("mix", t, half))
                    u1.free(dve.tensor_tensor(xtmp[:, half], ps[:], gate_a[:, cs], ALU.mult), ("mix", t, half))
                for half in range(2):
                    cs = slice(512 * half, 512 * half + 512)
                    u1.evacuated(dve, ("mix", t, half))
                    ins = dve.tensor_tensor(X[:, t, cs], X[:, t, cs], xtmp[:, half], ALU.add)
                    if half:
                        ins.then_inc(s_x1, 1)
                    else:
                        own.mark(ins)
                own.settle()
            dve.wait_ge(s_rstd2, 1)
            for t in range(T):
                dve.tensor_scalar(H[:, t], X[:, t], rstd[:, t:t + 1], None, ALU.mult).then_inc(s_xhat2, 1)
            for c in range(1, C8, 2):
                ps = u1.read(dve, ("h2T", c))
                u1.free(dve.tensor_scalar(HT[:, c], ps[:], mod[:, 3, c:c + 1], mod[:, 2, c:c + 1],
                                          ALU.mult, ALU.add), ("h2T", c))
            for t in range(T):
                ps = u1.read(dve, ("logit", t))
                u1.free(dve.tensor_tensor(L[:, t], ps[:, 0:NG + NE], b_route, ALU.add), ("logit", t))
            for t in range(T):
                u1.evacuated(dve, ("logit", t))
            u1.evacuated(dve, ("mix", T - 1, 1))
            dve.wait_ge(s_fill, 16)

            def wide(x, n):
                return x.unsqueeze(2).broadcast_to([P, T, n])

            def first_max(vals, n, top, onehot):
                own.link(dve.tensor_reduce(top, vals, AX, ALU.max))
                own.link(dve.tensor_tensor(onehot, vals, wide(top, n), ALU.is_equal))
                own.link(dve.tensor_tensor(onehot, onehot, ramp[:, 0:n].unsqueeze(1).broadcast_to([P, T, n]), ALU.mult))
                own.link(dve.tensor_reduce(ered[:, :, 7], onehot, AX, ALU.max))
                own.link(dve.tensor_tensor(onehot, onehot, wide(ered[:, :, 7], n), ALU.is_equal))

            GL, EL = L[:, :, 0:NG], L[:, :, NG:]
            first_max(GL, NG, ered[:, :, 0], gsel)
            dve.tensor_tensor(gexp, GL, wide(ered[:, :, 0], NG), ALU.subtract).then_inc(s_gdiff, 1)
            sel = gsel.unsqueeze(3).broadcast_to([P, T, NG, EPG])
            m4, e4, t4 = (x.rearrange("p t (g e) -> p t g e", g=NG) for x in (ML, EL, tmp32))
            own.mark(dve.tensor_tensor(m4, e4, sel, ALU.mult))
            own.mark(dve.tensor_copy(t4, sel))
            own.settle()
            own.link(dve.tensor_scalar(tmp32, tmp32, -NEG, NEG, ALU.mult, ALU.add))
            own.link(dve.tensor_tensor(ML, ML, tmp32, ALU.add))
            first_max(ML, NE, ered[:, :, 1], OH[0])
            own.link(dve.scalar_tensor_tensor(ML, OH[0], 2 * NEG, ML, ALU.mult, ALU.add))
            first_max(ML, NE, ered[:, :, 2], OH[1])
            dve.tensor_tensor(ered[:, :, 4], ered[:, :, 2], ered[:, :, 1], ALU.subtract).then_inc(s_ediff, 1)
            dve.tensor_tensor(MM, OH[0], OH[1], ALU.add).then_inc(s_masks, 1)
            dve.wait_ge(s_gexp, 1)
            own.link(dve.tensor_reduce(ered[:, :, 3], gexp, AX, ALU.add))
            own.link(dve.reciprocal(ered[:, :, 3], ered[:, :, 3]))
            dve.wait_ge(s_eexp, 1)
            own.link(dve.tensor_scalar(ered[:, :, 5], ered[:, :, 4], 1.0, None, ALU.add))
            own.link(dve.reciprocal(ered[:, :, 5], ered[:, :, 5]))
            own.link(dve.tensor_tensor(wts[:, :, 0], ered[:, :, 5], ered[:, :, 3], ALU.mult))
            own.mark(dve.tensor_tensor(wts[:, :, 1], wts[:, :, 0], ered[:, :, 4], ALU.mult))
            ps = u1.read(dve, ("rank",))
            own.mark(dve.tensor_copy(rank, ps[:, 0:T * NE].rearrange("p (t e) -> p t e", t=T)))
            own.settle()
            u1.free(dve.tensor_copy(cnt, ps[:, T * NE:T * NE + NE]), ("rank",))
            u1.evacuated(dve, ("rank",))
            own.link(dve.tensor_copy(pre[0], cnt))
            k = 0
            for d in (1, 2, 4, 8, 16):
                own.mark(dve.tensor_copy(pre[1 - k][:, 0:d], pre[k][:, 0:d]))
                own.mark(dve.tensor_tensor(pre[1 - k][:, d:], pre[k][:, d:], pre[k][:, 0:NE - d], ALU.add))
                own.settle()
                k = 1 - k
            own.link(dve.tensor_tensor(off_e, pre[k], cnt, ALU.subtract))
            for w, start in enumerate((off_e, slot0)):
                own.link(dve.tensor_tensor(tmp32, rank, start.unsqueeze(1).broadcast_to([P, T, NE]), ALU.add))
                for k in range(2):
                    own.link(dve.tensor_tensor(ML, tmp32, OH[k], ALU.mult))
                    own.link(dve.tensor_reduce(dest_f[:, w, :, k], ML, AX, ALU.add))
            dve.tensor_copy(dest, dest_f).then_inc(s_dest, 1)
            for r in range(ROUNDS):
                own.mark(dve.tensor_scalar(win_f[:, r], off_e, float(r * P), float(2 * S), ALU.add, ALU.min))
                own.mark(dve.tensor_scalar(tmp32[:, r], cnt, float(r * P), None, ALU.is_gt))
            own.settle()
            own.mark(dve.tensor_copy(win[:, 0:T * NE], win_f.rearrange("p t e -> p (t e)")))
            own.mark(dve.memset(win[:, T * NE:], 0))
            own.link(dve.tensor_reduce(rounds_f, tmp32, AX, ALU.max))
            own.link(dve.tensor_reduce(ered[:, 0, 6:7], rounds_f, AX, ALU.add))
            dve.tensor_copy(rounds[:, 0:1], ered[:, 0, 6:7]).then_inc(s_rounds, 1)
            ps = u1.read(dve, ("slots",))
            u1.free(dve.tensor_copy(slots_i, ps[:, 0:P]), ("slots",))
            for g in range(2):
                for c in range(1, C8, 2):
                    ps = u1.read(dve, ("xsT", g, c))
                    u1.free(dve.tensor_scalar(XsT[:, c, g * S:(g + 1) * S], ps[:], mod[:, 3, c:c + 1], mod[:, 2, c:c + 1],
                                              ALU.mult, ALU.add), ("xsT", g, c))
            dve.sem_inc(m_a, CREDIT)
            dve.sem_inc(m_ya, CREDIT)
            dve.sem_inc(m_xw, CREDIT)
            u1.all_evacuated(dve, [("xsT", g, c) for g in range(2) for c in range(C8)])
            dve.wait_ge(s_pad, 1)

            def window(e, s):
                w0 = dve.value_load(win[0:1, bass.ds(e, 1)], min_val=0, max_val=2 * S)
                dve.tensor_copy(XW[s % 2], XsT[:, :, bass.ds(w0, P)]).then_inc(m_xw, 1)

            def product(n, s):
                dve.wait_ge(m_silu, n + 1 + CREDIT)
                dve.wait_ge(m_at, n - 2 + 1 + CREDIT)
                dve.tensor_tensor(A[:, s % 2], SG[:, s % 2], bank[s % 2][:, FE:], ALU.mult).then_inc(m_a, 1)
                window(n + 2, s)

            def copy_ya(n, it, s):
                dve.wait_ge(m_y, n + 1 + CREDIT)
                dve.wait_ge(m_st[s], SCATTERED + 16 * it)
                dve.tensor_copy(Y[:, s, 0:512], bank[4 + 2 * (s % 2)][:]).then_inc(m_ya, 1)

            n_rounds = dve.value_load(rounds[0:1, 0:1], min_val=1, max_val=ROUNDS)
            window(0, 0)
            window(1, 1)
            with dve.Fori(0, n_rounds) as r:
                with dve.Fori(0, NE // 4) as it:
                    n = r * NE + it * 4
                    for s in range(4):
                        product(n + s, s)
                        if s:
                            copy_ya(n + s - 1, r * (NE // 4) + it, s - 1)
                    copy_ya(n + 3, r * (NE // 4) + it, 3)
            own.settle()
            for t in range(T):
                dve.wait_ge(s_yin[t], 16)
                for k in range(2):
                    if k == 0:
                        ins = dve.tensor_scalar(Yin[:, t, 0], Yin[:, t, 0], wts[:, t, 0:1], None, ALU.mult)
                    else:
                        ins = dve.scalar_tensor_tensor(Yin[:, t, 0], Yin[:, t, 1], wts[:, t, 1:2], Yin[:, t, 0], ALU.mult, ALU.add)
                    own.link(ins)
                own.link(dve.tensor_tensor(Yin[:, t, 0], Yin[:, t, 0], gate_f, ALU.mult))
                ins = dve.tensor_tensor(X[:, t], X[:, t], Yin[:, t, 0], ALU.add)
                if t < T - 1:
                    ins.then_inc(s_x2, 1)
                else:
                    ins.then_inc(a_free, 1)
            dve.wait_ge(a_free, 1)
            dve.wait_ge(s_x2, T - 1)
            own.restart()

            def stats(t):
                for half in range(2):
                    own.mark(dve.bn_stats(bst[:, t, half], X[:, t, 512 * half:512 * half + 512]))
                own.settle()
                return dve.bn_aggr(bag[:, t], bst[:, t])

            def centre_scale(t, gain):
                own.link(dve.tensor_scalar(X[:, t], X[:, t], bag[:, t, 0:1], lrs[:, t:t + 1], ALU.subtract, ALU.mult))
                return dve.tensor_tensor(X[:, t], X[:, t], gain, ALU.mult)

            for t in range(T):
                stats(t).then_inc(s_mean, 1)
            dve.wait_ge(s_lnr, 1)
            dve.wait_ge(s_lnin, 32)
            for t in range(T):
                own.link(centre_scale(t, lnin_g))
                dve.tensor_tensor(X[:, t], X[:, t], lnin_b, ALU.add).then_inc(layer_in, 1)
            dve.sem_inc(f_a, CREDIT)

            with dve.Fori(0, LAYERS) as l:
                own.settle()
                own.restart()
                for c in range(1, C8, 2):
                    ps = u2.read(dve, ("xT", c), l)
                    u2.free(dve.tensor_copy(HT[:, c], ps[:]), ("xT", c))
                dve.wait_ge(d_sm, 48 * (l + 1))
                own.mark(dve.tensor_scalar(nsinks, sinks, -1.0, None, ALU.mult))
                own.settle()

                def rotate(src, dst, cos, sin, heads, half, copies=1):
                    r = [rt[:, k, 0:T * heads * half].rearrange("p (t h d) -> p t h d", t=T, h=heads) for k in range(4)]
                    c, s_ = (x.unsqueeze(2).broadcast_to([P, T, heads, half]) for x in (cos, sin))
                    x1, x2 = src[:, :, :, 0:half], src[:, :, :, half:2 * half]
                    for k, (x, f) in enumerate(((x1, c), (x2, s_), (x2, c), (x1, s_))):
                        own.mark(dve.tensor_tensor(r[k], x, f, ALU.mult))
                    own.settle()
                    for n in range(copies):
                        for k, op, lo in ((0, ALU.subtract, 0), (2, ALU.add, half)):
                            ins = dve.tensor_tensor(dst[n][:, :, :, lo:lo + half], r[k], r[k + 1], op)
                            if n < copies - 1 or lo == 0:
                                own.mark(ins)
                    y_rot.inc(ins)
                    own.settle()

                def heads_of(a, n, d):
                    return PJ[:, :, a:a + n * d].rearrange("p t (h d) -> p t h d", d=d)

                c16, s16, c32, s32 = trig[:, 1, 0], trig[:, 1, 1], trig64[:, 0], trig64[:, 1]
                for t in range(T):
                    u2.evacuated(dve, ("in", t, 0), l)
                for t in range(T):
                    own.mark(dve.bn_stats(bst[:, t, 0], PJ[:, t, KI:KI + IXD]))
                own.settle()
                for t in range(T):
                    ins = dve.bn_aggr(bag[:, t], bst[:, t, 0:1])
                    if t < T - 1:
                        own.mark(ins)
                y_kst.inc(ins)
                own.settle()
                y_kst.wait(dve, l, 1)
                own.mark(dve.tensor_scalar(wi, PJ[:, :, WI:WI + IXH], float(IXH ** -0.5 * IXD ** -0.5), None, ALU.mult))
                qi = heads_of(QI, IXH, IXD)
                rotate(qi, [qi], c16, s16, IXH, 16)
                y_rot.wait(dve, l, 1)
                y_krs.wait(dve, l, 1)
                for t in range(T):
                    own.mark(dve.tensor_scalar(PJ[:, t, KI:KI + IXD], PJ[:, t, KI:KI + IXD], bag[:, t, 0:1], lrs[:, t:t + 1], ALU.subtract, ALU.mult))
                own.settle()
                for p, op in ((ix_g, ALU.mult), (ix_b, ALU.add)):
                    own.link(dve.tensor_tensor(PJ[:, :, KI:KI + IXD], PJ[:, :, KI:KI + IXD], p.unsqueeze(1).broadcast_to([P, T, IXD]), op))
                rotate(heads_of(KI, 1, IXD), [KID[:, :, n:n + 1] for n in range(4)], c16, s16, 1, 16, copies=4)
                for t in range(T):
                    u2.evacuated(dve, ("in", t, 2), l)
                y_rot.wait(dve, l, 2)
                rotate(heads_of(KA, 2, HD), [KD[:, :, :, n] for n in range(2)], c32, s32, 2, 32, copies=2)
                for t in range(T):
                    u2.evacuated(dve, ("in", t, 1), l)
                y_rot.wait(dve, l, 3)
                qa = heads_of(QA, 8, HD)
                rotate(qa, [qa], c32, s32, 8, 32)
                for t in range(T):
                    u2.evacuated(dve, ("in", t, 4), l)
                y_rot.wait(dve, l, 4)
                rotate(heads_of(KB, 1, HD), [KBD[:, :, n:n + 1] for n in range(2)], c32, s32, 1, 32, copies=2)
                for t in range(T):
                    u2.evacuated(dve, ("in", t, 3), l)
                y_rot.wait(dve, l, 5)
                qb = heads_of(QB, 8, HD)
                rotate(qb, [qb], c32, s32, 8, 32)
                for n, key in enumerate(TURNED):
                    if n % 2:
                        ps = u2.read(dve, key, l)
                        u2.free(dve.tensor_copy(turned[key], ps[:]), key)
                n = 0
                for t in range(1, T):
                    w = (t + 1) * P
                    for h in range(IXH):
                        u2.evacuated(dve, ("ix", t, h), l)
                        acc = IX[:, t - 1, 0:w]
                        if h == 0:
                            ins = dve.tensor_scalar(acc, R[:, n % 2, 0:w], wi[:, t, h:h + 1], None, ALU.mult)
                        else:
                            y_ix.wait(dve, l, n)
                            ins = dve.scalar_tensor_tensor(acc, R[:, n % 2, 0:w], wi[:, t, h:h + 1], acc, ALU.mult, ALU.add)
                        y_ix.inc(ins)
                        n += 1
                    y_ix.wait(dve, l, n)
                    own.mark(dve.tensor_tensor(IX[:, t - 1, t * P:w], IX[:, t - 1, t * P:w], own_mask, ALU.add))
                own.settle()

                def pick(n):
                    t, k = divmod(n, PICKS)
                    sc = IX[:, t, 0:(t + 2) * P]
                    own.link(dve.max(top8, sc))
                    own.link(dve.match_replace(sc, top8, sc, TAKEN))
                    if k == PICKS - 1:
                        own.link(dve.tensor_scalar(sc, sc, TAKEN, -NEG, ALU.is_equal, ALU.mult))
                        y_sel.inc(dve.tensor_scalar(SELM[:, t, 0:(t + 2) * P], sc, NEG, None, ALU.add))

                def row_max(n):
                    kind, t, h = UNITS[n]
                    kk = 0 if kind == "a" else 1
                    ps = u2.read(dve, ("s", kind, t, h), l)
                    own.link(dve.tensor_reduce(mx2[:, kk, t, h:h + 1], ps[:, 0:width(n)], AX, ALU.max))
                    if kind == "a":
                        ins = dve.tensor_scalar(nmx2[:, kk, t, h:h + 1], mx2[:, kk, t, h:h + 1], -(HD ** -0.5), nsinks[:, h:h + 1],
                                                ALU.mult, ALU.min)
                    else:
                        ins = dve.tensor_scalar(nmx2[:, kk, t, h:h + 1], mx2[:, kk, t, h:h + 1], -(HD ** -0.5), None, ALU.mult)
                    y_neg.inc(ins)
                    if kind == "a" and h == 7:
                        y_neg.wait(dve, l, n + 1)
                        y_sinkd.inc(dve.tensor_tensor(es2[:, t], nmx2[:, 0, t], sinks, ALU.add))

                def take_pt(n):
                    kind, t, h = UNITS[n]
                    w = width(n)
                    weighted2(dve, n - 3, l)
                    ps = u2.read(dve, ("pT", kind, t, h), l)
                    u2.free(dve.tensor_copy(PT2[:, n % 3, 0:w], ps[:, 0:w]), ("pT", kind, t, h))

                def take_o(kind, t):
                    kk = 0 if kind == "a" else 1
                    u2.evacuated(dve, ("s", kind, t, 7), l)
                    if kind == "a":
                        y_sinke.wait(dve, l, t + 1)
                        own.link(dve.tensor_tensor(ls2[:, 0, t], ls2[:, 0, t], es2[:, t], ALU.add))
                    own.link(dve.reciprocal(rl2[:, kk, t], ls2[:, kk, t]))
                    ps = u2.read(dve, ("o", kind, t), l)
                    u2.free(dve.tensor_tensor(O2[:, kk, t].rearrange("p (h d) -> p h d", d=HD), ps[:].rearrange("p (h d) -> p h d", d=HD),
                                              rl2[:, kk, t].unsqueeze(2).broadcast_to([P, 8, HD]), ALU.mult), ("o", kind, t))

                for n in range(len(UNITS) + 3):
                    if n < len(UNITS):
                        row_max(n)
                    if n < 3 * PICKS // 2:
                        pick(2 * n)
                        pick(2 * n + 1)
                    if 34 <= n < len(UNITS) + 2:
                        take_pt(n - 2)
                    if n >= 4 and (n - 3) % 8 == 0:
                        take_o(*UNITS[n - 4][:2])
                take_o("b", T - 1)
                for j in range(1, C8, 2):
                    ps = u2.read(dve, ("oT", j), l)
                    u2.free(dve.tensor_copy(HT[:, j], ps[:]), ("oT", j))

                def residual(key, t):
                    for half in range(2):
                        cs = slice(512 * half, 512 * half + 512)
                        ps = u2.read(dve, (key, t, half), l)
                        u2.free(dve.scalar_tensor_tensor(X[:, t, cs], X[:, t, cs], ALPHA, ps[:], ALU.mult, ALU.add), (key, t, half))
                    for half in range(2):
                        u2.evacuated(dve, (key, t, half), l)

                for t in range(T):
                    residual("mix", t)
                    ins = stats(t)
                    if t < T - 1:
                        own.mark(ins)
                y_mst.inc(ins)
                y_mrs.wait(dve, l, 1)
                own.settle()
                dve.wait_ge(d_ln1, 32 * (l + 1))
                for t in range(T):
                    y_mx.inc(centre_scale(t, lnG))
                for c in range(1, C8, 2):
                    ps = u2.read(dve, ("x1T", c), l)
                    u2.free(dve.tensor_copy(HT[:, c], ps[:]), ("x1T", c))
                ps = u2.read(dve, ("plT", 1), l)
                u2.free(dve.tensor_copy(pT[:, 1], ps[:]), ("plT", 1))
                n = 0
                for t in range(T):
                    for half in range(2):
                        u2.evacuated(dve, ("pg", t, half), l)
                        ps = u2.read(dve, ("pp", t, half), l)
                        cs = slice(512 * half, 512 * half + 512)
                        ins = dve.tensor_tensor(PLB[:, t, cs], ps[:], SF[:, n % 2], ALU.mult)
                        u2.free(ins, ("pp", t, half))
                        n += 1
                with dve.Fori(0, FC // 2) as it:
                    for s in range(2):
                        n = l * FC + it * 2 + s
                        dve.wait_ge(f_s, n + 1 + CREDIT)
                        dve.tensor_tensor(aT[:, bass.ds(it * 2 + s, 1)].rearrange("p a n -> p (a n)"), SF[:, s], bank[2 * s + 1][:],
                                          ALU.mult).then_inc(f_a, 1)
                u2.read(dve, ("dn", T - 1, 1), l)
                dve.sem_inc(a_free, 1)
                for t in range(T):
                    residual("dn", t)
                    own.link(dve.tensor_tensor(X[:, t], X[:, t], PLB[:, t], ALU.add))
                    ins = stats(t)
                    if t < T - 1:
                        own.mark(ins)
                y_est.inc(ins)
                y_ers.wait(dve, l, 1)
                own.settle()
                dve.wait_ge(d_ln2, 32 * (l + 1))
                for t in range(T):
                    y_ex.inc(centre_scale(t, lnG))

        @block.tensor
        def _(pe):
            def ada(j):
                ps = u1.begin(pe, ("ada", j))
                pe.wait_ge(s_ada[j % 2], 16 * (j // 2 + 1))
                for c in range(C8):
                    ins = pe.matmul(ps[:], c_wide[:, c], ada_w[j % 2][:, c], start=c == 0, stop=c == C8 - 1)
                u1.full(ins, ("ada", j))

            def mod_cols(n, row):
                for j in range(4):
                    u1.evacuated(pe, ("ada", 6 * n + j))
                ps = u1.begin(pe, ("modT", n))
                for v in range(2):
                    for c in range(C8):
                        ins = pe.matmul(ps[:, v * C8 + c:v * C8 + c + 1], row[0:1, v * D + c:v * D + D:C8],
                                        ones[0:1, 0:1], start=True, stop=True)
                u1.full(ins, ("modT", n))

            def turn(key, pieces):
                ps = u1.begin(pe, key)
                for n, x in enumerate(pieces):
                    ins = pe.transpose(ps[0:x.shape[-1], n * P:(n + 1) * P], x, ident)
                u1.full(ins, key)

            pe.wait_ge(s_const, 1)
            pe.wait_ge(s_cw, 1)
            for j in range(4):
                ada(j)
            pe.wait_ge(s_small, SMALL)
            ps = u1.begin(pe, ("taps",))
            for m in range(MC):
                ins = pe.transpose(ps[:, m * 32:m * 32 + TAPS], tap_rows[0:TAPS, m * P:(m + 1) * P], ident[0:TAPS, 0:TAPS])
            u1.full(ins, ("taps",))
            mod_cols(0, mod_row0)
            pe.wait_ge(s_xhat, T)
            for c in range(C8):
                turn(("hT", c), [H[:, t, c::C8] for t in range(T)])
            for c in range(C8):
                u1.evacuated(pe, ("hT", c))
            pe.wait_ge(s_win, 16)
            for m in range(MC):
                for kind, c0 in (("val", 0), ("gate", CONV)):
                    ps = u1.begin(pe, (kind, m))
                    for c in range(C8):
                        ins = pe.matmul(ps[:], w_in[:, c, c0 + m * P:c0 + (m + 1) * P], HT[:, c], start=c == 0, stop=c == C8 - 1)
                    u1.full(ins, (kind, m))
            for t in range(T):
                ps = u1.begin(pe, ("lat", t))
                for c in range(C8):
                    ins = pe.matmul(ps[:, 0:LAT], HT[:, c, t * P:(t + 1) * P], w_in[:, c, 2 * CONV:], start=c == 0, stop=c == C8 - 1)
                u1.full(ins, ("lat", t))
            pe.wait_ge(s_latn, 2 * T)
            for n in range(3):
                turn(("latT", n), [LATB[:, t, n * P:(n + 1) * P] for t in range(T)])
            for n in range(3):
                u1.evacuated(pe, ("latT", n))
            pe.wait_ge(s_wq, 32)
            for t in range(T):
                ts = slice(t * P, (t + 1) * P)
                for half in range(2):
                    ps = u1.begin(pe, ("q", t, half))
                    for c in range(2):
                        ins = pe.matmul(ps[:, 0:384], latT[:, c, ts], w_q[:, c, 384 * half:384 * half + 384], start=c == 0, stop=c == 1)
                    u1.full(ins, ("q", t, half))
                    ps = u1.begin(pe, ("kv", t, half))
                    u1.full(pe.matmul(ps[:], latT[:, 2, ts], w_kv[:, 512 * half:512 * half + 512], start=True, stop=True), ("kv", t, half))
            for j in range(4, 12):
                ada(j)
            mod_cols(1, mod_row1)
            for h in range(NH):
                pe.wait_ge(s_rot, 2)
                turn(("qT", h), [Q[:, t, h] for t in range(T)])
                turn(("kT", h), [K[:, t, h] for t in range(T)])

            def scores(n):
                t, h = divmod(n, NH)
                u1.evacuated(pe, ("qT", h))
                u1.evacuated(pe, ("kT", h))
                w = (t + 1) * P
                ps = u1.begin(pe, ("s", t, h))
                pe.matmul(ps[:, 0:w], QT[0:QK, h, t * P:w], KT[0:QK, h, 0:w], start=True, stop=False)
                u1.full(pe.matmul(ps[:, t * P:w], ident_b, chunk_mask, start=False, stop=True), ("s", t, h))

            def turn_p(n):
                t, h = divmod(n, NH)
                u1.evacuated(pe, ("s", t, h))
                turn(("pT", t, h), [Pr[:, n % 3, k * P:(k + 1) * P] for k in range(t + 1)])

            def values(n):
                t, h = divmod(n, NH)
                u1.evacuated(pe, ("pT", t, h))
                ps = u1.begin(pe, ("o", t)) if h == 0 else bank[u1.b.where[("o", t)][0]]
                for k in range(t + 1):
                    ins = pe.matmul(ps[:, h * VD:(h + 1) * VD], PT[:, n % 3, k * P:(k + 1) * P], V[:, k, h * VD:(h + 1) * VD],
                                    start=k == 0, stop=k == t)
                if h == NH - 1:
                    u1.full(ins, ("o", t))
                else:
                    ins.then_inc(s_pv, 1)

            for n in range(T * NH + 3):
                if n < T * NH:
                    scores(n)
                if 2 <= n < T * NH + 2:
                    turn_p(n - 2)
                if n >= 3:
                    values(n - 3)
            for j in range(4):
                for t in range(T):
                    u1.evacuated(pe, ("o", t))
                turn(("oT", j), [O[:, t, j * P:(j + 1) * P] for t in range(T)])
            ps = u1.begin(pe, ("mean",))
            pe.wait_ge(s_conv, MC)
            for m in range(MC):
                ins = pe.matmul(ps[:], ones, DW[:, m], start=m == 0, stop=m == MC - 1)
            u1.full(ins, ("mean",))
            ps = u1.begin(pe, ("var",))
            for m in range(MC):
                pe.wait_ge(s_csq, m + 1)
                ins = pe.matmul(ps[:], ones, stat[:, m % 2], start=m == 0, stop=m == MC - 1)
                if m < MC - 1:
                    ins.then_inc(s_csum, 1)
            u1.full(ins, ("var",))
            pe.wait_ge(s_wout, 64)
            pe.wait_ge(s_yconv, MC)
            for j in range(4):
                u1.evacuated(pe, ("oT", j))
            for t in range(T):
                for half in range(2):
                    ps = u1.begin(pe, ("mix", t, half))
                    for m in range(C8):
                        ins = pe.matmul(ps[:], mixT[:, m, t * P:(t + 1) * P], w_out[:, m, 512 * half:512 * half + 512],
                                        start=m == 0, stop=m == C8 - 1)
                    u1.full(ins, ("mix", t, half))

            pe.wait_ge(s_xhat2, T)
            for c in range(C8):
                turn(("h2T", c), [H[:, t, c::C8] for t in range(T)])
            for c in range(C8):
                u1.evacuated(pe, ("h2T", c))
            for t in range(T):
                ps = u1.begin(pe, ("logit", t))
                for c in range(C8):
                    ins = pe.matmul(ps[:, 0:NG + NE], HT[:, c, t * P:(t + 1) * P], w_route[:, c], start=c == 0, stop=c == C8 - 1)
                u1.full(ins, ("logit", t))
            pe.wait_ge(s_masks, 1)
            ps = u1.begin(pe, ("rank",))
            for t in range(T):
                for k in range(t):
                    pe.matmul(ps[:, t * NE:(t + 1) * NE], ones, MM[:, k], start=k == 0, stop=False)
                pe.matmul(ps[:, t * NE:(t + 1) * NE], before_me, MM[:, t], start=t == 0, stop=True)
            for t in range(T):
                ins = pe.matmul(ps[:, T * NE:T * NE + NE], ones, MM[:, t], start=t == 0, stop=t == T - 1)
            u1.full(ins, ("rank",))
            pe.wait_ge(s_slotin, 16)
            turn(("slots",), [slots_f])
            for g in range(2):
                pe.wait_ge(s_stage[g], 16 * T)
                for c in range(C8):
                    turn(("xsT", g, c), [stage[g][:, q, c::C8] for q in range(T)])
            for x in (m_gu, m_at, m_y):
                pe.sem_inc(x, CREDIT)
            for g in range(2):
                for c in range(C8):
                    u1.evacuated(pe, ("xsT", g, c))

            def gate_up(n, it, s):
                pe.wait_ge(m_xw, n + 1 + CREDIT)
                pe.wait_ge(s_w[s], 48 * (it + 1))
                pe.wait_ge(m_a, n - 2 + 1 + CREDIT)
                for c in range(C8):
                    ins = pe.matmul(bank[s % 2][:], XW[s % 2][:, c], ring[s][:, c], start=c == 0, stop=c == C8 - 1)
                ins.then_inc(m_gu, 1)

            def turn_a(n, s):
                pe.wait_ge(m_a, n + 1 + CREDIT)
                pe.wait_ge(m_atc, n - 2 + 1 + CREDIT)
                for c in range(2):
                    ins = pe.transpose(bank[2 + s % 2][:, c * P:(c + 1) * P], A[:, s % 2, c::2], ident)
                ins.then_inc(m_at, 1)

            def down(n, s):
                pe.wait_ge(m_atc, n + 1 + CREDIT)
                pe.wait_ge(m_ya, n - 2 + 1 + CREDIT)
                pe.wait_ge(m_yb, n - 2 + 1 + CREDIT)
                for half in range(2):
                    for c in range(2):
                        ins = pe.matmul(bank[4 + 2 * (s % 2) + half][:], AT[:, s % 2, c], ring_d[s][:, c, 512 * half:512 * half + 512],
                                        start=c == 0, stop=c == 1)
                ins.then_inc(m_y, 1)

            pe.wait_ge(s_rounds, 1)
            n_rounds = pe.value_load(rounds[0:1, 0:1], min_val=1, max_val=ROUNDS)
            with pe.Fori(0, n_rounds) as r:
                with pe.Fori(0, NE // 4) as it:
                    n = r * NE + it * 4
                    for s in range(4):
                        gate_up(n + s, r * (NE // 4) + it, s)
                        if s:
                            down(n + s - 1, s - 1)
                        turn_a(n + s, s)
                    down(n + 3, 3)
            pe.wait_ge(m_y, n_rounds * NE + CREDIT)
            pe.sem_inc(b_free, 1)
            pe.sem_inc(f_g, CREDIT)

            with pe.Fori(0, LAYERS) as l:
                def turn2(key, pieces):
                    ps = u2.begin(pe, key, l)
                    for n, x in enumerate(pieces):
                        ins = pe.transpose(ps[0:x.shape[-1], n * P:(n + 1) * P], x, ident)
                    u2.full(ins, key)

                pe.wait_ge(layer_in, l * T + T)
                for c in range(C8):
                    turn2(("xT", c), [X[:, t, c::C8] for t in range(T)])
                for c in range(C8):
                    u2.evacuated(pe, ("xT", c), l)
                pe.wait_ge(d_in2, 32 * (l + 1))
                for j, (a, b) in enumerate(IN_CUTS):
                    for t in range(T):
                        ps = u2.begin(pe, ("in", t, j), l)
                        for c in range(C8):
                            ins = pe.matmul(ps[:, 0:b - a], HT[:, c, t * P:(t + 1) * P], w_in2[:, c, a:b], start=c == 0, stop=c == C8 - 1)
                        u2.full(ins, ("in", t, j))
                source = {"qi": (1, lambda t, j: PJ[:, t, QI + j * P:QI + (j + 1) * P]),
                          "ki": (2, lambda t, j: KID[:, t].rearrange("p a b -> p (a b)")),
                          "ka": (3, lambda t, j: KD[:, t, j].rearrange("p a b -> p (a b)")),
                          "qa": (4, lambda t, j: PJ[:, t, QA + j * P:QA + (j + 1) * P]),
                          "kb": (5, lambda t, j: KBD[:, t].rearrange("p a b -> p (a b)")),
                          "qb": (6, lambda t, j: PJ[:, t, QB + j * P:QB + (j + 1) * P])}
                for kind, j in TURNED:
                    order, piece = source[kind]
                    y_rot.wait(pe, l, order)
                    turn2((kind, j), [piece(t, j) for t in range(T)])
                for key in TURNED[:3]:
                    u2.evacuated(pe, key, l)
                for t in range(1, T):
                    for h in range(IXH):
                        w = (t + 1) * P
                        p0 = IXD * (h % 4)
                        ps = u2.begin(pe, ("ix", t, h), l)
                        u2.full(pe.matmul(ps[:, 0:w], turned["qi", h // 4][p0:p0 + IXD, t * P:w], turned["ki", 0][p0:p0 + IXD, 0:w],
                                          start=True, stop=True), ("ix", t, h))
                u2.all_evacuated(pe, TURNED[3:], l)

                def scores(n):
                    kind, t, h = UNITS[n]
                    w = width(n)
                    k0 = (t + 1) * P - w
                    p0 = HD * (h % 2)
                    keys = turned["ka", h // 4] if kind == "a" else turned["kb", 0]
                    if kind == "b" and t and h == 0:
                        y_sel.wait(pe, l, t)
                    ps = u2.begin(pe, ("s", kind, t, h), l)
                    pe.matmul(ps[:, 0:w], turned["q" + kind, h // 2][p0:p0 + HD, t * P:(t + 1) * P], keys[p0:p0 + HD, k0:k0 + w],
                              start=True, stop=False)
                    if kind == "b" and t:
                        ins = pe.matmul(ps[:, 0:w], ident_b, SELM[:, t - 1, 0:w], start=False, stop=True)
                    else:
                        if t:
                            pe.matmul(ps[:, 0:P], ident_b, prev_mask, start=False, stop=False)
                        ins = pe.matmul(ps[:, w - P:w], ident_b, own_mask, start=False, stop=True)
                    u2.full(ins, ("s", kind, t, h))

                def turn_p(n):
                    key = UNITS[n]
                    u2.evacuated(pe, ("s",) + key, l)
                    turn2(("pT",) + key, [Pr2[:, n % 3, k * P:(k + 1) * P] for k in range(width(n) // P)])

                def values(n):
                    kind, t, h = UNITS[n]
                    nk = width(n) // P
                    u2.evacuated(pe, ("pT", kind, t, h), l)
                    ps = u2.begin(pe, ("o", kind, t), l) if h == 0 else bank[b2.where[("o", kind, t)][0]]
                    for k in range(nk):
                        kt = t + 1 - nk + k
                        v = PJ[:, kt, VA + HD * (h // 4):VA + HD * (h // 4) + HD] if kind == "a" else PJ[:, kt, VB:VB + HD]
                        ins = pe.matmul(ps[:, h * HD:(h + 1) * HD], PT2[:, n % 3, k * P:(k + 1) * P], v, start=k == 0, stop=k == nk - 1)
                    if h == 7:
                        u2.full(ins, ("o", kind, t))
                    else:
                        y_pv.inc(ins)

                for n in range(len(UNITS) + 3):
                    if n < len(UNITS):
                        scores(n)
                    if 2 <= n < len(UNITS) + 2:
                        turn_p(n - 2)
                    if n >= 3:
                        values(n - 3)
                for j in range(C8):
                    if j % 4 == 0:
                        u2.all_evacuated(pe, [("o", "ab"[j // 4], t) for t in range(T)], l)
                    turn2(("oT", j), [O2[:, j // 4, t, (j % 4) * P:(j % 4 + 1) * P] for t in range(T)])
                for j in range(C8):
                    u2.evacuated(pe, ("oT", j), l)
                pe.wait_ge(d_o2, 16 * (l + 1))
                for t in range(T):
                    for half in range(2):
                        ps = u2.begin(pe, ("mix", t, half), l)
                        for m in range(C8):
                            ins = pe.matmul(ps[:], HT[:, m, t * P:(t + 1) * P], w_o2[:, m, 512 * half:512 * half + 512], start=m == 0, stop=m == C8 - 1)
                        u2.full(ins, ("mix", t, half))
                y_x1.wait(pe, l, T)
                for c in range(C8):
                    turn2(("x1T", c), [X[:, t, c::C8] for t in range(T)])
                pe.wait_ge(d_pp, 32 * (l + 1))
                for c in range(2):
                    turn2(("plT", c), [p_in[:, t, c * P:(c + 1) * P] for t in range(T)])
                u2.all_evacuated(pe, [("x1T", c) for c in range(C8)] + [("plT", c) for c in range(2)], l)
                pe.wait_ge(d_pg, 16 * (l + 1))
                for t in range(T):
                    ts = slice(t * P, (t + 1) * P)
                    for half in range(2):
                        cs = slice(512 * half, 512 * half + 512)
                        ps = u2.begin(pe, ("pg", t, half), l)
                        for c in range(C8):
                            ins = pe.matmul(ps[:], HT[:, c, ts], w_pg[:, c, cs], start=c == 0, stop=c == C8 - 1)
                        u2.full(ins, ("pg", t, half))
                        ps = u2.begin(pe, ("pp", t, half), l)
                        for c in range(2):
                            ins = pe.matmul(ps[:], pT[:, c, ts], w_pp[:, c, cs], start=c == 0, stop=c == 1)
                        u2.full(ins, ("pp", t, half))
                u2.all_evacuated(pe, [(kind, t, half) for kind in ("pg", "pp") for t in range(T) for half in range(2)], l)
                apart(pe)
                with pe.Fori(0, FC // 2) as it:
                    for s in range(2):
                        n = l * FC + it * 2 + s
                        pe.wait_ge(d_gu[s], 32 * (l * (FC // 2) + it + 1))
                        pe.wait_ge(f_a, n - 2 + 1 + CREDIT)
                        for k in range(2):
                            for c in range(C8):
                                ins = pe.matmul(bank[2 * s + k][:], gu[s][:, k, c], HT[:, c], start=c == 0, stop=c == C8 - 1)
                        ins.then_inc(f_g, 1)
                pe.wait_ge(f_a, l * FC + FC + CREDIT)
                pe.sem_inc(b_free, 1)
                for f in range(FC):
                    pe.wait_ge(d_dn[f % 8], 16 * ((FC - 1 - f % 8) // 8 + 1) * l + 16 * (f // 8 + 1))
                    for t in range(T):
                        for half in range(2):
                            key = ("dn", t, half)
                            ps = u2.begin(pe, key, l) if f == 0 else bank[b2.where[key][0]]
                            ins = pe.matmul(ps[:], aT[:, f, t * P:(t + 1) * P], w_dn[:, f % 8, 512 * half:512 * half + 512],
                                            start=f == 0, stop=f == FC - 1)
                            if f == FC - 1:
                                u2.full(ins, key)
                    if f < FC - 1:
                        y_dn.inc(ins)


_OUTS = [((1, 512, 1024), "float32")]


def kernel(**inputs):
    from concourse import bacc
    from concourse.bass_utils import run_bass_kernel_spmd

    nc = bacc.Bacc("TRN2", target_bir_lowering=False, num_devices=1)
    arrays = {k: np.ascontiguousarray(v) for k, v in inputs.items()}
    arrays["freqs"] = np.concatenate([THETA ** (-np.arange(n) / n) for n in (16, 32)]).astype(np.float32)
    ins = {k: nc.dram_tensor(k, a.shape, mybir.dt.from_np(a.dtype), kind="ExternalInput").ap() for k, a in arrays.items()}
    out = nc.dram_tensor("y", (1, S, D), F32, kind="ExternalOutput").ap()
    build(nc, ins, out)
    return run_bass_kernel_spmd(nc, [arrays], core_ids=[0]).results[0]["y"]
```

```python
from contextlib import ExitStack

import numpy as np
import concourse.bass as bass
from concourse import mybir

P = 128
F32, F32R, BF16, I32 = mybir.dt.float32, mybir.dt.float32r, mybir.dt.bfloat16, mybir.dt.int32
ALU = mybir.AluOpType
ACT = mybir.ActivationFunctionType
AX = mybir.AxisListType.X

S, D = 512, 1024
T, C8 = S // P, D // P
CONV, TAPS = 512, 31
MC = CONV // P
PAD = TAPS - 1
NH, NOPE, ROPE, VD = 8, 64, 32, 64
QK = NOPE + ROPE
QR, KR = D // 4, D // 8
LAT = QR + KR + ROPE
IN1 = 2 * CONV + LAT
CHUNK = 64
NG, EPG = 4, 8
NE = NG * EPG
FE = D // 4
EPS, LN_EPS = 1e-6, 1e-5
NEG = -1e30

HD = 64
FF = 2816
FC = FF // P
PLE = 256
KTOP = 128
LAYERS = 2
ALPHA = (2 * LAYERS) ** 0.25
IXH, IXD = 8, 32
IN2 = 1704

SLOT = C8 * 2 * FE + 2 * D
XCOLS = 2 * S + P
ROUNDS = S // P
ARENA = 53200
CREDIT = 4

THETA = 10000.0
TWO_PI = [6.28125, 0.0019350051879882812, 3.0199159819567e-07]
DN_SLOTS = 6
ROUND = 12582912.0


QA, KA, VA, QB, KB, VB, QI, KI, WI = 0, 512, 640, 768, 1280, 1344, 1408, 1664, 1696
IN_CUTS = [(QI, IN2), (QA, KA), (KA, QB), (QB, KB), (KB, QI)]
TURNED = [("qi", 0), ("qi", 1), ("ki", 0), ("qa", 0), ("qa", 1), ("qa", 2), ("qa", 3), ("ka", 0), ("ka", 1),
          ("kb", 0), ("qb", 0), ("qb", 1), ("qb", 2), ("qb", 3)]
WINDOWED = [*range(1, T), 0]
UNITS = [(kind, t, h) for kind, t in [("a", t) for t in WINDOWED[:-1]] + [("b", t) for t in WINDOWED] + [("a", 0)] for h in range(8)]
TURN_AT = {8 * (T - 1) - 5 + n: 9 + n for n in range(5)}
TAKEN = -3e38
PICKS = KTOP // 8
PICKS_A, PICKS_B, PICKS_C = 24, 26, 27
PICK_AT = [n for n in range(6, 38) if n % 3]


class Banks:

    def __init__(self, before=None):
        self.before = before or [0] * 8
        self.uses = [0] * 8
        self.where = {}
        self.next = 0

    def take(self, key, bank=None, among=8):
        if bank is None:
            bank = self.next % among
            self.next = bank + 1
        self.where[key] = (bank, self.uses[bank])
        self.uses[bank] += 1


class Chain:

    def __init__(self, eng, sem):
        self.eng, self.sem, self.n = eng, sem, 0

    def mark(self, ins):
        ins.then_inc(self.sem, 1)
        self.n += 1

    def settle(self):
        self.eng.wait_ge(self.sem, self.n)

    def link(self, ins):
        self.mark(ins)
        self.settle()

    def restart(self):
        self.eng.sem_clear(self.sem)
        self.n = 0


def plan_first():
    b = Banks()
    for j in range(4):
        b.take(("ada", j))
    b.take(("taps",))
    b.take(("modT", 0))
    for c in range(C8):
        b.take(("hT", c))
    for m in range(MC):
        b.take(("val", m))
        b.take(("gate", m))
    for t in range(T):
        b.take(("lat", t))
    for n in range(3):
        b.take(("latT", n))
    for t in range(T):
        for half in range(2):
            b.take(("q", t, half))
            b.take(("kv", t, half))
    for j in range(4, 12):
        b.take(("ada", j))
    b.take(("modT", 1))
    for h in range(NH):
        b.take(("qT", h))
        b.take(("kT", h))
    b.next = 0
    for t in range(T):
        b.take(("o", t), bank=6 + t % 2)
        for h in range(NH):
            b.take(("s", t, h), among=6)
            b.take(("pT", t, h), among=6)
    b.next = 0
    for j in range(4):
        b.take(("oT", j))
    b.take(("mean",))
    b.take(("var",))
    for t in range(T):
        for half in range(2):
            b.take(("mix", t, half))
    for c in range(C8):
        b.take(("h2T", c))
    for t in range(T):
        b.take(("logit", t))
    b.take(("rank",))
    b.take(("slots",))
    for g in range(2):
        for c in range(C8):
            b.take(("xsT", g, c))
    return b


def plan_layer(before):
    b = Banks(before)
    for t in range(T):
        for half in range(2):
            b.take(("xT", t, half))
        for j in range(2):
            b.take(("in", t, j))
    for key in TURNED[:3]:
        b.take(key)
    b.next = 0
    for t in range(1, T):
        for h in range(IXH):
            b.take(("ix", t, h))
    for j in (3, 2):
        for t in range(T):
            b.take(("in", t, j))
    for key in TURNED[3:7]:
        b.take(key)
    b.take(("in", 0, 4))
    for key in TURNED[7:9]:
        b.take(key)
    b.take(("in", 1, 4))
    b.next = 0
    for n, (kind, t, h) in enumerate(UNITS):
        if h == 0:
            b.take(("o", kind, t), bank=6 + (n // 8) % 2)
        b.take(("s", kind, t, h), bank=n % 4)
        if n < T - 2:
            b.take(("in", n + 2, 4), bank=7)
        b.take(("pT", kind, t, h), bank=4 + n % 2)
        if n in TURN_AT:
            b.take(TURNED[TURN_AT[n]], bank=7)
    b.next = 0
    for j in range(C8):
        b.take(("oT", j))
    for t in range(T):
        for half in range(2):
            b.take(("mix", t, half))
        if t:
            for half in range(2):
                b.take(("x1T", t - 1, half))
    for c in range(2):
        b.take(("plT", c))
    for t in range(T):
        for half in range(2):
            b.take(("pp", t, half))
    for half in range(2):
        b.take(("x1T", T - 1, half))
    for t in range(T):
        for half in range(2):
            b.take(("pg", t, half))
    for t in range(T):
        for half in range(2):
            b.take(("dn", t, half), bank=2 * t + half)
    return b


def split_product(pe, ps, x, w, start, stop):
    xh, xl = x
    wh, wl = w
    pe.matmul(ps, xh, wh, start=start, stop=False)
    pe.matmul(ps, xh, wl, start=False, stop=False)
    return pe.matmul(ps, xl, wh, start=False, stop=stop)


def build(nc, i, out):
    ctx = ExitStack()
    with ctx:
        arena = ctx.enter_context(nc.sbuf_tensor("arena", [P, ARENA], F32))
        origin = nc.sbuf_base - 4 * ARENA

        def part(name, off, *shape, dt=F32R):
            ap = nc.alloc_sbuf_tensor_at(name, [P, int(np.prod(shape))], dt, offset=origin + 4 * off)[:]
            if len(shape) == 2:
                return ap.rearrange("p (a b) -> p a b", a=shape[0])
            if len(shape) == 3:
                return ap.rearrange("p (a b c) -> p a b c", a=shape[0], b=shape[1])
            return ap

        def at(off, *shape, dt=F32):
            n = int(np.prod(shape))
            ap = arena[:, off:off + n]
            if dt == BF16:
                ap = arena[:, off:off + n // 2].bitcast(BF16)
            elif dt == I32:
                ap = ap.bitcast(I32)
            if len(shape) == 2:
                return ap.rearrange("p (a b) -> p a b", a=shape[0])
            if len(shape) == 3:
                return ap.rearrange("p (a b c) -> p a b c", a=shape[0], b=shape[1])
            if len(shape) == 4:
                return ap.rearrange("p (a b c d) -> p a b c d", a=shape[0], b=shape[1], c=shape[2])
            return ap

        cursor = [0]

        def new(*shape, dt=F32):
            o = cursor[0]
            n = int(np.prod(shape))
            cursor[0] += (n + 1) // 2 if dt == BF16 else n
            cursor[0] += cursor[0] % 2
            return at(o, *shape, dt=dt)

        def sem(name):
            return ctx.enter_context(nc.semaphore(name))

        bank = [ctx.enter_context(nc.psum_tensor(f"bank{n}", [P, 512], F32)) for n in range(8)]
        bank_full = [sem(f"bank_full{n}") for n in range(8)]
        bank_free = [sem(f"bank_free{n}") for n in range(8)]

        ident = new(P)
        ones = new(P)
        before_me = new(P)
        ident_b = new(P, dt=BF16)
        chunk_mask = new(P, dt=BF16)
        own_mask = new(P, dt=BF16)
        prev_mask = new(P, dt=BF16)
        freqs = new(48)
        pos_i = new(2, T, dt=I32)
        pos = new(2, T)
        trig = new(2, 2, T, 16)
        trig64 = new(2, T, 32)
        half_neg = new(T)
        eps_col = new(2)
        spare = new(2)
        first_small = cursor[0]
        c_in = new(C8)
        c_silu = new(C8)
        b_ada = new(6, C8)
        g_mix = new(C8)
        g_ffn = new(C8)
        mod = new(4, C8)
        conv_w = new(MC, TAPS)
        conv_b = new(MC)
        cln_g = new(MC)
        cln_b = new(MC)
        qa_g = new(2)
        kva_g = new(1)
        qn_g = new(QK)
        kn_g = new(QK)
        b_route = new(NG + NE)
        ss = new(T)
        rstd = new(T)
        ss_q = new(2, T)
        r_q = new(2, T)
        hss = new(2, T, NH)
        hr = new(2, T, NH)
        mx = new(T, NH)
        nmx = new(T, NH)
        lsum = new(T, NH)
        rl = new(T, NH)
        end_small, cursor[0] = cursor[0], first_small
        sinks = new(8)
        nsinks = new(8)
        ix_g = new(IXD)
        ix_b = new(IXD)
        wi = new(T, IXH)
        mx2 = new(2, T, 8)
        nmx2 = new(2, T, 8)
        ls2 = new(2, T, 8)
        es2 = new(T, 8)
        rl2 = new(2, T, 8)
        top8 = new(8)
        bst = new(T, 2, 6)
        bag = new(T, 2)
        lrs = new(T)
        assert cursor[0] <= end_small
        cursor[0] = end_small
        gate_a = new(D)
        gate_f = new(D)
        cursor[0] += -cursor[0] % 8
        X = new(T, D)
        H = new(T, D)
        HT = new(C8, S)
        base = cursor[0]

        ada_w = [at(base, C8, 512), at(base + 4096, C8, 512)]
        w_out = at(base, C8, D)
        off = base + 8192
        w_in = at(off, C8, IN1)
        QT = at(off, NH, S)
        KT = at(off + NH * S, NH, S)
        V = at(off + 2 * NH * S, T, NH * VD)
        off += C8 * IN1
        w_q = at(off, 2, NH * QK)
        off += 2 * NH * QK
        w_kv = at(off, NH * (NOPE + VD))
        off += NH * (NOPE + VD)
        w_route = at(off, C8, NG + NE)
        off += C8 * (NG + NE)
        U = at(off, MC, PAD + S)
        off += MC * (PAD + S)
        DW = at(off, MC, S)
        mod_row0 = at(off, 2048)
        off += MC * S
        LATB = at(off, T, LAT)
        tap_rows = at(off, CONV)
        latT = at(off + T * LAT, 3, S)
        Pr = at(off, 3, S)
        PT = at(off + 3 * S, 3, S)
        mod_row1 = at(off, 2048)
        off += T * LAT + 3 * S
        K = at(off, T, NH, QK)
        off += T * NH * QK
        c_wide = at(off, C8, P)
        off += C8 * P
        junk = at(off, 256)
        off += 256
        sig = at(off, 2, 512)
        sqs = at(off, NH, QK)
        stat = at(off, 2, 512)
        xtmp = at(off + 1024, 2, 512)
        off += 2048
        assert off <= ARENA, off
        H0 = cursor[0] - C8 * S - T * D
        Q = at(H0, T, NH, QK)
        rope_t = QT.rearrange("p h n -> p (h n)")[:, 0:4 * T * NH * 16].rearrange("p (k n) -> p k n", k=4)
        O = at(H0, T, NH * VD)
        mixT = HT

        ring = [at(base + n * SLOT, C8, 2, FE) for n in range(4)]
        ring_d = [at(base + n * SLOT + C8 * 2 * FE, 2, D) for n in range(4)]
        stage = [at(base + 3 * SLOT, T, D), H]
        Yin = at(base + 4 * SLOT, T, 2, D)
        off = base + 4 * SLOT
        XsT = at(off, C8, XCOLS)
        off += C8 * XCOLS
        XW = [at(cursor[0] - C8 * S + n * C8 * P, C8, P) for n in range(2)]
        off2 = cursor[0] - C8 * S + 2 * C8 * P
        SG = at(off2, 2, FE)
        A = at(off2 + 2 * FE, 2, FE)
        AT = at(off2 + 4 * FE, 2, 2, P)
        Y = at(H0, 4, D)

        def route(*shape, dt=F32):
            nonlocal off
            ap = at(off, *shape, dt=dt)
            off += int(np.prod(shape))
            assert off <= ARENA, off
            return ap

        L = route(T, NG + NE)
        ramp = route(NE)
        slot0 = route(NE)
        ids = route(T, 2)
        gexp = route(T, NG)
        gsel = route(T, NG)
        ML = route(T, NE)
        tmp32 = route(T, NE)
        OH = [route(T, NE) for _ in range(2)]
        MM = route(T, NE)
        wts = route(T, 2)
        ered = route(T, 8)
        rank = route(T, NE)
        cnt = route(NE)
        pre = [route(NE) for _ in range(2)]
        off_e = route(NE)
        win_f = route(T, NE)
        win = route(T * NE + 2, dt=I32)
        rounds_f = route(4)
        rounds = route(2, dt=I32)
        dest_f = route(2, T, 2)
        dest = route(2, T, 2, dt=I32)
        slots_f = route(P)
        slots_i = route(P, dt=I32)
        idx_now = route(4, dt=I32)

        offB = base
        rest = QI
        w_in2 = [at(offB + C8 * rest, C8, IN2 - QI)]
        o = offB
        for a, b in IN_CUTS[1:]:
            w_in2.append(at(o, C8, b - a))
            o += C8 * (b - a)
        assert FC * S <= C8 * rest
        o = offB
        turned = {}
        for key in TURNED[3:]:
            turned[key] = at(o, S)
            o += S
        Pr2 = at(o, 4, S)
        PT2 = at(o + 4 * S, 3, S)
        assert o + 7 * S <= offB + C8 * sum(b - a for a, b in IN_CUTS[1:4])
        pg_hi = part("w_pg_hi", offB, C8, D)
        p_in = at(offB + C8 * D, T, PLE)
        w_pp = at(offB + C8 * D + T * PLE, 2, D)
        assert C8 * D + T * PLE + 2 * D <= C8 * rest
        pT = at(offB + C8 * rest, 2, S)
        aT = at(offB, FC, S)
        gu_lo = [part("gate_up_lo0", offB + C8 * rest, 2, C8, P), part("gate_up_lo1", H0, 2, C8, P)]
        HT_hi = part("ht_hi", H0 + T * D, C8, S)
        a_hi = [part(f"product_hi{n}", H0 + 2 * D + n * S, S) for n in range(2)]
        a_lo = [part(f"product_lo{n}", H0 + 3 * D + n * S, S) for n in range(2)]
        o = offB + C8 * IN2
        w_o2 = at(o, C8, D)
        gu_hi = [part(f"gate_up_hi{n}", o + 4 * D + n * 2 * D, 2, C8, P) for n in range(2)]
        dn_hi1, dn_lo1 = part("down_hi1", o + 4 * D, D), part("down_lo1", o + 5 * D, D)
        lnin_g = at(o, D)
        lnin_b = at(o + D, D)
        gu = [part(f"gate_up_whole{n}", o + n * 2 * D, 2, C8, P, dt=F32) for n in range(2)]
        o += C8 * D
        PJ = at(o, T, IN2)
        HT_lo = part("ht_lo", o, C8, S)
        SF = at(o + C8 * S, 2, S)
        o += T * IN2
        w_pg = part("w_pg_whole", o, C8, D, dt=F32)
        pg_lo = part("w_pg_lo", o, C8, D)
        w_dn = part("down_whole", o, DN_SLOTS, D, dt=F32)
        dn_hi = [part("down_hi0", o + DN_SLOTS * D, D), dn_hi1]
        dn_lo = [part("down_lo0", o + (DN_SLOTS + 1) * D, D), dn_lo1]
        assert o + C8 * D <= ARENA, o + C8 * D
        for key in TURNED[:3]:
            turned[key] = at(o, S)
            o += S
        IX = at(o, 3, S)
        SELM = at(o + 3 * S, 3, S, dt=BF16)
        R = at(o + 5 * S, 2, S)
        rt = H.rearrange("p t n -> p (t n)").rearrange("p (k n) -> p k n", k=4)
        O2 = at(H0, 2, T, 512)
        PLB = H
        lnG, lnB = gate_a, gate_f
        KD = gate_a.rearrange("p (t g n d) -> p t g n d", t=T, g=2, n=2)
        KBD = gate_f[:, 0:512].rearrange("p (t n d) -> p t n d", t=T, n=2)
        KID = gate_f[:, 512:].rearrange("p (t n d) -> p t n d", t=T, n=4)

        b1 = plan_first()
        b2 = plan_layer(b1.uses)

        class Use:

            def __init__(self, banks):
                self.b = banks

            def begin(self, pe, key, i=0):
                n, u = self.b.where[key]
                if self.b.before[n] + u > 0:
                    pe.wait_ge(bank_free[n], self.b.before[n] + u + i * self.b.uses[n])
                return bank[n]

            def full(self, ins, key):
                ins.then_inc(bank_full[self.b.where[key][0]], 1)

            def read(self, eng, key, i=0):
                n, u = self.b.where[key]
                eng.wait_ge(bank_full[n], self.b.before[n] + u + 1 + i * self.b.uses[n])
                return bank[n]

            def free(self, ins, key):
                ins.then_inc(bank_free[self.b.where[key][0]], 1)

            def evacuated(self, eng, key, i=0):
                n, u = self.b.where[key]
                eng.wait_ge(bank_free[n], self.b.before[n] + u + 1 + i * self.b.uses[n])

            def all_evacuated(self, eng, keys, i=0):
                last = {self.b.where[key][0]: key for key in sorted(keys, key=lambda k: self.b.where[k][1])}
                for key in last.values():
                    self.evacuated(eng, key, i)

        u1 = Use(b1)
        u2 = Use(b2)

        class Sig:

            def __init__(self, name, per):
                self.sem, self.per, self.n = sem(name), per, 0

            def inc(self, ins):
                ins.then_inc(self.sem, 1)
                self.n += 1

            def wait(self, eng, layer, k):
                eng.wait_ge(self.sem, layer * self.per + k)

        s_x = sem("x_loaded")
        s_small = sem("small_loaded")
        s_c = sem("c_loaded")
        s_ada = [sem("ada_loaded0"), sem("ada_loaded1")]
        s_win = sem("w_in_loaded")
        s_wq = sem("w_q_loaded")
        s_wout = sem("w_out_loaded")
        s_const = sem("constants")
        s_apart = sem("apart")
        s_silu = sem("c_silu_done")
        s_cw = sem("c_wide_done")
        s_ss = sem("square_sums")
        s_rstd = sem("rstd_done")
        s_xhat = sem("normalised")
        s_mod = sem("mod_done")
        s_conv = sem("conv_taps_done")
        s_cent = sem("conv_centred")
        s_csq = sem("conv_squared")
        s_cnorm = sem("conv_normalised")
        s_yconv = sem("conv_out")
        s_angle = sem("angles")
        s_trig = sem("trig_done")
        s_latss = sem("latent_sums")
        s_latr = sem("latent_rstd")
        s_latn = sem("latents_normalised")
        s_hss = sem("head_sums")
        s_hstd = sem("head_std")
        s_rot = sem("heads_rotated")
        s_negmax = sem("negated_max")
        s_csum = sem("conv_squares_summed")
        s_pv = sem("values_weighted")
        s_x1 = sem("x1_done")
        s_ss2 = sem("x1_square_sums")
        s_rstd2 = sem("x1_rstd")
        s_xhat2 = sem("x1_normalised")
        s_gexp = sem("group_exponentials")
        s_eexp = sem("expert_exponentials")
        s_gdiff = sem("group_differences")
        s_ediff = sem("expert_difference")
        s_masks = sem("expert_masks")
        s_dest = sem("destinations")
        s_fill = sem("slot_table_filled")
        s_slots = sem("slot_table_scattered")
        s_slotin = sem("slot_table_loaded")
        s_stage = [sem("sorted_rows0"), sem("sorted_rows1")]
        s_rounds = sem("rounds_known")
        s_pad = sem("xs_pad")
        s_w = [sem(f"expert_weights{n}") for n in range(4)]
        m_xw = sem("window_copied")
        m_gu = sem("gate_up_done")
        m_silu = sem("silu_done")
        m_a = sem("product_done")
        m_at = sem("product_transposed")
        m_atc = sem("product_copied")
        m_y = sem("down_done")
        m_ya = sem("down_copied_a")
        m_yb = sem("down_copied_b")
        m_st = [sem(f"rows_stored{n}") for n in range(4)]
        SCATTERED = 32
        s_yin = [sem(f"expert_rows_loaded{n}") for n in range(T)]
        s_lnin = sem("ln_in_loaded")
        s_mean = sem("ln_in_stats")
        s_lnr = sem("ln_in_rstd")
        a_free = sem("region_a_free")
        b_free = sem("region_b_free")
        layer_in = sem("layer_input_ready")
        d_in2 = [sem(f"w_in2_loaded{n}") for n in range(len(IN_CUTS))]
        d_o2 = sem("w_o_loaded")
        d_pg = sem("w_pg_loaded")
        d_sm = sem("layer_small_loaded")
        d_ln1 = sem("ln1_loaded")
        d_ln2 = sem("ln2_loaded")
        d_pp = sem("ple_loaded")
        d_gu = [sem("gate_up_loaded0"), sem("gate_up_loaded1")]
        d_dn = [sem(f"w_down_loaded{n}") for n in range(DN_SLOTS)]
        y_kst = Sig("key_stats", 1)
        y_krs = Sig("key_rstd", 1)
        y_rot = Sig("rotated", 6)
        s_w1 = sem("second_rows_weighted")
        y_ix = Sig("index_scores_added", 3 * IXH)
        y_sel = Sig("selected", 3)
        y_neg = Sig("negated_max2", 64)
        y_pv = Sig("values_weighted2", 56)
        y_sinkd = Sig("sink_differences", T)
        y_sinke = Sig("sink_exponentials", T)
        y_mst = Sig("ln1_stats", T)
        y_mrs = Sig("ln1_rstd", T)
        y_x1 = Sig("ln1_done", T)
        y_ple = Sig("ple_done", 2 * T)
        y_est = Sig("ln2_stats", T)
        y_ers = Sig("ln2_rstd", T)
        y_dn = Sig("down_chunk_used", FC - 1)
        y_xhi = Sig("x1_high_parts", 2 * T)
        y_ghi = Sig("w_pg_high_parts", C8)
        y_glo = Sig("w_pg_low_parts", C8)
        y_dhi = Sig("down_high_parts", FC)
        y_dlo = Sig("down_low_parts", FC)
        f_hi = sem("ff_high_parts")
        f_lo = sem("ff_low_parts")
        f_g = sem("ff_gate_up_done")
        f_s = sem("ff_silu_done")
        f_a = sem("ff_product_done")
        s_out = sem("out_stored")
        link_pe, link_dve, link_act, link_pool = sem("pe_own"), sem("dve_own"), sem("act_own"), sem("pool_own")

        slot_table = nc.dram_tensor("slot_table", (NE * S, 1), F32, kind="Internal").ap()
        sorted_rows = nc.dram_tensor("sorted_rows", (2 * S, D), F32, kind="Internal").ap()
        expert_rows = nc.dram_tensor("expert_rows", (2 * S, D), F32, kind="Internal").ap()

        block = ctx.enter_context(nc.Block())

        def apart(eng):
            eng.sem_inc(s_apart, 1)

        def width(n):
            kind, t, h = UNITS[n]
            return min(t + 1, 2) * P if kind == "a" else (t + 1) * P

        def weighted2(eng, n, l):
            kind, t, h = UNITS[n]
            if h == 7:
                u2.read(eng, ("o", kind, t), l)
            else:
                y_pv.wait(eng, l, n - n // 8 + 1)

        def down_loaded(eng, f, l):
            per = (FC - 1 - f % DN_SLOTS) // DN_SLOTS + 1
            eng.wait_ge(d_dn[f % DN_SLOTS], 16 * per * l + 16 * (f // DN_SLOTS + 1))

        @block.sync
        def _(sp):
            sp.dma_start(c_in, i["c"].rearrange("b (p c) -> (b p) c", c=C8)).then_inc(s_c, 16)
            def load_ada(j):
                if j >= 2:
                    u1.evacuated(sp, ("ada", j - 2))
                sp.dma_start(ada_w[j % 2], i["w_ada"][0, :, j * 512:(j + 1) * 512]
                             .rearrange("(p c) n -> p c n", c=C8)).then_inc(s_ada[j % 2], 16)

            load_ada(0)
            for t in range(T):
                sp.dma_start(X[:, t], i["x"][0, t * P:(t + 1) * P]).then_inc(s_x, 16)
            for j in range(1, 4):
                load_ada(j)
            sp.dma_start(w_in, i["w_in"][0].rearrange("(p c) n -> p c n", c=C8)).then_inc(s_win, 16)
            sp.dma_start(w_q, i["w_q_b"][0].rearrange("(c p) n -> p c n", c=2)).then_inc(s_wq, 16)
            sp.dma_start(w_kv, i["w_kv_b"][0]).then_inc(s_wq, 16)
            for j in range(4, 12):
                load_ada(j)
            for n in (10, 11):
                u1.evacuated(sp, ("ada", n))
            sp.dma_start(w_out[:, 0:4], i["w_out"][0, 0:512].rearrange("(m p) n -> p m n", p=P)).then_inc(s_wout, 16)
            sp.dma_start(w_out[:, 4:8], i["w_out"][0, 512:1024].rearrange("(m p) n -> p m n", p=P)).then_inc(s_wout, 16)
            sp.dma_start(w_route[:, :, 0:NG], i["w_group"][0].rearrange("(p c) n -> p c n", c=C8)).then_inc(s_wout, 16)
            sp.dma_start(w_route[:, :, NG:], i["w_expert"][0].rearrange("(p c) n -> p c n", c=C8)).then_inc(s_wout, 16)
            def load_expert(n, s, pre_use):
                sp.wait_ge(m_y, pre_use)
                for k, w in enumerate(("w_gate_e", "w_up_e")):
                    sp.dma_start(ring[s][:, :, k], i[w][0][bass.ds(n, 1)].rearrange("a (p c) n -> (a p) c n", c=C8)).then_inc(s_w[s], 16)
                sp.dma_start(ring_d[s], i["w_down_e"][0][bass.ds(n, 1)].rearrange("a (p c) n -> (a p) c n", c=2)).then_inc(s_w[s], 16)

            sp.wait_ge(s_x1, T)
            sp.wait_ge(s_slots, 16 * (2 * T))
            sp.dma_start(slots_f, slot_table.rearrange("(q p) o -> q (p o)", p=P)).then_inc(s_slotin, 16)
            for n in range(4):
                sp.wait_ge(m_st[n], SCATTERED)
            for g in range(2):
                for q in range(T):
                    sp.dma_start(stage[g][:, q], sorted_rows[(T * g + q) * P:(T * g + q + 1) * P]).then_inc(s_stage[g], 16)
            for c in range(C8):
                u1.evacuated(sp, ("xsT", 0, c))
            with sp.Fori(0, NE // 4) as it:
                for s in range(4):
                    load_expert(it * 4 + s, s, it * 4 + s + 1)
            sp.wait_ge(s_rounds, 1)
            n_rounds = sp.value_load(rounds[0:1, 0:1], min_val=1, max_val=ROUNDS)
            with sp.If(n_rounds > 1):
                with sp.Fori(1, n_rounds) as r:
                    with sp.Fori(0, NE // 4) as it:
                        for s in range(4):
                            load_expert(it * 4 + s, s, r * NE + it * 4 + s + 1)
            for n in range(4):
                sp.wait_ge(m_st[n], SCATTERED + 16 * (NE // 4) * n_rounds)
            for t in range(T):
                sp.dma_start(Yin[:, t], expert_rows[2 * t * P:2 * (t + 1) * P].rearrange("(p k) n -> p k n", k=2)).then_inc(s_yin[t], 16)
            sp.wait_ge(b_free, 1)
            sp.dma_start(lnin_g, i["ln_in_g_2"].partition_broadcast(P)).then_inc(s_lnin, 16)
            sp.dma_start(lnin_b, i["ln_in_b_2"].partition_broadcast(P)).then_inc(s_lnin, 16)
            with sp.Fori(0, LAYERS) as l:
                def of(name):
                    return i[name][bass.ds(l, 1)]

                def load_in(j):
                    a, b = IN_CUTS[j]
                    sp.dma_start(w_in2[j], of("w_in_2").rearrange("a (p c) n -> (a p) c n", c=C8)[:, :, a:b]).then_inc(d_in2[j], 16)

                sp.wait_ge(b_free, l + 1)
                apart(sp)
                load_in(0)
                sp.dma_start(sinks, of("attn_sinks_2").rearrange("a n -> (a n)").partition_broadcast(P)).then_inc(d_sm, 16)
                sp.dma_start(ix_g, of("idx_k_g_2").rearrange("a n -> (a n)").partition_broadcast(P)).then_inc(d_sm, 16)
                sp.dma_start(ix_b, of("idx_k_b_2").rearrange("a n -> (a n)").partition_broadcast(P)).then_inc(d_sm, 16)
                sp.wait_ge(a_free, l + 1)
                apart(sp)
                for j in range(1, len(IN_CUTS)):
                    load_in(j)
                sp.wait_ge(layer_in, l * T + T)
                apart(sp)
                sp.dma_start(w_o2, of("w_o_2").rearrange("a (m p) n -> (a p) m n", p=P)).then_inc(d_o2, 16)
                u2.read(sp, TURNED[-1], l)
                apart(sp)
                sp.dma_start(lnG, of("ln1_g_2").rearrange("a n -> (a n)").partition_broadcast(P)).then_inc(d_ln1, 16)
                sp.dma_start(lnB, of("ln1_b_2").rearrange("a n -> (a n)").partition_broadcast(P)).then_inc(d_ln1, 16)
                u2.read(sp, ("oT", 0), l)
                apart(sp)
                sp.dma_start(p_in, of("p_2").rearrange("l b (t p) n -> (l b p) t n", p=P)).then_inc(d_pp, 16)
                sp.dma_start(w_pp, of("w_pp_2").rearrange("a (c p) n -> (a p) c n", p=P)).then_inc(d_pp, 16)
                sp.dma_start(w_pg, of("w_pg_2").rearrange("a (p c) n -> (a p) c n", c=C8)).then_inc(d_pg, 16)
                u2.read(sp, ("mix", T - 1, 1), l)
                apart(sp)
                with sp.Fori(0, FC // 2) as it:
                    for s in range(2):
                        sp.wait_ge(f_lo, l * FC + it * 2 + s - 2 + 1 + CREDIT)
                        for k in range(2):
                            sp.dma_start(gu[s][:, k], of("w_gu_2").rearrange("a (p c) (k f n) -> k f (a p) c n", c=C8, k=2, n=P)
                                         [k, bass.ds(it * 2 + s, 1)].rearrange("f p c n -> (f p) c n")).then_inc(d_gu[s], 16)
                y_x1.wait(sp, l, T)
                apart(sp)
                sp.dma_start(lnG, of("ln2_g_2").rearrange("a n -> (a n)").partition_broadcast(P)).then_inc(d_ln2, 16)
                sp.dma_start(lnB, of("ln2_b_2").rearrange("a n -> (a n)").partition_broadcast(P)).then_inc(d_ln2, 16)
                u2.read(sp, ("pg", T - 1, 1), l)
                apart(sp)
                for f in range(FC):
                    if f >= DN_SLOTS:
                        y_dlo.wait(sp, l, f - DN_SLOTS + 1)
                        apart(sp)
                    sp.dma_start(w_dn[:, f % DN_SLOTS], of("w_down_2").rearrange("a (f p) n -> f (a p) n", p=P)[f]).then_inc(d_dn[f % DN_SLOTS], 16)
            for t in range(T):
                sp.wait_ge(layer_in, LAYERS * T + t + 1)
                sp.dma_start(out[0, t * P:(t + 1) * P], X[:, t]).then_inc(s_out, 16)
            sp.wait_ge(s_out, 16 * T)

        small = [
            (freqs, i["freqs"].partition_broadcast(P)),
            (pos_i[:, 0], i["positions"][0].rearrange("(t p) -> p t", p=P)),
            (pos_i[:, 1], i["positions_2"][0].rearrange("(t p) -> p t", p=P)),
            (b_ada, i["b_ada"][0].rearrange("(v p c) -> p v c", p=P, c=C8)),
            (g_mix, i["norm_mix"][0].rearrange("(p c) -> p c", c=C8)),
            (g_ffn, i["norm_ffn"][0].rearrange("(p c) -> p c", c=C8)),
            (qa_g, i["q_a_norm"][0].rearrange("(c p) -> p c", p=P)),
            (kva_g, i["kv_a_norm"][0].rearrange("(c p) -> p c", p=P)),
            (qn_g, i["q_norm"][0].partition_broadcast(P)),
            (kn_g, i["k_norm"][0].partition_broadcast(P)),
            (conv_b, i["conv_b"][0].rearrange("(m p) -> p m", p=P)),
            (cln_g, i["conv_ln_g"][0].rearrange("(m p) -> p m", p=P)),
            (cln_b, i["conv_ln_b"][0].rearrange("(m p) -> p m", p=P)),
            (b_route[:, 0:NG], i["b_group"][0].partition_broadcast(P)),
            (b_route[:, NG:], i["b_expert"][0].partition_broadcast(P)),
            (gate_a, i["b_ada"][0, 2 * D:3 * D].partition_broadcast(P)),
            (gate_f, i["b_ada"][0, 5 * D:6 * D].partition_broadcast(P)),
        ]
        small += [(tap_rows[0:TAPS], i["conv_w"][0])]
        SMALL = 16 * len(small)

        @block.gpsimd
        def _(pool):
            own = Chain(pool, link_pool)
            for k, (dst, src) in enumerate(small):
                pool.dma_start(dst, src, allow_slow_non_contiguous=True).then_inc(s_small, 16)
            own.mark(pool.memset(ident, 0.0))
            own.mark(pool.memset(ones, 1.0))
            own.mark(pool.memset(before_me, 1.0))
            own.mark(pool.memset(chunk_mask, 0.0))
            own.mark(pool.memset(own_mask, 0.0))
            own.mark(pool.memset(prev_mask, 0.0))
            own.mark(pool.memset(half_neg, -0.5))
            own.mark(pool.memset(eps_col, EPS))
            own.mark(pool.memset(U[:, :, 0:PAD], 0.0))
            own.settle()
            own.mark(pool.affine_select(ident, ident, [[-1, P]], ALU.not_equal, 1.0, base=0, channel_multiplier=1))
            own.mark(pool.affine_select(before_me, before_me, [[1, P]], ALU.is_gt, 0.0, base=0, channel_multiplier=-1))
            own.mark(pool.memset(chunk_mask[0:CHUNK, CHUNK:P], NEG))
            own.mark(pool.affine_select(own_mask, own_mask, [[-1, P]], ALU.is_ge, NEG, base=0, channel_multiplier=1))
            own.mark(pool.affine_select(prev_mask, prev_mask, [[1, P]], ALU.is_gt, NEG, base=0, channel_multiplier=-1))
            own.settle()
            pool.tensor_copy(ident_b, ident).then_inc(s_const, 1)
            pool.wait_ge(s_ss, T)
            own.link(pool.tensor_scalar(rstd, ss, 1.0 / D, EPS, ALU.mult, ALU.add))
            pool.tensor_tensor(rstd, rstd, half_neg, ALU.pow).then_inc(s_rstd, 1)
            pool.wait_ge(s_latss, 2 * T)
            own.mark(pool.tensor_scalar(r_q[:, 0], ss_q[:, 0], 1.0 / QR, EPS, ALU.mult, ALU.add))
            own.mark(pool.tensor_scalar(r_q[:, 1], ss_q[:, 1], 1.0 / KR, EPS, ALU.mult, ALU.add))
            own.settle()
            pool.tensor_tensor(r_q[:, 0], r_q[:, 0], half_neg, ALU.pow).then_inc(s_latr, 1)
            pool.tensor_tensor(r_q[:, 1], r_q[:, 1], half_neg, ALU.pow).then_inc(s_latr, 1)
            pool.wait_ge(s_x1, T)
            own.mark(pool.iota(ramp, [[-1, NE]], base=NE, channel_multiplier=0, allow_small_or_imprecise_dtypes=True))
            own.mark(pool.iota(slot0, [[S, NE]], base=0, channel_multiplier=0, allow_small_or_imprecise_dtypes=True))
            own.mark(pool.iota(ids, [[2 * P, T], [1, 2]], base=0, channel_multiplier=2, allow_small_or_imprecise_dtypes=True))
            own.mark(pool.memset(slots_f, 1e6))
            own.settle()
            pool.memset(XsT[:, :, 2 * S:], 0.0).then_inc(s_pad, 1)
            pool.dma_start(slot_table.rearrange("(q p) o -> q (p o)", p=P), slots_f).then_inc(s_fill, 16)
            pool.wait_ge(s_ss2, T)
            own.link(pool.tensor_scalar(rstd, ss, 1.0 / D, EPS, ALU.mult, ALU.add))
            pool.tensor_tensor(rstd, rstd, half_neg, ALU.pow).then_inc(s_rstd2, 1)
            pool.wait_ge(s_dest, 1)
            pool.wait_ge(s_fill, 16)
            for t in range(T):
                for k in range(2):
                    pool.indirect_dma_start(slot_table, bass.IndirectOffsetOnAxis(dest[:, 1, t, k:k + 1], 0),
                                            ids[:, t, k:k + 1], None).then_inc(s_slots, 16)
            for t in range(T):
                for k in range(2):
                    pool.indirect_dma_start(sorted_rows, bass.IndirectOffsetOnAxis(dest[:, 0, t, k:k + 1], 0),
                                            H[:, t], None).then_inc(m_st[t], 16)
            u1.evacuated(pool, ("slots",))
            last_row = pool.to_reg(2 * S - 1)
            n_rounds = pool.value_load(rounds[0:1, 0:1], min_val=1, max_val=ROUNDS)
            with pool.Fori(0, n_rounds) as r:
                with pool.Fori(0, NE // 4) as it:
                    own.restart()
                    for s in range(4):
                        n = r * NE + it * 4 + s
                        pool.wait_ge(m_st[s], SCATTERED + 16 * (r * (NE // 4) + it))
                        own.link(pool.tensor_copy(idx_now[:, s:s + 1], slots_i[:, bass.ds((it * 4 + s) * ROUNDS + r, 1)]))
                        pool.wait_ge(m_ya, n + 1 + CREDIT)
                        pool.wait_ge(m_yb, n + 1 + CREDIT)
                        apart(pool)
                        pool.indirect_dma_start(expert_rows, bass.IndirectOffsetOnAxis(idx_now[:, s:s + 1], 0), Y[:, s], None,
                                                bounds_check=last_row, oob_is_err=False).then_inc(m_st[s], 16)
            own.settle()

            def rstd_of(t, ready, done):
                ready()
                apart(pool)
                own.link(pool.tensor_scalar(lrs[:, t:t + 1], bag[:, t, 1:2], LN_EPS, None, ALU.add))
                done(pool.tensor_tensor(lrs[:, t:t + 1], lrs[:, t:t + 1], half_neg[:, 0:1], ALU.pow))

            for t in range(T):
                rstd_of(t, lambda: pool.wait_ge(s_mean, t + 1), lambda ins: ins.then_inc(s_lnr, 1))
            with pool.Fori(0, LAYERS) as l:
                own.restart()
                y_kst.wait(pool, l, 1)
                apart(pool)
                own.link(pool.tensor_scalar(lrs, bag[:, :, 1], LN_EPS, None, ALU.add))
                y_krs.inc(pool.tensor_tensor(lrs, lrs, half_neg, ALU.pow))
                for t in range(T):
                    rstd_of(t, lambda: y_mst.wait(pool, l, t + 1), y_mrs.inc)
                for t in range(T):
                    rstd_of(t, lambda: y_est.wait(pool, l, t + 1), y_ers.inc)

        @block.scalar
        def _(act):
            own = Chain(act, link_act)
            act.wait_ge(s_c, 16)
            act.activation(c_silu, c_in, ACT.Silu).then_inc(s_silu, 1)
            act.wait_ge(s_x, 16 * T)
            for t in range(T):
                act.activation(HT[:, t * 2:t * 2 + 2], X[:, t], ACT.Square, accum_out=ss[:, t:t + 1]).then_inc(s_ss, 1)
            act.wait_ge(s_angle, 1)
            own.mark(act.activation(trig[:, 0], trig[:, 0], ACT.Sin))
            own.mark(act.activation(trig[:, 1], trig[:, 1], ACT.Sin))
            act.activation(trig64, trig64, ACT.Sin).then_inc(s_trig, 1)
            for j in range(4):
                ps = u1.read(act, ("ada", j))
                u1.free(act.copy(mod_row0[:, j * 512:(j + 1) * 512], ps[:]), ("ada", j))
            act.wait_ge(s_mod, 1)
            for c in range(0, C8, 2):
                ps = u1.read(act, ("hT", c))
                u1.free(act.activation(HT[:, c], ps[:], ACT.Identity, bias=mod[:, 0, c:c + 1],
                                       scale=mod[:, 1, c:c + 1]), ("hT", c))
            for m in range(MC):
                ps = u1.read(act, ("gate", m))
                if m >= 2:
                    u1.evacuated(act, ("val", m - 2))
                u1.free(act.activation(sig[:, m % 2], ps[:], ACT.Sigmoid), ("gate", m))
            for t in range(T):
                ps = u1.read(act, ("lat", t))
                u1.free(act.copy(LATB[:, t], ps[:, 0:LAT]), ("lat", t))
                u1.evacuated(act, ("lat", t))
                if t:
                    act.wait_ge(s_latss, 2 * t)
                act.activation(junk[:, 0:QR], LATB[:, t, 0:QR], ACT.Square, accum_out=ss_q[:, 0, t:t + 1]).then_inc(s_latss, 1)
                act.wait_ge(s_latss, 2 * t + 1)
                act.activation(junk[:, 0:KR], LATB[:, t, QR:QR + KR], ACT.Square, accum_out=ss_q[:, 1, t:t + 1]).then_inc(s_latss, 1)
            for t in range(T):
                for half in range(2):
                    hs = slice(4 * half, 4 * half + 4)
                    ps = u1.read(act, ("q", t, half))
                    u1.free(act.copy(Q[:, t, hs], ps[:, 0:384].rearrange("p (h d) -> p h d", d=QK)), ("q", t, half))
                    ps = u1.read(act, ("kv", t, half))
                    kv = ps[:].rearrange("p (h d) -> p h d", d=NOPE + VD)
                    own.mark(act.copy(K[:, t, hs, 0:NOPE], kv[:, :, 0:NOPE]))
                    u1.free(act.copy(V[:, t, 256 * half:256 * half + 256].rearrange("p (h d) -> p h d", d=VD),
                                     kv[:, :, NOPE:]), ("kv", t, half))
            act.wait_ge(s_hss, 1)
            act.activation(hr, hss, ACT.Sqrt).then_inc(s_hstd, 1)
            for j in (6, 7, 8, 9):
                ps = u1.read(act, ("ada", j))
                u1.free(act.copy(mod_row1[:, (j - 6) * 512:(j - 5) * 512], ps[:]), ("ada", j))
            for h in range(NH):
                ps = u1.read(act, ("qT", h))
                u1.free(act.copy(QT[0:QK, h], ps[0:QK, :]), ("qT", h))
            n = 0
            for t in range(T):
                for h in range(NH):
                    w = (t + 1) * P
                    act.wait_ge(s_negmax, n + 1)
                    if n >= 3:
                        u1.evacuated(act, ("pT",) + divmod(n - 3, NH))
                    ps = u1.read(act, ("s", t, h))
                    ins = act.activation(Pr[:, n % 3, 0:w], ps[:, 0:w], ACT.Exp, bias=nmx[:, t, h:h + 1],
                                         scale=QK ** -0.5, accum_out=lsum[:, t, h:h + 1])
                    u1.free(ins, ("s", t, h))
                    n += 1
            for j in range(4):
                ps = u1.read(act, ("oT", j))
                u1.free(act.copy(mixT[:, 4 + j], ps[:]), ("oT", j))
            for m in range(MC):
                act.wait_ge(s_cent, m + 1)
                if m >= 2:
                    act.wait_ge(s_csum, m - 1)
                act.activation(stat[:, m % 2], DW[:, m], ACT.Square).then_inc(s_csq, 1)
            ps = u1.read(act, ("var",))
            u1.free(act.activation(stat[:, 0], ps[:], ACT.Sqrt, bias=eps_col[:, 0:1], scale=1.0 / CONV), ("var",))
            for m in range(MC):
                act.wait_ge(s_cnorm, m + 1)
                act.activation(mixT[:, m], DW[:, m], ACT.Silu, bias=cln_b[:, m:m + 1], scale=cln_g[:, m:m + 1]).then_inc(s_yconv, 1)
            for t in range(T):
                act.wait_ge(s_x1, t + 1)
                act.activation(H[:, t], X[:, t], ACT.Square, accum_out=ss[:, t:t + 1]).then_inc(s_ss2, 1)
            for c in range(0, C8, 2):
                ps = u1.read(act, ("h2T", c))
                u1.free(act.activation(HT[:, c], ps[:], ACT.Identity, bias=mod[:, 2, c:c + 1],
                                       scale=mod[:, 3, c:c + 1]), ("h2T", c))
            act.wait_ge(s_gdiff, 1)
            act.activation(gexp, gexp, ACT.Exp).then_inc(s_gexp, 1)
            act.wait_ge(s_ediff, 1)
            act.activation(ered[:, :, 4], ered[:, :, 4], ACT.Exp).then_inc(s_eexp, 1)
            for g in range(2):
                for c in range(0, C8, 2):
                    ps = u1.read(act, ("xsT", g, c))
                    u1.free(act.activation(XsT[:, c, g * S:(g + 1) * S], ps[:], ACT.Identity, bias=mod[:, 2, c:c + 1],
                                           scale=mod[:, 3, c:c + 1]), ("xsT", g, c))
            act.sem_inc(m_silu, CREDIT)
            act.sem_inc(m_atc, CREDIT)
            act.sem_inc(m_yb, CREDIT)

            def silu(n, s):
                act.wait_ge(m_gu, n + 1 + CREDIT)
                act.wait_ge(m_a, n - 2 + 1 + CREDIT)
                act.activation(SG[:, s % 2], bank[s % 2][:, 0:FE], ACT.Silu).then_inc(m_silu, 1)

            def copy_at(n, s):
                act.wait_ge(m_at, n + 1 + CREDIT)
                act.wait_ge(m_y, n - 2 + 1 + CREDIT)
                act.copy(AT[:, s % 2], bank[2 + s % 2][:, 0:2 * P].rearrange("p (c m) -> p c m", c=2)).then_inc(m_atc, 1)

            def copy_y(n, it, s):
                act.wait_ge(m_y, n + 1 + CREDIT)
                act.wait_ge(m_st[s], SCATTERED + 16 * it)
                act.copy(Y[:, s, 512:], bank[5 + 2 * (s % 2)][:]).then_inc(m_yb, 1)

            act.wait_ge(s_rounds, 1)
            n_rounds = act.value_load(rounds[0:1, 0:1], min_val=1, max_val=ROUNDS)
            with act.Fori(0, n_rounds) as r:
                with act.Fori(0, NE // 4) as it:
                    n = r * NE + it * 4
                    for s in range(4):
                        silu(n + s, s)
                        if s:
                            copy_y(n + s - 1, r * (NE // 4) + it, s - 1)
                        copy_at(n + s, s)
                    copy_y(n + 3, r * (NE // 4) + it, 3)
            for t in range(T):
                act.wait_ge(s_yin[t], 16)
                act.activation(Yin[:, t, 1], Yin[:, t, 1], ACT.Copy, scale=wts[:, t, 1:2]).then_inc(s_w1, 1)
            act.sem_inc(f_s, CREDIT)
            act.sem_inc(f_hi, CREDIT)
            with act.Fori(0, LAYERS) as l:
                own.restart()
                def take_in(t, j):
                    a, b = IN_CUTS[j]
                    ps = u2.read(act, ("in", t, j), l)
                    u2.free(act.copy(PJ[:, t, a:b], ps[:, 0:b - a]), ("in", t, j))

                def take_turned(key, dst):
                    ps = u2.read(act, key, l)
                    u2.free(act.copy(dst, ps[:]), key)

                def take_tile(kind, t):
                    for half in range(2):
                        ps = u2.read(act, (kind, t, half), l)
                        u2.free(act.copy(HT[:, 4 * half:4 * half + 4, t * P:(t + 1) * P], ps[:].rearrange("p (c m) -> p c m", c=4)),
                                (kind, t, half))

                def split_x1(t):
                    for half in range(2):
                        ps = u2.read(act, ("x1T", t, half), l)
                        y_xhi.inc(act.copy(HT_hi[:, 4 * half:4 * half + 4, t * P:(t + 1) * P], ps[:].rearrange("p (c m) -> p c m", c=4)))

                def gate_up_high(it, s):
                    n = l * FC + it * 2 + s
                    act.wait_ge(d_gu[s], 32 * (l * (FC // 2) + it + 1))
                    act.wait_ge(f_g, n - 2 + 1 + CREDIT)
                    act.copy(gu_hi[s], gu[s]).then_inc(f_hi, 1)

                def ff_silu(it, s):
                    n = l * FC + it * 2 + s
                    act.wait_ge(f_g, n + 1 + CREDIT)
                    act.wait_ge(f_a, n - 2 + 1 + CREDIT)
                    act.activation(SF[:, s], bank[2 * s][:], ACT.Silu).then_inc(f_s, 1)

                def down_high(f):
                    down_loaded(act, f, l)
                    if f >= 2:
                        y_dn.wait(act, l, f - 2 + 1)
                    act.copy(dn_hi[f % 2], w_dn[:, f % DN_SLOTS])
                    act.wait_ge(f_a, l * FC + f + 1 + CREDIT)
                    y_dhi.inc(act.copy(a_hi[f % 2], aT[:, f]))

                for t in range(T):
                    take_tile("xT", t)
                    take_in(t, 0)
                    take_in(t, 1)
                for key in TURNED[:3]:
                    take_turned(key, turned[key])
                n = 0
                for t in range(1, T):
                    for h in range(IXH):
                        if n >= 2:
                            y_ix.wait(act, l, n - 1)
                        ps = u2.read(act, ("ix", t, h), l)
                        u2.free(act.activation(R[:, n % 2, 0:(t + 1) * P], ps[:, 0:(t + 1) * P], ACT.Relu), ("ix", t, h))
                        n += 1
                for j in (3, 2):
                    for t in range(T):
                        take_in(t, j)
                own.mark(act.activation(spare, eps_col, ACT.Exp))
                for key in TURNED[3:7]:
                    take_turned(key, turned[key])
                take_in(0, 4)
                for key in TURNED[7:9]:
                    take_turned(key, turned[key])
                take_in(1, 4)

                def take_pt(n):
                    kind, t, h = UNITS[n]
                    w = width(n)
                    if n >= 3:
                        weighted2(act, n - 3, l)
                    ps = u2.read(act, ("pT", kind, t, h), l)
                    u2.free(act.copy(PT2[:, n % 3, 0:w], ps[:, 0:w]), ("pT", kind, t, h))

                for n, (kind, t, h) in enumerate(UNITS):
                    w = width(n)
                    kk = 0 if kind == "a" else 1
                    y_neg.wait(act, l, n + 1)
                    if n >= 4:
                        u2.evacuated(act, ("pT",) + UNITS[n - 4], l)
                    ps = u2.read(act, ("s", kind, t, h), l)
                    u2.free(act.activation(Pr2[:, n % 4, 0:w], ps[:, 0:w], ACT.Exp, bias=nmx2[:, kk, t, h:h + 1],
                                           scale=HD ** -0.5, accum_out=ls2[:, kk, t, h:h + 1]), ("s", kind, t, h))
                    if n < T - 2:
                        take_in(n + 2, 4)
                    if n >= 3:
                        take_pt(n - 3)
                    if n in TURN_AT:
                        key = TURNED[TURN_AT[n]]
                        take_turned(key, turned[key])
                    if kind == "a" and h == 7:
                        y_sinkd.wait(act, l, WINDOWED.index(t) + 1)
                        y_sinke.inc(act.activation(es2[:, t], es2[:, t], ACT.Exp))
                for n in range(len(UNITS) - 3, len(UNITS)):
                    take_pt(n)
                for j in range(C8):
                    take_turned(("oT", j), HT[:, j])
                split_x1(0)
                act.wait_ge(d_pg, 16 * (l + 1))
                apart(act)
                for c in range(C8):
                    y_ghi.inc(act.copy(pg_hi[:, c], w_pg[:, c]))
                for t in range(1, T - 1):
                    split_x1(t)
                for c in range(2):
                    take_turned(("plT", c), pT[:, c])
                for t in range(T):
                    for half in range(2):
                        take_turned(("pp", t, half), PLB[:, t, 512 * half:512 * half + 512])
                split_x1(T - 1)
                gate_up_high(0, 0)
                n = 0
                for t in range(T):
                    for half in range(2):
                        if n >= 2:
                            y_ple.wait(act, l, n - 1)
                        ps = u2.read(act, ("pg", t, half), l)
                        u2.free(act.activation(SF[:, n % 2], ps[:], ACT.Sigmoid), ("pg", t, half))
                        n += 1
                y_ple.wait(act, l, n)
                apart(act)
                with act.Fori(0, FC // 2 - 1) as it:
                    gate_up_high(it, 1)
                    ff_silu(it, 0)
                    gate_up_high(it + 1, 0)
                    ff_silu(it, 1)
                gate_up_high(FC // 2 - 1, 1)
                ff_silu(FC // 2 - 1, 0)
                for f in range(2):
                    down_high(f)
                ff_silu(FC // 2 - 1, 1)
                for f in range(2, FC):
                    down_high(f)
                own.settle()

        @block.vector
        def _(dve):
            own = Chain(dve, link_dve)
            dve.wait_ge(s_silu, 1)
            dve.tensor_copy(c_wide, c_silu.unsqueeze(2).broadcast_to([P, C8, P])).then_inc(s_cw, 1)
            dve.wait_ge(s_small, SMALL)
            own.link(dve.tensor_copy(pos, pos_i))

            def angles(cos, sin, blk, f0, n):
                for t in range(T):
                    own.mark(dve.tensor_scalar(sin[:, t], freqs[:, f0:f0 + n], pos[:, blk, t:t + 1], None, ALU.mult))
                own.settle()
                own.link(dve.tensor_scalar(cos, sin, 1 / (2 * np.pi), ROUND, ALU.mult, ALU.add))
                own.link(dve.tensor_scalar(cos, cos, -ROUND, None, ALU.add))
                for part in TWO_PI:
                    own.link(dve.scalar_tensor_tensor(sin, cos, -part, sin, ALU.mult, ALU.add))
                own.link(dve.tensor_scalar(sin, sin, 3.1415925, -3.1415925, ALU.min, ALU.max))
                own.link(dve.tensor_scalar(cos, sin, -1.0, None, ALU.mult))
                own.link(dve.tensor_tensor(cos, cos, sin, ALU.min))
                own.mark(dve.tensor_scalar(cos, cos, float(np.pi / 2), None, ALU.add))

            angles(trig[:, 0, 0], trig[:, 0, 1], 0, 0, 16)
            angles(trig[:, 1, 0], trig[:, 1, 1], 1, 0, 16)
            angles(trig64[:, 0], trig64[:, 1], 1, 16, 32)
            own.settle()
            dve.tensor_copy(ss_q[:, 0, 0:1], pos[:, 0, 0:1]).then_inc(s_angle, 1)
            ps = u1.read(dve, ("taps",))
            u1.free(dve.tensor_copy(conv_w, ps[:, 0:MC * 32].rearrange("p (m k) -> p m k", m=MC)[:, :, 0:TAPS]), ("taps",))
            dve.wait_ge(s_rstd, 1)
            for t in range(T):
                dve.tensor_scalar(H[:, t], X[:, t], rstd[:, t:t + 1], None, ALU.mult).then_inc(s_xhat, 1)

            def modulation(n, gain):
                ps = u1.read(dve, ("modT", n))
                pm = ps[:, 0:2 * C8].rearrange("p (v c) -> p v c", v=2)
                own.link(dve.tensor_tensor(mod[:, 2 * n:2 * n + 2], pm, b_ada[:, 3 * n:3 * n + 2], ALU.add))
                u1.free(dve.tensor_scalar(mod[:, 2 * n + 1], mod[:, 2 * n + 1], 1.0, None, ALU.add), ("modT", n))
                u1.evacuated(dve, ("modT", n))
                dve.tensor_tensor(mod[:, 2 * n + 1], mod[:, 2 * n + 1], gain, ALU.mult).then_inc(s_mod, 1)

            modulation(0, g_mix)
            dve.wait_ge(s_mod, 1)
            for c in range(1, C8, 2):
                ps = u1.read(dve, ("hT", c))
                u1.free(dve.tensor_scalar(HT[:, c], ps[:], mod[:, 1, c:c + 1], mod[:, 0, c:c + 1],
                                          ALU.mult, ALU.add), ("hT", c))
            for m in range(MC):
                u1.evacuated(dve, ("gate", m))
                ps = u1.read(dve, ("val", m))
                ins = dve.tensor_tensor(U[:, m, PAD:], ps[:], sig[:, m % 2], ALU.mult)
                u1.free(ins, ("val", m))

            dve.wait_ge(s_latr, 2)
            for t in range(T):
                dve.tensor_scalar(LATB[:, t, 0:QR], LATB[:, t, 0:QR], r_q[:, 0, t:t + 1], None, ALU.mult).then_inc(s_latn, 1)
                dve.tensor_scalar(LATB[:, t, QR:QR + KR], LATB[:, t, QR:QR + KR], r_q[:, 1, t:t + 1], None, ALU.mult).then_inc(s_latn, 1)
            for n in range(3):
                ps = u1.read(dve, ("latT", n))
                gain = qa_g[:, n:n + 1] if n < 2 else kva_g
                u1.free(dve.tensor_scalar(latT[:, n], ps[:], gain, None, ALU.mult), ("latT", n))

            def conv(m, k):
                if k == 0:
                    u1.evacuated(dve, ("val", m))
                    own.mark(dve.tensor_scalar(DW[:, m], U[:, m, 0:S], conv_w[:, m, 0:1], conv_b[:, m:m + 1], ALU.mult, ALU.add))
                    return
                own.settle()
                ins = dve.scalar_tensor_tensor(DW[:, m], U[:, m, k:k + S], conv_w[:, m, k:k + 1], DW[:, m], ALU.mult, ALU.add)
                if k < TAPS - 1:
                    own.mark(ins)
                else:
                    ins.then_inc(s_conv, 1)

            for k in range(TAPS):
                conv(0, k)
            for t in range(T):
                for half in range(2):
                    u1.evacuated(dve, ("kv", t, half))
                    u1.evacuated(dve, ("q", t, half))
                own.link(dve.tensor_copy(K[:, t, :, NOPE:], LATB[:, t, LAT - ROPE:].unsqueeze(1).broadcast_to([P, NH, ROPE])))
                for n, B in ((0, Q), (1, K)):
                    own.link(dve.tensor_tensor(sqs, B[:, t], B[:, t], ALU.mult))
                    own.link(dve.tensor_reduce(hss[:, n, t], sqs, AX, ALU.add))
            dve.tensor_scalar(hss, hss, 1.0 / QK, EPS, ALU.mult, ALU.add).then_inc(s_hss, 1)
            for j in (4, 5):
                ps = u1.read(dve, ("ada", j))
                g = gate_a[:, (j % 2) * 512:(j % 2 + 1) * 512]
                u1.free(dve.tensor_tensor(g, ps[:], g, ALU.add), ("ada", j))
            dve.wait_ge(s_hstd, 1)
            own.link(dve.reciprocal(hr, hr))
            for n, (B, g) in enumerate(((Q, qn_g), (K, kn_g))):
                for t in range(T):
                    own.mark(dve.tensor_tensor(B[:, t], B[:, t], hr[:, n, t].unsqueeze(2).broadcast_to([P, NH, QK]), ALU.mult))
                own.settle()
                for t in range(T):
                    own.mark(dve.tensor_tensor(B[:, t], B[:, t], g.unsqueeze(1).broadcast_to([P, NH, QK]), ALU.mult))
                own.settle()
                x1, x2 = B[:, :, :, NOPE:NOPE + 16], B[:, :, :, NOPE + 16:]
                cos, sin = (trig[:, 0, k].unsqueeze(2).broadcast_to([P, T, NH, 16]) for k in range(2))
                r = [rope_t[:, k].rearrange("p (t h d) -> p t h d", t=T, h=NH) for k in range(4)]
                dve.wait_ge(s_trig, 1)
                for k, (x, f) in enumerate(((x1, cos), (x2, sin), (x1, sin), (x2, cos))):
                    own.mark(dve.tensor_tensor(r[k], x, f, ALU.mult))
                own.settle()
                own.mark(dve.tensor_tensor(x1, r[0], r[1], ALU.subtract))
                dve.tensor_tensor(x2, r[2], r[3], ALU.add).then_inc(s_rot, 1)
            own.settle()
            for k in range(TAPS):
                conv(1, k)
            for j in (10, 11):
                ps = u1.read(dve, ("ada", j))
                g = gate_f[:, (j % 2) * 512:(j % 2 + 1) * 512]
                u1.free(dve.tensor_tensor(g, ps[:], g, ALU.add), ("ada", j))
            modulation(1, g_ffn)
            for h in range(NH):
                ps = u1.read(dve, ("kT", h))
                u1.free(dve.tensor_copy(KT[0:QK, h], ps[0:QK, :]), ("kT", h))

            def weighted(eng, n):
                t, h = divmod(n, NH)
                if h == NH - 1:
                    u1.read(eng, ("o", t))
                else:
                    eng.wait_ge(s_pv, t * (NH - 1) + h + 1)

            def row_max(n):
                t, h = divmod(n, NH)
                ps = u1.read(dve, ("s", t, h))
                own.link(dve.tensor_reduce(mx[:, t, h:h + 1], ps[:, 0:(t + 1) * P], AX, ALU.max))
                dve.tensor_scalar(nmx[:, t, h:h + 1], mx[:, t, h:h + 1], -(QK ** -0.5), None, ALU.mult).then_inc(s_negmax, 1)

            def take_pt(n):
                t, h = divmod(n, NH)
                if n >= 3:
                    weighted(dve, n - 3)
                ps = u1.read(dve, ("pT", t, h))
                u1.free(dve.tensor_copy(PT[:, n % 3, 0:(t + 1) * P], ps[:, 0:(t + 1) * P]), ("pT", t, h))

            def take_o(t):
                u1.evacuated(dve, ("s", t, NH - 1))
                own.link(dve.reciprocal(rl[:, t], lsum[:, t]))
                ps = u1.read(dve, ("o", t))
                u1.free(dve.tensor_tensor(O[:, t].rearrange("p (h d) -> p h d", d=VD), ps[:].rearrange("p (h d) -> p h d", d=VD),
                                          rl[:, t].unsqueeze(2).broadcast_to([P, NH, VD]), ALU.mult), ("o", t))

            for n in range(T * NH + 3):
                if n < T * NH:
                    row_max(n)
                for k in (2 * n, 2 * n + 1):
                    if k < 2 * TAPS:
                        conv(2 + k // TAPS, k % TAPS)
                if 2 <= n < T * NH + 2:
                    take_pt(n - 2)
                if n >= 4 and (n - 3) % NH == 0:
                    take_o((n - 3) // NH - 1)
            take_o(T - 1)
            ps = u1.read(dve, ("mean",))
            for m in range(MC):
                dve.scalar_tensor_tensor(DW[:, m], ps[:], -1.0 / CONV, DW[:, m], ALU.mult, ALU.add).then_inc(s_cent, 1)
            dve.wait_ge(s_cent, MC)
            u1.free(dve.memset(mx[:, 0, 0:1], 0.0), ("mean",))
            u1.evacuated(dve, ("var",))
            own.link(dve.reciprocal(stat[:, 1], stat[:, 0]))
            for m in range(MC):
                dve.tensor_tensor(DW[:, m], DW[:, m], stat[:, 1], ALU.mult).then_inc(s_cnorm, 1)
            for t in range(T):
                if t:
                    dve.wait_ge(s_x1, t)
                for half in range(2):
                    cs = slice(512 * half, 512 * half + 512)
                    ps = u1.read(dve, ("mix", t, half))
                    u1.free(dve.tensor_tensor(xtmp[:, half], ps[:], gate_a[:, cs], ALU.mult), ("mix", t, half))
                for half in range(2):
                    cs = slice(512 * half, 512 * half + 512)
                    u1.evacuated(dve, ("mix", t, half))
                    ins = dve.tensor_tensor(X[:, t, cs], X[:, t, cs], xtmp[:, half], ALU.add)
                    if half:
                        ins.then_inc(s_x1, 1)
                    else:
                        own.mark(ins)
                own.settle()
            dve.wait_ge(s_rstd2, 1)
            for t in range(T):
                dve.tensor_scalar(H[:, t], X[:, t], rstd[:, t:t + 1], None, ALU.mult).then_inc(s_xhat2, 1)
            for c in range(1, C8, 2):
                ps = u1.read(dve, ("h2T", c))
                u1.free(dve.tensor_scalar(HT[:, c], ps[:], mod[:, 3, c:c + 1], mod[:, 2, c:c + 1],
                                          ALU.mult, ALU.add), ("h2T", c))
            for t in range(T):
                ps = u1.read(dve, ("logit", t))
                u1.free(dve.tensor_tensor(L[:, t], ps[:, 0:NG + NE], b_route, ALU.add), ("logit", t))
            for t in range(T):
                u1.evacuated(dve, ("logit", t))
            u1.evacuated(dve, ("mix", T - 1, 1))
            dve.wait_ge(s_fill, 16)

            def wide(x, n):
                return x.unsqueeze(2).broadcast_to([P, T, n])

            def first_max(vals, n, top, onehot):
                own.link(dve.tensor_reduce(top, vals, AX, ALU.max))
                own.link(dve.tensor_tensor(onehot, vals, wide(top, n), ALU.is_equal))
                own.link(dve.tensor_tensor(onehot, onehot, ramp[:, 0:n].unsqueeze(1).broadcast_to([P, T, n]), ALU.mult))
                own.link(dve.tensor_reduce(ered[:, :, 7], onehot, AX, ALU.max))
                own.link(dve.tensor_tensor(onehot, onehot, wide(ered[:, :, 7], n), ALU.is_equal))

            GL, EL = L[:, :, 0:NG], L[:, :, NG:]
            first_max(GL, NG, ered[:, :, 0], gsel)
            dve.tensor_tensor(gexp, GL, wide(ered[:, :, 0], NG), ALU.subtract).then_inc(s_gdiff, 1)
            sel = gsel.unsqueeze(3).broadcast_to([P, T, NG, EPG])
            m4, e4, t4 = (x.rearrange("p t (g e) -> p t g e", g=NG) for x in (ML, EL, tmp32))
            own.mark(dve.tensor_tensor(m4, e4, sel, ALU.mult))
            own.mark(dve.tensor_copy(t4, sel))
            own.settle()
            own.link(dve.tensor_scalar(tmp32, tmp32, -NEG, NEG, ALU.mult, ALU.add))
            own.link(dve.tensor_tensor(ML, ML, tmp32, ALU.add))
            first_max(ML, NE, ered[:, :, 1], OH[0])
            own.link(dve.scalar_tensor_tensor(ML, OH[0], 2 * NEG, ML, ALU.mult, ALU.add))
            first_max(ML, NE, ered[:, :, 2], OH[1])
            dve.tensor_tensor(ered[:, :, 4], ered[:, :, 2], ered[:, :, 1], ALU.subtract).then_inc(s_ediff, 1)
            dve.tensor_tensor(MM, OH[0], OH[1], ALU.add).then_inc(s_masks, 1)
            dve.wait_ge(s_gexp, 1)
            own.link(dve.tensor_reduce(ered[:, :, 3], gexp, AX, ALU.add))
            own.link(dve.reciprocal(ered[:, :, 3], ered[:, :, 3]))
            dve.wait_ge(s_eexp, 1)
            own.link(dve.tensor_scalar(ered[:, :, 5], ered[:, :, 4], 1.0, None, ALU.add))
            own.link(dve.reciprocal(ered[:, :, 5], ered[:, :, 5]))
            own.link(dve.tensor_tensor(wts[:, :, 0], ered[:, :, 5], ered[:, :, 3], ALU.mult))
            own.mark(dve.tensor_tensor(wts[:, :, 1], wts[:, :, 0], ered[:, :, 4], ALU.mult))
            ps = u1.read(dve, ("rank",))
            own.mark(dve.tensor_copy(rank, ps[:, 0:T * NE].rearrange("p (t e) -> p t e", t=T)))
            own.settle()
            u1.free(dve.tensor_copy(cnt, ps[:, T * NE:T * NE + NE]), ("rank",))
            u1.evacuated(dve, ("rank",))
            own.link(dve.tensor_copy(pre[0], cnt))
            k = 0
            for d in (1, 2, 4, 8, 16):
                own.mark(dve.tensor_copy(pre[1 - k][:, 0:d], pre[k][:, 0:d]))
                own.mark(dve.tensor_tensor(pre[1 - k][:, d:], pre[k][:, d:], pre[k][:, 0:NE - d], ALU.add))
                own.settle()
                k = 1 - k
            own.link(dve.tensor_tensor(off_e, pre[k], cnt, ALU.subtract))
            for w, start in enumerate((off_e, slot0)):
                own.link(dve.tensor_tensor(tmp32, rank, start.unsqueeze(1).broadcast_to([P, T, NE]), ALU.add))
                for k in range(2):
                    own.link(dve.tensor_tensor(ML, tmp32, OH[k], ALU.mult))
                    own.link(dve.tensor_reduce(dest_f[:, w, :, k], ML, AX, ALU.add))
            dve.tensor_copy(dest, dest_f).then_inc(s_dest, 1)
            for r in range(ROUNDS):
                own.mark(dve.tensor_scalar(win_f[:, r], off_e, float(r * P), float(2 * S), ALU.add, ALU.min))
                own.mark(dve.tensor_scalar(tmp32[:, r], cnt, float(r * P), None, ALU.is_gt))
            own.settle()
            own.mark(dve.tensor_copy(win[:, 0:T * NE], win_f.rearrange("p t e -> p (t e)")))
            own.mark(dve.memset(win[:, T * NE:], 0))
            own.link(dve.tensor_reduce(rounds_f, tmp32, AX, ALU.max))
            own.link(dve.tensor_reduce(ered[:, 0, 6:7], rounds_f, AX, ALU.add))
            dve.tensor_copy(rounds[:, 0:1], ered[:, 0, 6:7]).then_inc(s_rounds, 1)
            ps = u1.read(dve, ("slots",))
            u1.free(dve.tensor_copy(slots_i, ps[:, 0:P]), ("slots",))
            for g in range(2):
                for c in range(1, C8, 2):
                    ps = u1.read(dve, ("xsT", g, c))
                    u1.free(dve.tensor_scalar(XsT[:, c, g * S:(g + 1) * S], ps[:], mod[:, 3, c:c + 1], mod[:, 2, c:c + 1],
                                              ALU.mult, ALU.add), ("xsT", g, c))
            dve.sem_inc(m_a, CREDIT)
            dve.sem_inc(m_ya, CREDIT)
            dve.sem_inc(m_xw, CREDIT)
            u1.all_evacuated(dve, [("xsT", g, c) for g in range(2) for c in range(C8)])
            dve.wait_ge(s_pad, 1)

            def window(e, s):
                w0 = dve.value_load(win[0:1, bass.ds(e, 1)], min_val=0, max_val=2 * S)
                dve.tensor_copy(XW[s % 2], XsT[:, :, bass.ds(w0, P)]).then_inc(m_xw, 1)

            def product(n, s):
                dve.wait_ge(m_silu, n + 1 + CREDIT)
                dve.wait_ge(m_at, n - 2 + 1 + CREDIT)
                dve.tensor_tensor(A[:, s % 2], SG[:, s % 2], bank[s % 2][:, FE:], ALU.mult).then_inc(m_a, 1)
                window(n + 2, s)

            def copy_ya(n, it, s):
                dve.wait_ge(m_y, n + 1 + CREDIT)
                dve.wait_ge(m_st[s], SCATTERED + 16 * it)
                dve.tensor_copy(Y[:, s, 0:512], bank[4 + 2 * (s % 2)][:]).then_inc(m_ya, 1)

            n_rounds = dve.value_load(rounds[0:1, 0:1], min_val=1, max_val=ROUNDS)
            window(0, 0)
            window(1, 1)
            with dve.Fori(0, n_rounds) as r:
                with dve.Fori(0, NE // 4) as it:
                    n = r * NE + it * 4
                    for s in range(4):
                        product(n + s, s)
                        if s:
                            copy_ya(n + s - 1, r * (NE // 4) + it, s - 1)
                    copy_ya(n + 3, r * (NE // 4) + it, 3)
            own.settle()
            def stats(t):
                for half in range(2):
                    own.mark(dve.bn_stats(bst[:, t, half], X[:, t, 512 * half:512 * half + 512]))
                own.settle()
                return dve.bn_aggr(bag[:, t], bst[:, t])

            def normalise(t, gain, shift, rstd_ready):
                own.link(dve.scalar_tensor_tensor(X[:, t], X[:, t], bag[:, t, 0:1], gain, ALU.subtract, ALU.mult))
                rstd_ready()
                return dve.scalar_tensor_tensor(X[:, t], X[:, t], lrs[:, t:t + 1], shift, ALU.mult, ALU.add)

            for t in range(T):
                dve.wait_ge(s_yin[t], 16)
                dve.wait_ge(s_w1, t + 1)
                own.link(dve.scalar_tensor_tensor(Yin[:, t, 0], Yin[:, t, 0], wts[:, t, 0:1], Yin[:, t, 1], ALU.mult, ALU.add))
                own.link(dve.tensor_tensor(Yin[:, t, 0], Yin[:, t, 0], gate_f, ALU.mult))
                own.link(dve.tensor_tensor(X[:, t], X[:, t], Yin[:, t, 0], ALU.add))
                stats(t).then_inc(s_mean, 1)
                dve.wait_ge(s_mean, t + 1)
                dve.wait_ge(s_lnin, 32)
                normalise(t, lnin_g, lnin_b, lambda: dve.wait_ge(s_lnr, t + 1)).then_inc(layer_in, 1)
            dve.sem_inc(f_a, CREDIT)
            dve.sem_inc(f_lo, CREDIT)

            own.settle()
            with dve.Fori(0, LAYERS) as l:
                own.restart()
                dve.wait_ge(d_sm, 48 * (l + 1))
                own.mark(dve.tensor_scalar(nsinks, sinks, -1.0, None, ALU.mult))
                own.settle()

                def rotate(src, dst, cos, sin, heads, half, copies=1):
                    r = [rt[:, k, 0:T * heads * half].rearrange("p (t h d) -> p t h d", t=T, h=heads) for k in range(4)]
                    c, s_ = (x.unsqueeze(2).broadcast_to([P, T, heads, half]) for x in (cos, sin))
                    x1, x2 = src[:, :, :, 0:half], src[:, :, :, half:2 * half]
                    for k, (x, f) in enumerate(((x1, c), (x2, s_), (x2, c), (x1, s_))):
                        own.mark(dve.tensor_tensor(r[k], x, f, ALU.mult))
                    own.settle()
                    for n in range(copies):
                        for k, op, lo in ((0, ALU.subtract, 0), (2, ALU.add, half)):
                            ins = dve.tensor_tensor(dst[n][:, :, :, lo:lo + half], r[k], r[k + 1], op)
                            if n < copies - 1 or lo == 0:
                                own.mark(ins)
                    y_rot.inc(ins)
                    own.settle()

                def heads_of(a, n, d):
                    return PJ[:, :, a:a + n * d].rearrange("p t (h d) -> p t h d", d=d)

                c16, s16, c32, s32 = trig[:, 1, 0], trig[:, 1, 1], trig64[:, 0], trig64[:, 1]
                for t in range(T):
                    u2.evacuated(dve, ("in", t, 0), l)
                for t in range(T):
                    own.mark(dve.bn_stats(bst[:, t, 0], PJ[:, t, KI:KI + IXD]))
                own.settle()
                for t in range(T):
                    ins = dve.bn_aggr(bag[:, t], bst[:, t, 0:1])
                    if t < T - 1:
                        own.mark(ins)
                y_kst.inc(ins)
                own.settle()
                y_kst.wait(dve, l, 1)
                own.mark(dve.tensor_scalar(wi, PJ[:, :, WI:WI + IXH], float(IXH ** -0.5 * IXD ** -0.5), None, ALU.mult))
                qi = heads_of(QI, IXH, IXD)
                rotate(qi, [qi], c16, s16, IXH, 16)
                y_rot.wait(dve, l, 1)
                y_krs.wait(dve, l, 1)
                for t in range(T):
                    own.mark(dve.tensor_scalar(PJ[:, t, KI:KI + IXD], PJ[:, t, KI:KI + IXD], bag[:, t, 0:1], lrs[:, t:t + 1], ALU.subtract, ALU.mult))
                own.settle()
                for p, op in ((ix_g, ALU.mult), (ix_b, ALU.add)):
                    own.link(dve.tensor_tensor(PJ[:, :, KI:KI + IXD], PJ[:, :, KI:KI + IXD], p.unsqueeze(1).broadcast_to([P, T, IXD]), op))
                rotate(heads_of(KI, 1, IXD), [KID[:, :, n:n + 1] for n in range(4)], c16, s16, 1, 16, copies=4)
                n = 0
                for t in range(1, T):
                    w = (t + 1) * P
                    for h in range(IXH):
                        u2.evacuated(dve, ("ix", t, h), l)
                        acc = IX[:, t - 1, 0:w]
                        if h == 0:
                            ins = dve.tensor_scalar(acc, R[:, n % 2, 0:w], wi[:, t, h:h + 1], None, ALU.mult)
                        else:
                            y_ix.wait(dve, l, n)
                            ins = dve.scalar_tensor_tensor(acc, R[:, n % 2, 0:w], wi[:, t, h:h + 1], acc, ALU.mult, ALU.add)
                        y_ix.inc(ins)
                        n += 1
                    y_ix.wait(dve, l, n)
                    own.mark(dve.tensor_tensor(IX[:, t - 1, t * P:w], IX[:, t - 1, t * P:w], own_mask, ALU.add))
                own.settle()

                def pick(n):
                    t, k = divmod(n, PICKS)
                    sc = IX[:, t, 0:(t + 2) * P]
                    own.link(dve.max(top8, sc))
                    own.link(dve.match_replace(sc, top8, sc, TAKEN))
                    if k == PICKS - 1:
                        own.link(dve.tensor_scalar(sc, sc, TAKEN, -NEG, ALU.is_equal, ALU.mult))
                        y_sel.inc(dve.tensor_scalar(SELM[:, t, 0:(t + 2) * P], sc, NEG, None, ALU.add))

                y_rot.wait(dve, l, 2)
                qa, qb = heads_of(QA, 8, HD), heads_of(QB, 8, HD)
                rotate(qa, [qa], c32, s32, 8, 32)
                for n in range(PICKS_A):
                    pick(n)
                u2.all_evacuated(dve, [("in", t, 3) for t in range(T)], l)
                y_rot.wait(dve, l, 3)
                rotate(qb, [qb], c32, s32, 8, 32)
                for n in range(PICKS_A, PICKS_B):
                    pick(n)
                u2.all_evacuated(dve, [("in", t, 2) for t in range(T)], l)
                y_rot.wait(dve, l, 4)
                rotate(heads_of(KA, 2, HD), [KD[:, :, :, n] for n in range(2)], c32, s32, 2, 32, copies=2)
                for n in range(PICKS_B, PICKS_C):
                    pick(n)

                def row_max(n):
                    kind, t, h = UNITS[n]
                    kk = 0 if kind == "a" else 1
                    ps = u2.read(dve, ("s", kind, t, h), l)
                    own.link(dve.tensor_reduce(mx2[:, kk, t, h:h + 1], ps[:, 0:width(n)], AX, ALU.max))
                    if kind == "a":
                        ins = dve.tensor_scalar(nmx2[:, kk, t, h:h + 1], mx2[:, kk, t, h:h + 1], -(HD ** -0.5), nsinks[:, h:h + 1],
                                                ALU.mult, ALU.min)
                    else:
                        ins = dve.tensor_scalar(nmx2[:, kk, t, h:h + 1], mx2[:, kk, t, h:h + 1], -(HD ** -0.5), None, ALU.mult)
                    y_neg.inc(ins)
                    if kind == "a" and h == 7:
                        y_neg.wait(dve, l, n + 1)
                        y_sinkd.inc(dve.tensor_tensor(es2[:, t], nmx2[:, 0, t], sinks, ALU.add))

                def take_o(kind, t):
                    kk = 0 if kind == "a" else 1
                    u2.evacuated(dve, ("s", kind, t, 7), l)
                    if kind == "a":
                        y_sinke.wait(dve, l, WINDOWED.index(t) + 1)
                        own.link(dve.tensor_tensor(ls2[:, 0, t], ls2[:, 0, t], es2[:, t], ALU.add))
                    own.link(dve.reciprocal(rl2[:, kk, t], ls2[:, kk, t]))
                    ps = u2.read(dve, ("o", kind, t), l)
                    u2.free(dve.tensor_tensor(O2[:, kk, t].rearrange("p (h d) -> p h d", d=HD), ps[:].rearrange("p (h d) -> p h d", d=HD),
                                              rl2[:, kk, t].unsqueeze(2).broadcast_to([P, 8, HD]), ALU.mult), ("o", kind, t))

                for n in range(len(UNITS) + 3):
                    if n < len(UNITS):
                        row_max(n)
                    if n == 5:
                        u2.all_evacuated(dve, [("in", t, 4) for t in range(T)], l)
                        y_rot.wait(dve, l, 5)
                        rotate(heads_of(KB, 1, HD), [KBD[:, :, n:n + 1] for n in range(2)], c32, s32, 1, 32, copies=2)
                    if n in PICK_AT:
                        pick(PICKS_C + PICK_AT.index(n))
                    if n >= 4 and (n - 3) % 8 == 0:
                        take_o(*UNITS[n - 4][:2])
                take_o(*UNITS[-1][:2])

                def split_x1(t):
                    for half in range(2):
                        ps = u2.read(dve, ("x1T", t, half), l)
                        y_xhi.wait(dve, l, 2 * t + half + 1)
                        place = (slice(None), slice(4 * half, 4 * half + 4), slice(t * P, (t + 1) * P))
                        u2.free(dve.tensor_tensor(HT_lo[place], ps[:].rearrange("p (c m) -> p c m", c=4), HT_hi[place].bitcast(F32), ALU.subtract),
                                ("x1T", t, half))

                def gate_up_low(it, s):
                    dve.wait_ge(f_hi, l * FC + it * 2 + s + 1 + CREDIT)
                    dve.tensor_tensor(gu_lo[s], gu[s], gu_hi[s].bitcast(F32), ALU.subtract).then_inc(f_lo, 1)

                def ff_product(it, s):
                    n = l * FC + it * 2 + s
                    dve.wait_ge(f_s, n + 1 + CREDIT)
                    dst = aT[:, bass.ds(it * 2 + s, 1)].rearrange("p a n -> p (a n)")
                    dve.tensor_tensor(dst, SF[:, s], bank[2 * s + 1][:], ALU.mult).then_inc(f_a, 1)

                def down_low(f):
                    y_dhi.wait(dve, l, f + 1)
                    dve.tensor_tensor(dn_lo[f % 2], w_dn[:, f % DN_SLOTS], dn_hi[f % 2].bitcast(F32), ALU.subtract)
                    y_dlo.inc(dve.tensor_tensor(a_lo[f % 2], aT[:, f], a_hi[f % 2].bitcast(F32), ALU.subtract))

                dve.wait_ge(d_ln1, 32 * (l + 1))
                for t in range(T):
                    for half in range(2):
                        cs = slice(512 * half, 512 * half + 512)
                        ps = u2.read(dve, ("mix", t, half), l)
                        u2.free(dve.scalar_tensor_tensor(X[:, t, cs], X[:, t, cs], ALPHA, ps[:], ALU.mult, ALU.add), ("mix", t, half))
                    u2.all_evacuated(dve, [("mix", t, half) for half in range(2)], l)
                    y_mst.inc(stats(t))
                    y_mst.wait(dve, l, t + 1)
                    y_x1.inc(normalise(t, lnG, lnB, lambda: y_mrs.wait(dve, l, t + 1)))
                    if t:
                        split_x1(t - 1)
                    if t == T - 2:
                        for c in range(C8):
                            y_ghi.wait(dve, l, c + 1)
                            y_glo.inc(dve.tensor_tensor(pg_lo[:, c], w_pg[:, c], pg_hi[:, c].bitcast(F32), ALU.subtract))
                split_x1(T - 1)
                gate_up_low(0, 0)
                n = 0
                for t in range(T):
                    for half in range(2):
                        u2.evacuated(dve, ("pg", t, half), l)
                        cs = slice(512 * half, 512 * half + 512)
                        y_ple.inc(dve.tensor_tensor(PLB[:, t, cs], PLB[:, t, cs], SF[:, n % 2], ALU.mult))
                        n += 1
                y_ple.wait(dve, l, n)
                for t in range(T):
                    own.mark(dve.scalar_tensor_tensor(X[:, t], X[:, t], ALPHA, PLB[:, t], ALU.mult, ALU.add))
                own.settle()
                with dve.Fori(0, FC // 2 - 1) as it:
                    gate_up_low(it, 1)
                    ff_product(it, 0)
                    gate_up_low(it + 1, 0)
                    ff_product(it, 1)
                gate_up_low(FC // 2 - 1, 1)
                ff_product(FC // 2 - 1, 0)
                for f in range(2):
                    down_low(f)
                ff_product(FC // 2 - 1, 1)
                for f in range(2, FC):
                    down_low(f)
                y_dlo.wait(dve, l, FC)
                dve.sem_inc(a_free, 1)
                own.settle()
                dve.wait_ge(d_ln2, 32 * (l + 1))
                for t in range(T):
                    for half in range(2):
                        cs = slice(512 * half, 512 * half + 512)
                        ps = u2.read(dve, ("dn", t, half), l)
                        u2.free(dve.tensor_tensor(X[:, t, cs], X[:, t, cs], ps[:], ALU.add), ("dn", t, half))
                    u2.all_evacuated(dve, [("dn", t, half) for half in range(2)], l)
                    y_est.inc(stats(t))
                    y_est.wait(dve, l, t + 1)
                    normalise(t, lnG, lnB, lambda: y_ers.wait(dve, l, t + 1)).then_inc(layer_in, 1)

        @block.tensor
        def _(pe):
            def ada(j):
                ps = u1.begin(pe, ("ada", j))
                pe.wait_ge(s_ada[j % 2], 16 * (j // 2 + 1))
                for c in range(C8):
                    ins = pe.matmul(ps[:], c_wide[:, c], ada_w[j % 2][:, c], start=c == 0, stop=c == C8 - 1)
                u1.full(ins, ("ada", j))

            def mod_cols(n, row):
                for j in range(4):
                    u1.evacuated(pe, ("ada", 6 * n + j))
                ps = u1.begin(pe, ("modT", n))
                for v in range(2):
                    for c in range(C8):
                        ins = pe.matmul(ps[:, v * C8 + c:v * C8 + c + 1], row[0:1, v * D + c:v * D + D:C8],
                                        ones[0:1, 0:1], start=True, stop=True)
                u1.full(ins, ("modT", n))

            def turn(key, pieces):
                ps = u1.begin(pe, key)
                for n, x in enumerate(pieces):
                    ins = pe.transpose(ps[0:x.shape[-1], n * P:(n + 1) * P], x, ident)
                u1.full(ins, key)

            pe.wait_ge(s_const, 1)
            pe.wait_ge(s_cw, 1)
            for j in range(4):
                ada(j)
            pe.wait_ge(s_small, SMALL)
            ps = u1.begin(pe, ("taps",))
            for m in range(MC):
                ins = pe.transpose(ps[:, m * 32:m * 32 + TAPS], tap_rows[0:TAPS, m * P:(m + 1) * P], ident[0:TAPS, 0:TAPS])
            u1.full(ins, ("taps",))
            mod_cols(0, mod_row0)
            pe.wait_ge(s_xhat, T)
            for c in range(C8):
                turn(("hT", c), [H[:, t, c::C8] for t in range(T)])
            for c in range(C8):
                u1.evacuated(pe, ("hT", c))
            pe.wait_ge(s_win, 16)
            for m in range(MC):
                for kind, c0 in (("val", 0), ("gate", CONV)):
                    ps = u1.begin(pe, (kind, m))
                    for c in range(C8):
                        ins = pe.matmul(ps[:], w_in[:, c, c0 + m * P:c0 + (m + 1) * P], HT[:, c], start=c == 0, stop=c == C8 - 1)
                    u1.full(ins, (kind, m))
            for t in range(T):
                ps = u1.begin(pe, ("lat", t))
                for c in range(C8):
                    ins = pe.matmul(ps[:, 0:LAT], HT[:, c, t * P:(t + 1) * P], w_in[:, c, 2 * CONV:], start=c == 0, stop=c == C8 - 1)
                u1.full(ins, ("lat", t))
            pe.wait_ge(s_latn, 2 * T)
            for n in range(3):
                turn(("latT", n), [LATB[:, t, n * P:(n + 1) * P] for t in range(T)])
            for n in range(3):
                u1.evacuated(pe, ("latT", n))
            pe.wait_ge(s_wq, 32)
            for t in range(T):
                ts = slice(t * P, (t + 1) * P)
                for half in range(2):
                    ps = u1.begin(pe, ("q", t, half))
                    for c in range(2):
                        ins = pe.matmul(ps[:, 0:384], latT[:, c, ts], w_q[:, c, 384 * half:384 * half + 384], start=c == 0, stop=c == 1)
                    u1.full(ins, ("q", t, half))
                    ps = u1.begin(pe, ("kv", t, half))
                    u1.full(pe.matmul(ps[:], latT[:, 2, ts], w_kv[:, 512 * half:512 * half + 512], start=True, stop=True), ("kv", t, half))
            for j in range(4, 12):
                ada(j)
            mod_cols(1, mod_row1)
            for h in range(NH):
                pe.wait_ge(s_rot, 2)
                turn(("qT", h), [Q[:, t, h] for t in range(T)])
                turn(("kT", h), [K[:, t, h] for t in range(T)])

            def scores(n):
                t, h = divmod(n, NH)
                u1.evacuated(pe, ("qT", h))
                u1.evacuated(pe, ("kT", h))
                w = (t + 1) * P
                ps = u1.begin(pe, ("s", t, h))
                pe.matmul(ps[:, 0:w], QT[0:QK, h, t * P:w], KT[0:QK, h, 0:w], start=True, stop=False)
                u1.full(pe.matmul(ps[:, t * P:w], ident_b, chunk_mask, start=False, stop=True), ("s", t, h))

            def turn_p(n):
                t, h = divmod(n, NH)
                u1.evacuated(pe, ("s", t, h))
                turn(("pT", t, h), [Pr[:, n % 3, k * P:(k + 1) * P] for k in range(t + 1)])

            def values(n):
                t, h = divmod(n, NH)
                u1.evacuated(pe, ("pT", t, h))
                ps = u1.begin(pe, ("o", t)) if h == 0 else bank[u1.b.where[("o", t)][0]]
                for k in range(t + 1):
                    ins = pe.matmul(ps[:, h * VD:(h + 1) * VD], PT[:, n % 3, k * P:(k + 1) * P], V[:, k, h * VD:(h + 1) * VD],
                                    start=k == 0, stop=k == t)
                if h == NH - 1:
                    u1.full(ins, ("o", t))
                else:
                    ins.then_inc(s_pv, 1)

            for n in range(T * NH + 3):
                if n < T * NH:
                    scores(n)
                if 2 <= n < T * NH + 2:
                    turn_p(n - 2)
                if n >= 3:
                    values(n - 3)
            for j in range(4):
                for t in range(T):
                    u1.evacuated(pe, ("o", t))
                turn(("oT", j), [O[:, t, j * P:(j + 1) * P] for t in range(T)])
            ps = u1.begin(pe, ("mean",))
            pe.wait_ge(s_conv, MC)
            for m in range(MC):
                ins = pe.matmul(ps[:], ones, DW[:, m], start=m == 0, stop=m == MC - 1)
            u1.full(ins, ("mean",))
            ps = u1.begin(pe, ("var",))
            for m in range(MC):
                pe.wait_ge(s_csq, m + 1)
                ins = pe.matmul(ps[:], ones, stat[:, m % 2], start=m == 0, stop=m == MC - 1)
                if m < MC - 1:
                    ins.then_inc(s_csum, 1)
            u1.full(ins, ("var",))
            pe.wait_ge(s_wout, 64)
            pe.wait_ge(s_yconv, MC)
            for j in range(4):
                u1.evacuated(pe, ("oT", j))
            for t in range(T):
                for half in range(2):
                    ps = u1.begin(pe, ("mix", t, half))
                    for m in range(C8):
                        ins = pe.matmul(ps[:], mixT[:, m, t * P:(t + 1) * P], w_out[:, m, 512 * half:512 * half + 512],
                                        start=m == 0, stop=m == C8 - 1)
                    u1.full(ins, ("mix", t, half))

            pe.wait_ge(s_xhat2, T)
            for c in range(C8):
                turn(("h2T", c), [H[:, t, c::C8] for t in range(T)])
            for c in range(C8):
                u1.evacuated(pe, ("h2T", c))
            for t in range(T):
                ps = u1.begin(pe, ("logit", t))
                for c in range(C8):
                    ins = pe.matmul(ps[:, 0:NG + NE], HT[:, c, t * P:(t + 1) * P], w_route[:, c], start=c == 0, stop=c == C8 - 1)
                u1.full(ins, ("logit", t))
            pe.wait_ge(s_masks, 1)
            ps = u1.begin(pe, ("rank",))
            for t in range(T):
                for k in range(t):
                    pe.matmul(ps[:, t * NE:(t + 1) * NE], ones, MM[:, k], start=k == 0, stop=False)
                pe.matmul(ps[:, t * NE:(t + 1) * NE], before_me, MM[:, t], start=t == 0, stop=True)
            for t in range(T):
                ins = pe.matmul(ps[:, T * NE:T * NE + NE], ones, MM[:, t], start=t == 0, stop=t == T - 1)
            u1.full(ins, ("rank",))
            pe.wait_ge(s_slotin, 16)
            turn(("slots",), [slots_f])
            for g in range(2):
                pe.wait_ge(s_stage[g], 16 * T)
                for c in range(C8):
                    turn(("xsT", g, c), [stage[g][:, q, c::C8] for q in range(T)])
            for x in (m_gu, m_at, m_y):
                pe.sem_inc(x, CREDIT)
            for g in range(2):
                for c in range(C8):
                    u1.evacuated(pe, ("xsT", g, c))

            def gate_up(n, it, s):
                pe.wait_ge(m_xw, n + 1 + CREDIT)
                pe.wait_ge(s_w[s], 48 * (it + 1))
                pe.wait_ge(m_a, n - 2 + 1 + CREDIT)
                for c in range(C8):
                    ins = pe.matmul(bank[s % 2][:], XW[s % 2][:, c], ring[s][:, c], start=c == 0, stop=c == C8 - 1)
                ins.then_inc(m_gu, 1)

            def turn_a(n, s):
                pe.wait_ge(m_a, n + 1 + CREDIT)
                pe.wait_ge(m_atc, n - 2 + 1 + CREDIT)
                for c in range(2):
                    ins = pe.transpose(bank[2 + s % 2][:, c * P:(c + 1) * P], A[:, s % 2, c::2], ident)
                ins.then_inc(m_at, 1)

            def down(n, s):
                pe.wait_ge(m_atc, n + 1 + CREDIT)
                pe.wait_ge(m_ya, n - 2 + 1 + CREDIT)
                pe.wait_ge(m_yb, n - 2 + 1 + CREDIT)
                for half in range(2):
                    for c in range(2):
                        ins = pe.matmul(bank[4 + 2 * (s % 2) + half][:], AT[:, s % 2, c], ring_d[s][:, c, 512 * half:512 * half + 512],
                                        start=c == 0, stop=c == 1)
                ins.then_inc(m_y, 1)

            pe.wait_ge(s_rounds, 1)
            n_rounds = pe.value_load(rounds[0:1, 0:1], min_val=1, max_val=ROUNDS)
            with pe.Fori(0, n_rounds) as r:
                with pe.Fori(0, NE // 4) as it:
                    n = r * NE + it * 4
                    for s in range(4):
                        gate_up(n + s, r * (NE // 4) + it, s)
                        if s:
                            down(n + s - 1, s - 1)
                        turn_a(n + s, s)
                    down(n + 3, 3)
            pe.wait_ge(m_y, n_rounds * NE + CREDIT)
            pe.sem_inc(b_free, 1)
            pe.sem_inc(a_free, 1)
            pe.sem_inc(f_g, CREDIT)

            with pe.Fori(0, LAYERS) as l:
                def turn2(key, pieces):
                    ps = u2.begin(pe, key, l)
                    for n, x in enumerate(pieces):
                        ins = pe.transpose(ps[0:x.shape[-1], n * P:(n + 1) * P], x, ident)
                    u2.full(ins, key)

                def tile(kind, t):
                    for half in range(2):
                        turn2((kind, t, half), [X[:, t, c::C8] for c in range(4 * half, 4 * half + 4)])

                def project(t, j):
                    a, b = IN_CUTS[j]
                    pe.wait_ge(d_in2[j], 16 * (l + 1))
                    ps = u2.begin(pe, ("in", t, j), l)
                    for c in range(C8):
                        ins = pe.matmul(ps[:, 0:b - a], HT[:, c, t * P:(t + 1) * P], w_in2[j][:, c], start=c == 0, stop=c == C8 - 1)
                    u2.full(ins, ("in", t, j))

                for t in range(T):
                    pe.wait_ge(layer_in, l * T + t + 1)
                    tile("xT", t)
                    u2.all_evacuated(pe, [("xT", t, half) for half in range(2)], l)
                    project(t, 0)
                    project(t, 1)
                source = {"qi": (1, lambda t, j: PJ[:, t, QI + j * P:QI + (j + 1) * P]),
                          "ki": (2, lambda t, j: KID[:, t].rearrange("p a b -> p (a b)")),
                          "ka": (5, lambda t, j: KD[:, t, j].rearrange("p a b -> p (a b)")),
                          "qa": (3, lambda t, j: PJ[:, t, QA + j * P:QA + (j + 1) * P]),
                          "kb": (6, lambda t, j: KBD[:, t].rearrange("p a b -> p (a b)")),
                          "qb": (4, lambda t, j: PJ[:, t, QB + j * P:QB + (j + 1) * P])}
                def turn_heads(keys):
                    for kind, j in keys:
                        order, piece = source[kind]
                        y_rot.wait(pe, l, order)
                        turn2((kind, j), [piece(t, j) for t in range(T)])

                turn_heads(TURNED[:3])
                u2.all_evacuated(pe, TURNED[:3], l)
                for t in range(1, T):
                    for h in range(IXH):
                        w = (t + 1) * P
                        p0 = IXD * (h % 4)
                        ps = u2.begin(pe, ("ix", t, h), l)
                        u2.full(pe.matmul(ps[:, 0:w], turned["qi", h // 4][p0:p0 + IXD, t * P:w], turned["ki", 0][p0:p0 + IXD, 0:w],
                                          start=True, stop=True), ("ix", t, h))
                for j in (3, 2):
                    for t in range(T):
                        project(t, j)
                turn_heads(TURNED[3:7])
                project(0, 4)
                turn_heads(TURNED[7:9])
                project(1, 4)
                u2.all_evacuated(pe, TURNED[3:9], l)

                def scores(n):
                    kind, t, h = UNITS[n]
                    w = width(n)
                    k0 = (t + 1) * P - w
                    p0 = HD * (h % 2)
                    keys = turned["ka", h // 4] if kind == "a" else turned["kb", 0]
                    if kind == "b" and t and h == 0:
                        y_sel.wait(pe, l, t)
                    if kind == "b" and t == 1 and h % 2 == 0:
                        u2.evacuated(pe, ("qb", h // 2), l)
                    ps = u2.begin(pe, ("s", kind, t, h), l)
                    pe.matmul(ps[:, 0:w], turned["q" + kind, h // 2][p0:p0 + HD, t * P:(t + 1) * P], keys[p0:p0 + HD, k0:k0 + w],
                              start=True, stop=False)
                    if kind == "b" and t:
                        ins = pe.matmul(ps[:, 0:w], ident_b, SELM[:, t - 1, 0:w], start=False, stop=True)
                    else:
                        if t:
                            pe.matmul(ps[:, 0:P], ident_b, prev_mask, start=False, stop=False)
                        ins = pe.matmul(ps[:, w - P:w], ident_b, own_mask, start=False, stop=True)
                    u2.full(ins, ("s", kind, t, h))

                def turn_p(n):
                    key = UNITS[n]
                    u2.evacuated(pe, ("s",) + key, l)
                    turn2(("pT",) + key, [Pr2[:, n % 4, k * P:(k + 1) * P] for k in range(width(n) // P)])

                def values(n):
                    kind, t, h = UNITS[n]
                    nk = width(n) // P
                    u2.evacuated(pe, ("pT", kind, t, h), l)
                    ps = u2.begin(pe, ("o", kind, t), l) if h == 0 else bank[b2.where[("o", kind, t)][0]]
                    for k in range(nk):
                        kt = t + 1 - nk + k
                        v = PJ[:, kt, VA + HD * (h // 4):VA + HD * (h // 4) + HD] if kind == "a" else PJ[:, kt, VB:VB + HD]
                        ins = pe.matmul(ps[:, h * HD:(h + 1) * HD], PT2[:, n % 3, k * P:(k + 1) * P], v, start=k == 0, stop=k == nk - 1)
                    if h == 7:
                        u2.full(ins, ("o", kind, t))
                    else:
                        y_pv.inc(ins)

                for n in range(len(UNITS) + 4):
                    if n < len(UNITS):
                        scores(n)
                    if n < T - 2:
                        project(n + 2, 4)
                    if 3 <= n < len(UNITS) + 3:
                        turn_p(n - 3)
                    if n >= 4:
                        values(n - 4)
                    if n in TURN_AT:
                        turn_heads([TURNED[TURN_AT[n]]])
                for j in range(C8):
                    if j % 4 == 0:
                        u2.all_evacuated(pe, [("o", "ab"[j // 4], t) for t in range(T)], l)
                    turn2(("oT", j), [O2[:, j // 4, t, (j % 4) * P:(j % 4 + 1) * P] for t in range(T)])
                for j in range(C8):
                    u2.evacuated(pe, ("oT", j), l)
                pe.wait_ge(d_o2, 16 * (l + 1))
                for t in range(T):
                    for half in range(2):
                        ps = u2.begin(pe, ("mix", t, half), l)
                        for m in range(C8):
                            ins = pe.matmul(ps[:], HT[:, m, t * P:(t + 1) * P], w_o2[:, m, 512 * half:512 * half + 512], start=m == 0, stop=m == C8 - 1)
                        u2.full(ins, ("mix", t, half))
                    if t:
                        y_x1.wait(pe, l, t)
                        tile("x1T", t - 1)
                pe.wait_ge(d_pp, 32 * (l + 1))
                for c in range(2):
                    turn2(("plT", c), [p_in[:, t, c * P:(c + 1) * P] for t in range(T)])
                u2.all_evacuated(pe, [("plT", c) for c in range(2)], l)
                for t in range(T):
                    for half in range(2):
                        ps = u2.begin(pe, ("pp", t, half), l)
                        for c in range(2):
                            ins = pe.matmul(ps[:], pT[:, c, t * P:(t + 1) * P], w_pp[:, c, 512 * half:512 * half + 512], start=c == 0, stop=c == 1)
                        u2.full(ins, ("pp", t, half))
                y_x1.wait(pe, l, T)
                tile("x1T", T - 1)
                y_glo.wait(pe, l, C8)
                u2.all_evacuated(pe, [("x1T", t, half) for t in range(T) for half in range(2)], l)
                for t in range(T):
                    for half in range(2):
                        ps = u2.begin(pe, ("pg", t, half), l)
                        for c in range(C8):
                            ts, cs = slice(t * P, (t + 1) * P), slice(512 * half, 512 * half + 512)
                            ins = split_product(pe, ps[:], (HT_hi[:, c, ts], HT_lo[:, c, ts]), (pg_hi[:, c, cs], pg_lo[:, c, cs]),
                                                c == 0, c == C8 - 1)
                        u2.full(ins, ("pg", t, half))
                u2.all_evacuated(pe, [("pg", t, half) for t in range(T) for half in range(2)], l)
                apart(pe)
                with pe.Fori(0, FC // 2) as it:
                    for s in range(2):
                        n = l * FC + it * 2 + s
                        pe.wait_ge(f_lo, n + 1 + CREDIT)
                        pe.wait_ge(f_a, n - 2 + 1 + CREDIT)
                        for k in range(2):
                            for c in range(C8):
                                ins = split_product(pe, bank[2 * s + k][:], (gu_hi[s][:, k, c], gu_lo[s][:, k, c]),
                                                    (HT_hi[:, c], HT_lo[:, c]), c == 0, c == C8 - 1)
                        ins.then_inc(f_g, 1)
                pe.wait_ge(f_a, l * FC + FC + CREDIT)
                pe.sem_inc(b_free, 1)
                for f in range(FC):
                    y_dlo.wait(pe, l, f + 1)
                    for t in range(T):
                        for half in range(2):
                            key = ("dn", t, half)
                            ps = u2.begin(pe, key, l) if f == 0 else bank[b2.where[key][0]]
                            ts, cs = slice(t * P, (t + 1) * P), slice(512 * half, 512 * half + 512)
                            ins = split_product(pe, ps[:], (a_hi[f % 2][:, ts], a_lo[f % 2][:, ts]), (dn_hi[f % 2][:, cs], dn_lo[f % 2][:, cs]),
                                                f == 0, f == FC - 1)
                            if f == FC - 1:
                                u2.full(ins, key)
                    if f < FC - 1:
                        y_dn.inc(ins)


_OUTS = [((1, 512, 1024), "float32")]


def kernel(**inputs):
    from concourse import bacc
    from concourse.bass_utils import run_bass_kernel_spmd

    nc = bacc.Bacc("TRN2", target_bir_lowering=False, num_devices=1)
    arrays = {k: np.ascontiguousarray(v) for k, v in inputs.items()}
    arrays["freqs"] = np.concatenate([THETA ** (-np.arange(n) / n) for n in (16, 32)]).astype(np.float32)
    ins = {k: nc.dram_tensor(k, a.shape, mybir.dt.from_np(a.dtype), kind="ExternalInput").ap() for k, a in arrays.items()}
    out = nc.dram_tensor("y", (1, S, D), F32, kind="ExternalOutput").ap()
    build(nc, ins, out)
    return run_bass_kernel_spmd(nc, [arrays], core_ids=[0]).results[0]["y"]
```
